# Optimizing a Trainium2 kernel written in Bass

```python
import math
import jax, jax.numpy as jnp
from jax import lax
import numpy as np

D_MODEL = 1024
BATCH = 1
SEQ = 2048
DEPTH = 1
DEC_BATCH = 8
DEC_SEQ = 4
PAST_LEN = 4096
PAGE_SIZE = 128

MIX_WIDTH = D_MODEL
WIDTH_A = MIX_WIDTH // 2
HEAD_DIM_A = 128
N_HEADS_A = WIDTH_A // HEAD_DIM_A
CONV_WIDTH = 4
CONV_CH = 3 * WIDTH_A
CHUNK = 64
WIDTH_B = MIX_WIDTH - WIDTH_A
HEAD_DIM_B = 64
N_Q_HEADS_B = WIDTH_B // HEAD_DIM_B
N_KV_HEADS_B = 2
GQA_GROUP = N_Q_HEADS_B // N_KV_HEADS_B
KV_WIDTH_B = N_KV_HEADS_B * HEAD_DIM_B
WINDOW = 128
D_FF = 4 * D_MODEL
N_MOD = 6
IN_COLS = CONV_CH + WIDTH_A + 2 * N_HEADS_A + WIDTH_B + 2 * KV_WIDTH_B
EPS = 1e-6

kernel_name = 'hymba_gdn_swa_sink_decoder'

def rmsnorm(x, w):
    xf = x.astype(jnp.float32)
    y = xf * lax.rsqrt(jnp.mean(xf * xf, axis=-1, keepdims=True) + EPS)
    return (y * w.astype(jnp.float32)).astype(x.dtype)

def l2norm(x):
    return x * lax.rsqrt(jnp.sum(x * x, axis=-1, keepdims=True) + EPS)

def gated_delta_rule(q, k, v, beta, g, s0, chunk):
    b, t, h, dk = q.shape
    dv = v.shape[-1]
    n = t // chunk

    def blk(a):
        a = a.reshape((b, n, chunk, h) + a.shape[3:])
        return jnp.moveaxis(a, 3, 1)

    q, k, v, beta, g = blk(q), blk(k), blk(v), blk(beta), blk(g)
    gc = jnp.cumsum(g, axis=-1)
    idx = jnp.arange(chunk)
    lower = idx[:, None] >= idx[None, :]
    strict = idx[:, None] > idx[None, :]
    decay = jnp.exp(jnp.where(lower, gc[..., :, None] - gc[..., None, :], -jnp.inf))
    kb = k * beta[..., None]
    lmat = jnp.where(strict, jnp.einsum('bhnid,bhnjd->bhnij', kb, k) * decay, 0.0)
    amat = lmat + jnp.eye(chunk, dtype=lmat.dtype)
    rhs = jnp.concatenate([v * beta[..., None], kb * jnp.exp(gc)[..., None]], axis=-1)
    sol = lax.linalg.triangular_solve(amat, rhs, left_side=True, lower=True, unit_diagonal=True)
    u, w = sol[..., :dv], sol[..., dv:]
    attn = jnp.einsum('bhnid,bhnjd->bhnij', q, k) * decay
    qg = q * jnp.exp(gc)[..., None]
    kg = k * jnp.exp(gc[..., -1:] - gc)[..., None]
    g_last = jnp.exp(gc[..., -1])

    def step(s, xs):
        qg_n, kg_n, u_n, w_n, attn_n, gl_n = xs
        v_new = u_n - jnp.einsum('bhck,bhkv->bhcv', w_n, s)
        o = jnp.einsum('bhck,bhkv->bhcv', qg_n, s) + jnp.einsum('bhij,bhjv->bhiv', attn_n, v_new)
        s = s * gl_n[..., None, None] + jnp.einsum('bhck,bhcv->bhkv', kg_n, v_new)
        return s, o

    xs = tuple(jnp.moveaxis(a, 2, 0) for a in (qg, kg, u, w, attn, g_last))
    s_fin, o = lax.scan(step, s0, xs)
    o = jnp.moveaxis(jnp.moveaxis(o, 0, 2), 1, 3).reshape(b, t, h, dv)
    return o, s_fin

def sink_attention(q, k, v, sinks, mask):
    s = jnp.einsum('...qhgd,...khd->...hgqk', q, k).astype(jnp.float32) * (HEAD_DIM_B ** -0.5)
    s = jnp.where(mask, s, -jnp.inf)
    sk = sinks.astype(jnp.float32)[..., None, None]
    m = jnp.maximum(jnp.max(s, axis=-1, keepdims=True), sk)
    p = jnp.exp(s - m)
    p = (p / (jnp.sum(p, axis=-1, keepdims=True) + jnp.exp(sk - m))).astype(v.dtype)
    return jnp.einsum('...hgqk,...khd->...qhgd', p, v)

def swa_prompt(q, k, v, sinks):
    b, t = q.shape[:2]
    nb = t // WINDOW
    qb = q.reshape(b, nb, WINDOW, N_KV_HEADS_B, GQA_GROUP, HEAD_DIM_B)
    kb = k.reshape(b, nb, WINDOW, N_KV_HEADS_B, HEAD_DIM_B)
    vb = v.reshape(b, nb, WINDOW, N_KV_HEADS_B, HEAD_DIM_B)

    def with_prev(a):
        prev = jnp.concatenate([jnp.zeros_like(a[:, :1]), a[:, :-1]], axis=1)
        return jnp.concatenate([prev, a], axis=2)

    kc, vc = with_prev(kb), with_prev(vb)
    qi = jnp.arange(WINDOW)[:, None]
    kj = jnp.arange(2 * WINDOW)[None, :]
    band = (kj > qi) & (kj <= qi + WINDOW)
    real = (jnp.arange(nb)[:, None, None] > 0) | (kj[None] >= WINDOW)
    mask = (band[None] & real)[:, None, None]
    o = sink_attention(qb, kc, vc, sinks, mask)
    return o.reshape(b, t, WIDTH_B), k[:, -WINDOW:], v[:, -WINDOW:]

def swa_sample(q, k, v, kbuf, vbuf, sinks):
    b, t = q.shape[:2]
    kc = jnp.concatenate([kbuf.astype(k.dtype), k], axis=1)
    vc = jnp.concatenate([vbuf.astype(v.dtype), v], axis=1)
    qi = jnp.arange(t)[:, None]
    kj = jnp.arange(WINDOW + t)[None, :]
    mask = (kj > qi) & (kj <= qi + WINDOW)
    o = sink_attention(q, kc, vc, sinks, mask)
    return o.reshape(b, t, WIDTH_B), kc[:, -WINDOW:], vc[:, -WINDOW:]

def trunk_layer(x, c, conv_buf, ssm0, kbuf, vbuf,
                g_pre_mix, g_post_mix, g_pre_ffn, g_post_ffn, w_ada, b_ada,
                w_in, conv_w, a_log, dt_bias, gdn_norm_w, sinks, w_o, w_up, w_down):
    prompt = conv_buf is None
    b, t, _ = x.shape
    dt = x.dtype
    f32 = jnp.float32
    mod = (jax.nn.silu(c) @ w_ada + b_ada).reshape(b, 1, N_MOD, D_MODEL)
    shift_m, scale_m, gate_m = mod[:, :, 0], mod[:, :, 1], mod[:, :, 2]
    shift_f, scale_f, gate_f = mod[:, :, 3], mod[:, :, 4], mod[:, :, 5]

    h = rmsnorm(x, g_pre_mix) * (1 + scale_m) + shift_m
    proj = h @ w_in
    o1 = CONV_CH
    o2 = o1 + WIDTH_A
    o3 = o2 + N_HEADS_A
    o4 = o3 + N_HEADS_A
    o5 = o4 + WIDTH_B
    o6 = o5 + KV_WIDTH_B
    xc, z, b_lg, a_lg, q_b, k_b, v_b = jnp.split(proj, [o1, o2, o3, o4, o5, o6], axis=-1)

    if prompt:
        xp = jnp.concatenate([jnp.zeros((b, CONV_WIDTH - 1, CONV_CH), dt), xc], axis=1)
    else:
        xp = jnp.concatenate([conv_buf.astype(dt), xc], axis=1)
    new_conv = xp[:, -(CONV_WIDTH - 1):]
    xconv = jax.nn.silu(sum(xp[:, i:i + t] * conv_w[i] for i in range(CONV_WIDTH)))
    qa, ka, va = jnp.split(xconv, 3, axis=-1)
    qa = l2norm(qa.reshape(b, t, N_HEADS_A, HEAD_DIM_A).astype(f32)) * (HEAD_DIM_A ** -0.5)
    ka = l2norm(ka.reshape(b, t, N_HEADS_A, HEAD_DIM_A).astype(f32))
    va = va.reshape(b, t, N_HEADS_A, HEAD_DIM_A).astype(f32)
    beta = jax.nn.sigmoid(b_lg.astype(f32))
    g = -jnp.exp(a_log.astype(f32)) * jax.nn.softplus(a_lg.astype(f32) + dt_bias.astype(f32))
    if prompt:
        s0 = jnp.zeros((b, N_HEADS_A, HEAD_DIM_A, HEAD_DIM_A), f32)
        chunk = min(CHUNK, t)
    else:
        s0 = ssm0.astype(f32)
        chunk = t
    o_a, new_ssm = gated_delta_rule(qa, ka, va, beta, g, s0, chunk)
    o_a = rmsnorm(o_a, gdn_norm_w) * jax.nn.silu(z.reshape(b, t, N_HEADS_A, HEAD_DIM_A).astype(f32))
    o_a = o_a.astype(dt).reshape(b, t, WIDTH_A)

    q_b = q_b.reshape(b, t, N_KV_HEADS_B, GQA_GROUP, HEAD_DIM_B)
    k_b = k_b.reshape(b, t, N_KV_HEADS_B, HEAD_DIM_B)
    v_b = v_b.reshape(b, t, N_KV_HEADS_B, HEAD_DIM_B)
    sk = sinks.reshape(N_KV_HEADS_B, GQA_GROUP)
    if prompt:
        o_b, new_k, new_v = swa_prompt(q_b, k_b, v_b, sk)
    else:
        o_b, new_k, new_v = swa_sample(q_b, k_b, v_b, kbuf, vbuf, sk)

    mix = jnp.concatenate([o_a, o_b], axis=-1) @ w_o
    x = x + gate_m * rmsnorm(mix, g_post_mix)

    h = rmsnorm(x, g_pre_ffn) * (1 + scale_f) + shift_f
    y = jnp.square(jax.nn.relu(h @ w_up)) @ w_down
    x = x + gate_f * rmsnorm(y, g_post_ffn)
    return x, new_conv, new_ssm.astype(dt), new_k, new_v

def setup_inputs(seed: int = 0) -> dict:
    key = jax.random.key(seed)
    ks = jax.random.split(key, 24)
    f32 = jnp.float32

    def nrm(k, shape, scale=1.0):
        return jax.random.normal(k, shape, f32) * scale

    def gain(k, shape):
        return 1.0 + 0.05 * jax.random.normal(k, shape, f32)

    dt0 = jnp.exp(jax.random.uniform(ks[17], (DEPTH, N_HEADS_A), f32, math.log(1e-3), math.log(1e-1)))
    return {
        'x_prompt': nrm(ks[0], (BATCH, SEQ, D_MODEL)),
        'x_sample': nrm(ks[1], (DEC_BATCH, DEC_SEQ, D_MODEL)),
        'state_conv': nrm(ks[2], (DEPTH, DEC_BATCH, CONV_WIDTH - 1, CONV_CH)),
        'state_ssm': nrm(ks[3], (DEPTH, DEC_BATCH, N_HEADS_A, HEAD_DIM_A, HEAD_DIM_A), 0.1),
        'cache_swa_k': nrm(ks[4], (DEPTH, DEC_BATCH, WINDOW, N_KV_HEADS_B, HEAD_DIM_B)),
        'cache_swa_v': nrm(ks[5], (DEPTH, DEC_BATCH, WINDOW, N_KV_HEADS_B, HEAD_DIM_B)),
        'c_prompt': nrm(ks[6], (BATCH, D_MODEL)),
        'c_sample': nrm(ks[7], (DEC_BATCH, D_MODEL)),
        'g_pre_mix': gain(ks[8], (DEPTH, D_MODEL)),
        'g_post_mix': gain(ks[9], (DEPTH, D_MODEL)),
        'g_pre_ffn': gain(ks[10], (DEPTH, D_MODEL)),
        'g_post_ffn': gain(ks[11], (DEPTH, D_MODEL)),
        'w_ada': nrm(ks[12], (DEPTH, D_MODEL, N_MOD * D_MODEL), D_MODEL ** -0.5),
        'b_ada': nrm(ks[13], (DEPTH, N_MOD * D_MODEL), 0.01),
        'w_in': nrm(ks[14], (DEPTH, D_MODEL, IN_COLS), D_MODEL ** -0.5),
        'conv_w': nrm(ks[15], (DEPTH, CONV_WIDTH, CONV_CH), CONV_WIDTH ** -0.5),
        'a_log': jnp.log(jax.random.uniform(ks[16], (DEPTH, N_HEADS_A), f32, 1.0, 16.0)),
        'dt_bias': dt0 + jnp.log(-jnp.expm1(-dt0)),
        'gdn_norm_w': gain(ks[18], (DEPTH, HEAD_DIM_A)),
        'sinks': nrm(ks[19], (DEPTH, N_Q_HEADS_B), 0.5),
        'w_o': nrm(ks[20], (DEPTH, MIX_WIDTH, D_MODEL), MIX_WIDTH ** -0.5),
        'w_up': nrm(ks[21], (DEPTH, D_MODEL, D_FF), D_MODEL ** -0.5),
        'w_down': nrm(ks[22], (DEPTH, D_FF, D_MODEL), D_FF ** -0.5),
    }

def reference(x_prompt, x_sample, state_conv, state_ssm, cache_swa_k, cache_swa_v, c_prompt, c_sample,
              g_pre_mix, g_post_mix, g_pre_ffn, g_post_ffn, w_ada, b_ada, w_in, conv_w, a_log, dt_bias,
              gdn_norm_w, sinks, w_o, w_up, w_down):
    yp, ys = x_prompt, x_sample
    pc, ps, pk, pv = [], [], [], []
    sc, ss, skk, svv = [], [], [], []
    for l in range(DEPTH):
        lp = (g_pre_mix[l], g_post_mix[l], g_pre_ffn[l], g_post_ffn[l], w_ada[l], b_ada[l],
              w_in[l], conv_w[l], a_log[l], dt_bias[l], gdn_norm_w[l], sinks[l], w_o[l], w_up[l], w_down[l])
        yp, c1, s1, k1, v1 = trunk_layer(yp, c_prompt, None, None, None, None, *lp)
        ys, c2, s2, k2, v2 = trunk_layer(ys, c_sample, state_conv[l], state_ssm[l],
                                         cache_swa_k[l], cache_swa_v[l], *lp)
        pc.append(c1); ps.append(s1); pk.append(k1); pv.append(v1)
        sc.append(c2); ss.append(s2); skk.append(k2); svv.append(v2)
    return (yp, ys, jnp.stack(pc), jnp.stack(ps), jnp.stack(pk), jnp.stack(pv),
            jnp.stack(sc), jnp.stack(ss), jnp.stack(skk), jnp.stack(svv))


_drawn_inputs = setup_inputs


def setup_inputs(seed=0):
    import zlib

    import numpy as np

    out = dict(_drawn_inputs(seed))
    spreads = {}
    factors = {'b_ada': 3.027, 'sinks': 8.0}
    for name, (base, spread) in spreads.items():
        noise = np.random.default_rng([zlib.crc32(name.encode()), seed]).standard_normal(out[name].shape)
        drawn = base * np.exp(spread * noise) if base else spread * noise
        out[name] = __import__('jax').numpy.asarray(drawn.astype(out[name].dtype))
    for name, factor in factors.items():
        out[name] = (out[name] * factor).astype(out[name].dtype)
    return out
```

```python
from contextlib import ExitStack

import concourse.bass as bass
import numpy as np
from concourse import mybir

F32 = mybir.dt.float32
FR = mybir.dt.float32r
ALU = mybir.AluOpType
ACT = mybir.ActivationFunctionType
AX = mybir.AxisListType

P = 128
D = 1024
KD = D // P
T = 2048
NT = T // P
NB = 8
NS = 4
TS = NB * NS
HA = 4
CC = 12
CW = 4
NCH = 22
HB = 8
DB = 64
W = 128
FF = 4 * D
EPS = 1e-6
NEG = -1e30
BLK = 512
NBLK = T // BLK
SB = TS // NBLK
LEAD = 4
BT = LEAD + BLK + SB
PAD = W
V_BADA, V_GPM, V_GQM, V_GPF, V_GQF, V_GDN = 0, 48, 56, 64, 72, 80
NV = 81


class Mem:

    def __init__(self, nc, ctx):
        self.nc, self.ctx, self.sems = nc, ctx, []

    def sb(self, name, shape, dt=F32):
        return self.ctx.enter_context(self.nc.sbuf_tensor(name, shape, dt))

    def ps(self, name, shape):
        return self.ctx.enter_context(self.nc.psum_tensor(name, shape, F32))

    def sem(self, name):
        self.sems.append(self.nc.alloc_semaphore(name=name))
        return self.sems[-1]

    def clear_sems(self):
        self.nc.clear_and_free_semaphores(self.sems)
        self.nc.all_engine_barrier()


def three_pass(nc, out, whi, wlo, mhi, mlo, first, last):
    nc.tensor.matmul(out, whi, mhi, start=first, stop=False)
    nc.tensor.matmul(out, whi, mlo, start=False, stop=False)
    return nc.tensor.matmul(out, wlo, mhi, start=False, stop=last)


def constants(nc, io, k):
    with ExitStack() as ctx:
        m = Mem(nc, ctx)
        vec = m.sb("vec_rows", [NV, P])
        cwr = m.sb("conv_rows", [CW * CC, P])
        cin = m.sb("c_rows", [1 + NB, D])
        cth = m.sb("c_tanh", [1 + NB, D])
        csl = m.sb("c_silu", [1 + NB, D])
        scr = m.sb("cache_rows", [NB * (CW - 1), CC * P])
        pc = m.ps("const_ps", [P, 4, 512])
        s_vec, s_c = m.sem("vectors_loaded"), m.sem("c_loaded")
        s_set, s_sel, s_th, s_si = m.sem("masks_set"), m.sem("masks_cut"), m.sem("c_tanh_done"), m.sem("c_silu_done")
        s_tr, s_der, s_nap = m.sem("columns_turned"), m.sem("derived"), m.sem("tap_halved")
        with nc.Block() as block:
            @block.sync
            def _(sp):
                rows = lambda v, n: v.rearrange("a (c p) -> (a c) p", p=P)
                for src, at, n in ((io["b_ada"], V_BADA, 48), (io["g_pre_mix"], V_GPM, 8), (io["g_post_mix"], V_GQM, 8),
                                   (io["g_pre_ffn"], V_GPF, 8), (io["g_post_ffn"], V_GQF, 8), (io["gdn_norm_w"], V_GDN, 1)):
                    sp.dma_start(vec[at:at + n, :], rows(src, n)).then_inc(s_vec, 16)
                sp.dma_start(cwr[:], io["conv_w"].rearrange("a i (c p) -> (a i c) p", p=P)).then_inc(s_vec, 16)
                sp.dma_start(scr[:], io["state_conv"].rearrange("a b i c -> (a b i) c")).then_inc(s_vec, 16)
                sp.dma_start(cin[0:1, :], io["c_prompt"]).then_inc(s_c, 16)
                sp.dma_start(cin[1:1 + NB, :], io["c_sample"]).then_inc(s_c, 16)
                for src, dst in ((io["a_log"], k["alog"]), (io["dt_bias"], k["dtb"]), (io["sinks"], k["sink"])):
                    sp.dma_start(dst[:], src.partition_broadcast(P).rearrange("p a h -> p (a h)")).then_inc(s_vec, 16)
                for s in range(NS):
                    sp.dma_start(k["sink_s"][s * 4:s * 4 + 4, :], io["sinks"].rearrange("a (g c) -> (a c) g", g=2), allow_slow_non_contiguous=True
                                 ).then_inc(s_vec, 16)
                sp.wait_ge(s_vec, 16 * (8 + 3 + NS))

            @block.gpsimd
            def _(pool):
                g = nc.gpsimd
                g.memset(k["zeros"][:], 0.0).then_inc(s_set, 1)
                g.memset(k["ones"][:], 1.0).then_inc(s_set, 1)
                g.memset(k["ident"][:], 0.0).then_inc(s_set, 1)
                g.memset(k["ut"][:], 1.0).then_inc(s_set, 1)
                g.memset(k["neg"][:], 0.0).then_inc(s_set, 1)
                g.memset(k["band"][:], 0.0).then_inc(s_set, 1)
                g.memset(k["band_now"][:, 0:W], NEG).then_inc(s_set, 1)
                g.memset(k["band_now"][:, W:2 * W], 0.0).then_inc(s_set, 1)
                g.memset(k["lev"][:], 0.0).then_inc(s_set, 1)
                g.memset(k["state"][:], 0.0).then_inc(s_set, 1)
                g.memset(k["xnT"][:, :, 0:LEAD], 0.0).then_inc(s_set, 1)
                g.memset(k["same"][:], 1.0).then_inc(s_set, 1)
                g.memset(k["seg"][:], 1.0).then_inc(s_set, 1)
                g.memset(k["uts"][:], 1.0).then_inc(s_set, 1)
                g.memset(k["negs"][:], 0.0).then_inc(s_set, 1)
                g.memset(k["masks"][:], 0.0).then_inc(s_set, 1)
                g.memset(k["nhalf"][:], -0.5).then_inc(s_set, 1)
                n = 17
                pool.wait_ge(s_set, n)
                for lv in range(7):
                    b = 1 << lv
                    g.memset(k["lev"][:, lv, :].rearrange("p (m r) -> p m r", r=2 * b)[:, :, b:2 * b], 1.0).then_inc(s_set, 1)
                    n += 1
                pool.wait_ge(s_set, n)
                cut = 0

                def sel(ap, op, fill, base, pattern, mul, after=True):
                    nonlocal cut
                    if after:
                        pool.wait_ge(s_sel, cut)
                    g.affine_select(out=ap, in_=ap, pattern=pattern, compare_op=op, fill=fill, base=base,
                                    channel_multiplier=mul).then_inc(s_sel, 1)
                    cut += 1

                sel(k["ident"][:], ALU.not_equal, 1.0, 0, [[-1, P]], 1, False)
                sel(k["ut"][:], ALU.is_ge, 0.0, 0, [[1, P]], -1)
                sel(k["neg"][:], ALU.is_ge, NEG, 0, [[1, P]], -1)
                sel(k["band"][:], ALU.is_gt, NEG, 0, [[1, 2 * W]], -1)
                sel(k["band"][:], ALU.is_ge, NEG, W, [[-1, 2 * W]], 1)
                sel(k["band_now"][:, W:2 * W], ALU.is_ge, NEG, 0, [[-1, W]], 1)
                for lv in range(7):
                    b = 1 << lv
                    v = k["lev"][:, lv, :].rearrange("p (m r) -> p m r", r=2 * b)
                    sel(v, ALU.is_ge, 0.0, 0, [[-2 * b, P // (2 * b)], [0, 2 * b]], 1)
                    sel(v, ALU.is_ge, 0.0, b - 1, [[2 * b, P // (2 * b)], [0, 2 * b]], -1)
                sv = k["same"][:].rearrange("p (m r) -> p m r", r=NS)
                sel(sv, ALU.is_ge, 0.0, 0, [[-NS, NB], [0, NS]], 1)
                sel(sv, ALU.is_ge, 0.0, NS - 1, [[NS, NB], [0, NS]], -1)
                sel(k["seg"][:], ALU.is_ge, 0.0, 0, [[-NS, NB]], 1)
                sel(k["seg"][:], ALU.is_ge, 0.0, NS - 1, [[NS, NB]], -1)
                uv = k["uts"][:].rearrange("p (m r) -> p m r", r=NS)
                sel(k["uts"][:], ALU.is_ge, 0.0, 0, [[1, TS]], -1)
                sel(uv, ALU.is_ge, 0.0, 0, [[-NS, NB], [0, NS]], 1)
                sel(uv, ALU.is_ge, 0.0, NS - 1, [[NS, NB], [0, NS]], -1)
                nv = k["negs"][:].rearrange("p (m r) -> p m r", r=NS)
                sel(k["negs"][:], ALU.is_ge, NEG, 0, [[1, TS]], -1)
                sel(nv, ALU.is_ge, NEG, 0, [[-NS, NB], [0, NS]], 1)
                sel(nv, ALU.is_ge, NEG, NS - 1, [[NS, NB], [0, NS]], -1)
                sel(k["masks"][:], ALU.is_gt, NEG, 0, [[NS, W + NS]], -1)
                sel(k["masks"][:], ALU.is_ge, NEG, NS * W, [[-NS, W + NS]], 1)

            @block.scalar
            def _(act):
                act.wait_ge(s_c, 32)
                nc.scalar.activation(cth[:], cin[:], ACT.Tanh, scale=0.5).then_inc(s_th, 1)

            @block.vector
            def _(dve):
                v = nc.vector
                dve.wait_ge(s_th, 1)
                v.scalar_tensor_tensor(csl[:], cth[:], 1.0, cin[:], ALU.add, ALU.mult).then_inc(s_si, 1)
                dve.wait_ge(s_tr, 1)
                v.tensor_copy(k["vcol"][:], pc[:, 0, 0:NV]).then_inc(s_der, 1)
                v.tensor_scalar(k["taps"][:], pc[:, 1, 0:CW * CC], 0.5, None, ALU.mult).then_inc(s_der, 1)
                v.tensor_copy(k["xs_pad"][:, :, :, 0:CW - 1],
                              pc[:, 2, 0:CC * 24].rearrange("p (c b i) -> p c b i", c=CC, b=NB)).then_inc(s_der, 1)
                dve.wait_ge(s_tr, 2)
                v.tensor_scalar(k["scT"][:], pc[:, 3, 0:KD * 9].rearrange("p (k n) -> p k n", n=9), 0.5, None,
                                ALU.mult).then_inc(s_der, 1)

            @block.tensor
            def _(pe):
                pe.wait_ge(s_vec, 16 * (8 + 3 + NS))
                pe.wait_ge(s_sel, 1)
                nc.tensor.transpose(pc[:, 0, 0:NV], vec[:], k["ident"][0:NV, 0:NV])
                nc.tensor.transpose(pc[:, 1, 0:CW * CC], cwr[:], k["ident"][0:CW * CC, 0:CW * CC])
                for c in range(CC):
                    last = nc.tensor.transpose(pc[:, 2, c * 24:c * 24 + 24], scr[:, c * P:(c + 1) * P], k["ident"][0:24, 0:24])
                last.then_inc(s_tr, 1)
                pe.wait_ge(s_si, 1)
                for c in range(KD):
                    last = nc.tensor.transpose(pc[:, 3, c * 9:c * 9 + 9], csl[:, c * P:(c + 1) * P], k["ident"][0:9, 0:9])
                last.then_inc(s_tr, 1)
        m.clear_sems()


def modulation(nc, io, k):
    GC = 3
    with ExitStack() as ctx:
        m = Mem(nc, ctx)
        xt = m.sb("x_tile", [P, 2, D])
        xn = m.sb("x_normed", [P, 2, D])
        sq = m.sb("x_squares", [P, D])
        ss = m.sb("x_sumsq", [P, 2])
        ms = m.sb("x_meansq", [P, 2])
        rr = m.sb("x_rrms", [P, 2])
        wa = m.sb("w_ada_cols", [P, 2, KD, GC * P])
        modT = m.sb("modT", [P, 6 * KD, 9])
        gcol, gcs = k["gate_col"], k["gate_col_s"]
        one = m.sb("one_plus", [P, 2, KD, 9])
        pt = m.ps("xT_ps", [P, 2, 2, 512])
        pm = m.ps("mod_ps", [P, 2, 512])
        s_x = [m.sem(f"x_loaded_{p}") for p in range(2)]
        s_wa = [m.sem(f"w_ada_loaded_{p}") for p in range(2)]
        s_ss, s_ms, s_rr, s_xn = m.sem("x_sumsq_done"), m.sem("x_meansq_done"), m.sem("x_rrms_done"), m.sem("x_normed_done")
        s_xT, s_ev = m.sem("x_turned"), m.sem("xnT_written")
        s_mod, s_me = m.sem("mod_summed"), m.sem("mod_written")
        s_free = m.sem("mod_ps_free")
        s_d, s_c = m.sem("mod_derived"), m.sem("mod_chain")
        N = NT + 1
        with nc.Block() as block:
            @block.sync
            def _(sp):
                with sp.Fori(0, NT // 2) as i:
                    for p in range(2):
                        t = i * 2 + p
                        sp.wait_ge(s_free, t + 1)
                        sp.dma_start(wa[:, p], io["w_ada"][:, bass.ds(t * (GC * P), GC * P)]
                                     .rearrange("(k p) n -> p k n", p=P)).then_inc(s_wa[p], 16)
                        sp.wait_ge(s_free, t + 1)
                        sp.dma_start(xt[:, p], io["x"][bass.ds(t * P, P), :]).then_inc(s_x[p], 16)
                sp.wait_ge(s_free, NT + 1)
                sp.dma_start(xt[0:TS, 0], io["xs"]).then_inc(s_x[0], 16)

            @block.scalar
            def _(act):
                a = nc.scalar

                def square(i, t, p, n):
                    act.wait_ge(s_x[p], i * 16 + 16)
                    a.activation(sq[0:n], xt[0:n, p], ACT.Square, accum_out=ss[0:n, p:p + 1]).then_inc(s_ss, 1)

                def evac(t, p, n, dst):
                    act.wait_ge(s_xT, t + 1)
                    src = pt[:, p].rearrange("p a (b t) -> p (a b) t", t=P)[:, :, 0:n]
                    a.copy(dst, src).then_inc(s_ev, 1)

                with act.Fori(0, NT // 2) as i:
                    for p in range(2):
                        t = i * 2 + p
                        square(i, t, p, P)
                        evac(t, p, P, k["xnT"][:, :, bass.ds(t * P + LEAD, P)])
                square(NT // 2, NT, 0, TS)
                evac(NT, 0, TS, k["xnT"][:, :, LEAD + T:LEAD + T + TS])

            @block.gpsimd
            def _(pool):
                g = nc.gpsimd

                def rrms(t, p, n):
                    pool.wait_ge(s_ms, t + 1)
                    g.tensor_tensor(rr[0:n, p:p + 1], ms[0:n, p:p + 1], k["nhalf"][0:n, 0:1], ALU.pow).then_inc(s_rr, 1)

                with pool.Fori(0, NT // 2) as i:
                    for p in range(2):
                        rrms(i * 2 + p, p, P)
                rrms(NT, 0, TS)

            @block.vector
            def _(dve):
                v = nc.vector

                def norm(i, t, p, n):
                    dve.wait_ge(s_ss, t + 1)
                    v.tensor_scalar(ms[0:n, p:p + 1], ss[0:n, p:p + 1], 1.0 / D, EPS, ALU.mult, ALU.add).then_inc(s_ms, 1)
                    dve.wait_ge(s_rr, t + 1)
                    dve.wait_ge(s_x[p], i * 16 + 16)
                    v.tensor_scalar(xn[0:n, p], xt[0:n, p], rr[0:n, p:p + 1], None, ALU.mult).then_inc(s_xn, 1)

                dve.sem_inc(s_free, 2)
                with dve.Fori(0, NT // 2) as i:
                    for p in range(2):
                        t = i * 2 + p
                        norm(i, t, p, P)
                        dve.wait_ge(s_mod, t + 1)
                        v.tensor_copy(modT[:, bass.ds(t * GC, GC), :],
                                      pm[:, p, 0:GC * 9].rearrange("p (c n) -> p c n", n=9)).then_inc(s_free, 1)
                norm(NT // 2, NT, 0, TS)
                dve.wait_ge(s_free, NT + 2)
                v.tensor_tensor(modT[:], modT[:], k["vcol"][:, V_BADA:V_BADA + 48].unsqueeze(2).broadcast_to([P, 48, 9]),
                                ALU.add).then_inc(s_c, 1)
                dve.wait_ge(s_c, 1)
                mo = modT[:].rearrange("p (m k) n -> p m k n", m=6)
                for f, (gate, post) in enumerate(((2, V_GQM), (5, V_GQF))):
                    v.tensor_tensor(gcol[:, f], mo[:, gate, :, 0], k["vcol"][:, post:post + KD], ALU.mult).then_inc(s_d, 1)
                    v.tensor_tensor(gcs[:, f], mo[:, gate, :, 1:9].unsqueeze(3).broadcast_to([P, KD, NB, NS]),
                                    k["vcol"][:, post:post + KD].unsqueeze(2).unsqueeze(3).broadcast_to([P, KD, NB, NS]),
                                    ALU.mult).then_inc(s_d, 1)
                for f, (shift, scale, pre) in enumerate(((0, 1, V_GPM), (3, 4, V_GPF))):
                    v.tensor_scalar(one[:, f], mo[:, scale], 1.0, None, ALU.add).then_inc(s_c, 1)
                    dve.wait_ge(s_c, 2 + f)
                    v.tensor_tensor(k["mscale"][:, f], one[:, f], k["vcol"][:, pre:pre + KD].unsqueeze(2)
                                    .broadcast_to([P, KD, 9]), ALU.mult).then_inc(s_d, 1)
                    v.tensor_copy(k["mshift"][:, f], mo[:, shift]).then_inc(s_d, 1)
                    v.tensor_tensor(k["pscale"][:, f], one[:, f, :, 0], k["vcol"][:, pre:pre + KD], ALU.mult).then_inc(s_d, 1)
                    v.tensor_copy(k["pshift"][:, f], mo[:, shift, :, 0]).then_inc(s_d, 1)

            @block.tensor
            def _(pe):
                def turn(t, p, n):
                    pe.wait_ge(s_xn, t + 1)
                    pe.wait_ge(s_ev, t + 1)
                    for c in range(KD):
                        last = nc.tensor.transpose(pt[:, p, c // 4, (c % 4) * P:(c % 4) * P + n],
                                                   xn[0:n, p, c * P:(c + 1) * P], k["ident"][0:n, 0:n])
                    last.then_inc(s_xT, 1)

                pe.sem_inc(s_ev, 2)
                with pe.Fori(0, NT // 2) as i:
                    for p in range(2):
                        t = i * 2 + p
                        turn(t, p, P)
                        pe.wait_ge(s_wa[p], i * 16 + 16)
                        pe.wait_ge(s_free, t + 1)
                        for c in range(GC):
                            for kk in range(KD):
                                last = nc.tensor.matmul(pm[:, p, c * 9:c * 9 + 9], wa[:, p, kk, c * P:(c + 1) * P],
                                                        k["scT"][:, kk, :], start=(kk == 0), stop=(kk == KD - 1))
                        last.then_inc(s_mod, 1)
                turn(NT, 0, TS)
        m.clear_sems()


def projection(nc, io, k):
    with ExitStack() as ctx:
        m = Mem(nc, ctx)
        raw = m.sb("w_in_raw", [P, 2, KD, P])
        whi = m.sb("w_in_hi", [P, 2, KD, P], FR)
        wlo = m.sb("w_in_lo", [P, 2, KD, P], FR)
        hf = m.sb("h_slice", [P, LEAD + BLK])
        hhi = m.sb("h_hi", [P, 2, KD, BT], FR)
        hlo = m.sb("h_lo", [P, 2, KD, BT], FR)
        hsf = m.sb("hs_full", [P, KD, TS])
        hshi = m.sb("hs_hi", [P, KD, TS], FR)
        hslo = m.sb("hs_lo", [P, KD, TS], FR)
        wba = m.sb("w_ba", [P, KD, 2 * HA])
        wbh = m.sb("w_ba_hi", [P, KD, 2 * HA], FR)
        wbl = m.sb("w_ba_lo", [P, KD, 2 * HA], FR)
        xb = m.sb("chunk_read", [P, 2, BT])
        yb = m.sb("chunk_convolved", [P, 2, BLK])
        so = m.sb("chunk_out", [P, 2, BLK])
        pp = m.ps("proj_ps", [P, 2, 2, 512])
        pb = m.ps("ba_ps", [P, 2, 512])
        s_raw = [m.sem(f"w_in_loaded_{q}") for q in range(2)]
        s_hi, s_lo = m.sem("w_in_hi_split"), m.sem("w_in_lo_split")
        s_h, s_hh, s_hl = m.sem("h_modulated"), m.sem("h_hi_split"), m.sem("h_lo_split")
        s_mm, s_ev = m.sem("chunk_summed"), m.sem("chunk_evacuated")
        s_tap, s_y, s_th, s_so = m.sem("tap_added"), m.sem("chunk_conv_done"), m.sem("chunk_tanh_done"), m.sem("chunk_out_done")
        s_st = k["chunk_stored"]
        s_keep = m.sem("chunk_tails_kept")
        s_wb, s_wbs, s_ba, s_be = m.sem("w_ba_loaded"), m.sem("w_ba_split"), m.sem("ba_summed"), m.sem("ba_read")
        s_hs0, s_hs = m.sem("hs_scaled"), m.sem("hs_full_then_hi_then_lo")
        half = BT // 2
        PARTS = KD + 1
        SEG = (("conv", 0, 6), ("silu", 12, 2), ("plain", 16, 3))

        def pairs(eng, b, body):
            for kind, c0, n in SEG:
                with eng.Fori(0, n) as j:
                    for q in range(2):
                        body(kind, j * 2 + (c0 + q), q, b * NCH + j * 2 + (c0 + q), j + c0 // 2)

        with nc.Block() as block:
            @block.sync
            def _(sp):
                sp.dma_start(wba[:], io["w_in"][:, 2048:2056].rearrange("(k p) n -> p k n", p=P)).then_inc(s_wb, 16)

                def load(kind, c, q, n, j):
                    sp.wait_ge(s_lo, n + 1)
                    col = c * P + (2 * HA if kind == "plain" else 0)
                    sp.dma_start(raw[:, q], io["w_in"][:, bass.ds(col, P)].rearrange("(k p) n -> p k n", p=P)
                                 ).then_inc(s_raw[q], 16)
                with sp.Fori(0, NBLK) as b:
                    pairs(sp, b, load)
                for q in range(2):
                    sp.wait_ge(s_lo, NBLK * NCH + q + 1)
                    sp.dma_start(raw[:, q], io["w_in"][:, q * P:(q + 1) * P].rearrange("(k p) n -> p k n", p=P)
                                 ).then_inc(s_raw[q], 16)

            @block.tensor
            def _(pe):
                pe.wait_ge(s_hs, 1)
                pe.wait_ge(s_wb, 16)
                for kk in range(KD):
                    last = nc.tensor.matmul(pb[0:TS, 1, 0:8], hsf[:, kk, :], wba[:, kk, :], start=(kk == 0), stop=(kk == KD - 1))
                last.then_inc(s_ba, 1)
                pe.wait_ge(s_wbs, 2)

                def block_of(b, q2):
                    def chunk(kind, c, q, n, j):
                        pe.wait_ge(s_hh, (b + 1) * PARTS)
                        pe.wait_ge(s_hl, (b + 1) * PARTS)
                        pe.wait_ge(s_hi, n + 1)
                        pe.wait_ge(s_lo, n + 3)
                        pe.wait_ge(s_ev, n + 1)
                        for kk in range(KD):
                            for h in range(2):
                                at = slice(h * half, (h + 1) * half)
                                last = three_pass(nc, pp[:, q, h, 0:half], whi[:, q, kk, :], wlo[:, q, kk, :],
                                                  hhi[:, q2, kk, at], hlo[:, q2, kk, at], kk == 0, kk == KD - 1)
                        last.then_inc(s_mm, 1)
                    pairs(pe, b, chunk)
                    pe.wait_ge(s_be, b + 1)
                    for jj in range(BLK // P):
                        for kk in range(KD):
                            at = slice(LEAD + jj * P, LEAD + (jj + 1) * P)
                            last = three_pass(nc, pb[:, 0, jj * 8:jj * 8 + 8], hhi[:, q2, kk, at], hlo[:, q2, kk, at],
                                              wbh[:, kk, :], wbl[:, kk, :], kk == 0, kk == KD - 1)
                    last.then_inc(s_ba, 1)

                with pe.Fori(0, NBLK // 2) as i:
                    for q2 in range(2):
                        block_of(i * 2 + q2, q2)

            @block.scalar
            def _(act):
                a = nc.scalar
                act.sem_inc(s_ev, 2)
                act.wait_ge(s_hs, 1)
                a.copy(hshi[:], hsf[:]).then_inc(s_hs, 1)
                act.wait_ge(s_wb, 16)
                a.copy(wbh[:], wba[:]).then_inc(s_wbs, 1)

                def split(pair, q):
                    act.wait_ge(s_raw[q], pair * 16 + 16)
                    a.copy(whi[:, q], raw[:, q]).then_inc(s_hi, 1)

                def slice_hi(count, q2, kk, lead):
                    act.wait_ge(s_h, count + 1)
                    a.copy(hhi[:, q2, kk, lead:LEAD + BLK], hf[:, lead:]).then_inc(s_hh, 1)

                def samples_hi(b, q2):
                    act.wait_ge(s_hs, 2)
                    a.copy(hhi[:, q2, :, LEAD + BLK:BT], hshi[:, :, bass.ds(b * SB, SB)].bitcast(F32)).then_inc(s_hh, 1)

                split(0, 0)
                split(0, 1)
                for kk in range(KD):
                    slice_hi(kk, 0, kk, LEAD)
                samples_hi(0, 0)
                with act.Fori(0, NBLK // 2) as i:
                    for q2 in range(2):
                        b = i * 2 + q2
                        following = i * 2 + 1 if q2 == 0 else 2 - i * 2

                        def chunk(kind, c, q, n, j):
                            act.wait_ge(s_mm, n + 1)
                            act.wait_ge(s_so, n + 1)
                            act.wait_ge(s_keep, n + 1)
                            a.mul(xb[:, q, :].rearrange("p (h t) -> p h t", h=2), pp[:, q, :, 0:half],
                                  0.5 if kind == "silu" else 1.0).then_inc(s_ev, 1)
                            split(b * (NCH // 2) + j + 1, q)
                            if kind != "plain":
                                if q == 0:
                                    slice_hi((b + 1) * KD + j, 1 - q2, bass.ds(j, 1), 0)
                                if kind == "conv":
                                    act.wait_ge(s_y, b * CC + c + 1)
                                else:
                                    act.wait_ge(s_ev, n + 3)
                                act.wait_ge(s_st[q], (b * (NCH // 2) + j) * 16 + 16)
                                src = yb[:, q] if kind == "conv" else xb[:, q, LEAD:LEAD + BLK]
                                a.activation(so[:, q], src, ACT.Tanh).then_inc(s_th, 1)

                        pairs(act, b, chunk)
                        samples_hi(following, 1 - q2)

            @block.vector
            def _(dve):
                v = nc.vector
                dve.sem_inc(s_lo, 2)
                dve.sem_inc(s_be, 1)
                dve.sem_inc(s_so, 2)
                xs = k["xnT"][:, :, LEAD + T:LEAD + T + TS].rearrange("p k (b s) -> p k b s", s=NS)
                hv = hsf[:].rearrange("p k (b s) -> p k b s", s=NS)
                for kk in range(KD):
                    v.tensor_tensor(hv[:, kk], xs[:, kk], k["mscale"][:, 0, kk, 1:9].unsqueeze(2).broadcast_to([P, NB, NS]),
                                    ALU.mult).then_inc(s_hs0, 1)
                dve.wait_ge(s_hs0, KD)
                for kk in range(KD):
                    last = v.tensor_tensor(hv[:, kk], hv[:, kk], k["mshift"][:, 0, kk, 1:9].unsqueeze(2)
                                           .broadcast_to([P, NB, NS]), ALU.add)
                last.then_inc(s_hs, 1)
                dve.wait_ge(s_hs, 2)
                v.tensor_tensor(hslo[:], hsf[:], hshi[:].bitcast(F32), ALU.subtract).then_inc(s_hs, 1)
                dve.wait_ge(s_wbs, 1)
                v.tensor_tensor(wbl[:], wba[:], wbh[:].bitcast(F32), ALU.subtract).then_inc(s_wbs, 1)
                v.memset(hhi[:, 0, :, 0:LEAD].bitcast(F32), 0.0)
                v.memset(hlo[:, 0, :, 0:LEAD].bitcast(F32), 0.0)
                dve.wait_ge(s_ba, 1)
                v.tensor_copy(k["ba_s"][:], pb[0:TS, 1, 0:8])

                def split(n, q):
                    dve.wait_ge(s_hi, n + 1)
                    v.tensor_tensor(wlo[:, q], raw[:, q], whi[:, q].bitcast(F32), ALU.subtract).then_inc(s_lo, 1)

                def modulate(block0, kk, lead):
                    cols = bass.ds(block0 * BLK + lead, LEAD + BLK - lead)
                    one = slice(kk, kk + 1) if isinstance(kk, int) else bass.ds(kk, 1)
                    v.tensor_scalar(hf[:, lead:], k["xnT"][:, one, cols].rearrange("p a t -> p (a t)"),
                                    k["pscale"][:, 0, one], k["pshift"][:, 0, one], ALU.mult, ALU.add).then_inc(s_h, 1)

                def slice_lo(count, q2, kk, lead):
                    dve.wait_ge(s_hh, count + 1)
                    one = slice(kk, kk + 1) if isinstance(kk, int) else bass.ds(kk, 1)
                    v.tensor_tensor(hlo[:, q2, one, lead:LEAD + BLK].rearrange("p a t -> p (a t)"), hf[:, lead:],
                                    hhi[:, q2, one, lead:LEAD + BLK].rearrange("p a t -> p (a t)").bitcast(F32),
                                    ALU.subtract).then_inc(s_hl, 1)

                def samples_lo(b, q2):
                    dve.wait_ge(s_hs, 3)
                    v.tensor_copy(hlo[:, q2, :, LEAD + BLK:BT], hslo[:, :, bass.ds(b * SB, SB)].bitcast(F32)).then_inc(s_hl, 1)

                split(0, 0)
                split(1, 1)
                for kk in range(KD):
                    dve.wait_ge(s_hl, kk)
                    modulate(0, kk, LEAD)
                    slice_lo(kk, 0, kk, LEAD)
                samples_lo(0, 0)
                with dve.Fori(0, NBLK // 2) as i:
                    for q2 in range(2):
                        b = i * 2 + q2
                        following = i * 2 + 1 if q2 == 0 else 2 - i * 2

                        def chunk(kind, c, q, n, j):
                            fresh = kind != "plain" and q == 0
                            if fresh:
                                dve.wait_ge(s_ba, b + 1)
                                dve.wait_ge(s_hl, (b + 1) * PARTS + j)
                                modulate(following, j, 0)
                            dve.wait_ge(s_ev, n + 3)
                            if kind == "conv":
                                taps = (b * CC + c) * (CW - 1)
                                for t in range(CW):
                                    src = xb[:, q, t + 1:t + 1 + BLK]
                                    tap = k["taps"][:, bass.ds(t * CC + c, 1)]
                                    if t == 0:
                                        ins = v.tensor_scalar(yb[:, q], src, tap, None, ALU.mult)
                                    else:
                                        dve.wait_ge(s_tap, taps + t)
                                        ins = v.scalar_tensor_tensor(yb[:, q], src, tap, yb[:, q], ALU.mult, ALU.add)
                                    ins.then_inc(s_tap if t < CW - 1 else s_y, 1)
                            split(n + 2, q)
                            if fresh:
                                slice_lo((b + 1) * PARTS + j, 1 - q2, j, 0)
                            if kind == "plain":
                                dve.wait_ge(s_st[q], (b * (NCH // 2) + j) * 16 + 16)
                                v.tensor_copy(so[:, q], xb[:, q, LEAD:LEAD + BLK]).then_inc(s_so, 1)
                            else:
                                dve.wait_ge(s_th, b * 16 + c + 1)
                                src = yb[:, q] if kind == "conv" else xb[:, q, LEAD:LEAD + BLK]
                                v.scalar_tensor_tensor(so[:, q], so[:, q], 1.0, src, ALU.add, ALU.mult).then_inc(s_so, 1)

                        pairs(dve, b, chunk)
                        samples_lo(following, 1 - q2)
                        dve.wait_ge(s_ba, b + 2)
                        v.tensor_copy(k["ba"][:, bass.ds(b * 4, 4), :], pb[:, 0, 0:32].rearrange("p (j n) -> p j n", n=8)
                                      ).then_inc(s_be, 1)

            @block.gpsimd
            def _(pool):
                g = nc.gpsimd
                pool.sem_inc(s_keep, 2)
                for q in range(2):
                    pool.dma_start(io["projT"][q * 11:q * 11 + 11, :, 0:PAD].rearrange("c p t -> p c t"),
                                   k["zeros"][:].broadcast_to([P, 11, P])).then_inc(s_st[q], 16)
                with pool.Fori(0, NBLK) as b:
                    def chunk(kind, c, q, n, j):
                        pool.wait_ge(s_ev, n + 3)
                        if kind == "conv":
                            g.tensor_copy(k["xlast"][:, :, bass.ds(c, 1)], xb[:, q, LEAD + BLK - 3:LEAD + BLK].unsqueeze(2))
                        g.tensor_copy(k["projS"][:, bass.ds(c, 1), bass.ds(b * SB, SB)], xb[:, q:q + 1, LEAD + BLK:BT]
                                      ).then_inc(s_keep, 1)
                        pool.wait_ge(s_so, n + 3)
                        pool.dma_start(io["projT"][bass.ds(c, 1), :, bass.ds(b * BLK + PAD, BLK)].rearrange("c p t -> (c p) t"),
                                       so[:, q]).then_inc(s_st[q], 16)
                    pairs(pool, b, chunk)
                for q in range(2):
                    pool.wait_ge(s_st[q], NBLK * NCH // 2 * 16 + 16)
        m.clear_sems()


class Front:

    def __init__(self, m, tag, n, levels):
        sem = lambda name: m.sem(tag + name)
        self.n, self.levels = n, levels
        self.qkv = m.sb(tag + "qkv", [P, CC, n])
        self.sq = m.sb(tag + "squares", [n, 2 * HA, P])
        self.ss, self.ms, self.rs = (m.sb(tag + x, [n, 2, HA]) for x in ("sumsq", "sumsq_eps", "rnorm"))
        self.f = m.sb(tag + "factors", [n, 6, HA])
        self.g = m.sb(tag + "g_now", [n, HA])
        self.qq = m.sb(tag + "q_scaled", [n, 2, HA, P])
        self.kk = m.sb(tag + "k_scaled", [n, 4, HA, P])
        self.vb = m.sb(tag + "v_beta", [n, HA, P])
        self.knT = m.sb(tag + "knT", [P, HA, n])
        self.kqT = m.sb(tag + "kbT_qnT", [P, HA, 2, n])
        self.qgT = m.sb(tag + "qgT", [P, HA, n])
        self.dec = m.sb(tag + "decay", [n, HA, n])
        self.al = m.sb(tag + "LT_attnT", [n, HA, 2, n])
        self.ct = m.sb(tag + "CT", [n, levels, HA, n])
        self.xx = m.sb(tag + "X_XT", [n, 2, HA, n])
        self.ys = m.sb(tag + "Y", [n, HA, n])
        self.nwT = m.sb(tag + "minus_wT", [P, HA, n])
        self.gp = m.ps(tag + "delta_ps", [P, 4, 512])
        self.s_in = sem("qkv_loaded")
        self.s_g = sem("g_placed")
        self.s_t1, self.s_r = sem("qkv_turned"), sem("cumsum_spread")
        self.s_sq, self.s_ss, self.s_ms, self.s_rs, self.s_f = (sem(x) for x in ("squared", "sumsq_done", "sumsq_eps_done", "rnorm_done", "factors_done"))
        self.s_sc, self.s_dec, self.s_bt, self.s_kt = (sem(x) for x in ("scaled", "decay_done", "turned_back", "turned_read"))
        self.s_gm, self.s_al, self.s_c, self.s_c1 = (sem(x) for x in ("gram_done", "gram_decayed", "level_cut", "level0_turned"))
        self.s_x, self.s_y, self.s_ye, self.s_z = (sem(x) for x in ("X_done", "Y_done", "Y_read", "Z_done"))
        self.s_w, self.s_nw = sem("wT_done"), sem("wT_read")

    def credits_pe(self):
        return (self.s_t1, self.s_r, self.s_bt, self.s_gm, self.s_c1, self.s_y, self.s_z, self.s_w)

    def credits_act(self):
        return (self.s_sq, self.s_dec, self.s_kt, self.s_ye, self.s_nw)

    def credits_dve(self):
        return (self.s_ss, self.s_ms, self.s_f, self.s_sc, self.s_al, self.s_x)


def was(t, per=1):
    return t * per + 1


def now(t, per=1, step=None):
    return t * per + 2 + (per - 1 if step is None else step)


def front_pe(nc, pe, F, k, t, ut, neg, free):
    n, L = F.n, F.levels
    mm, tr, ident = nc.tensor.matmul, nc.tensor.transpose, k["ident"]
    pn = ident[0:n, 0:n]
    bank = lambda b: F.gp[:, b, :]
    flat = F.gp[:].rearrange("p b c -> p (b c)")

    def turn():
        pe.wait_ge(F.s_in, now(t) * 16)
        free()
        for c in range(CC):
            last = tr(F.gp[0:n, c // HA, (c % HA) * P:(c % HA) * P + P], F.qkv[:, c, :], ident[:])
        last.then_inc(F.s_t1, 1)

    def spread():
        pe.wait_ge(F.s_g, now(t))
        out = F.gp[0:n, 3, 0:HA * n].rearrange("p (h i) -> p h i", h=HA)
        mm(out, pn, neg.unsqueeze(1).broadcast_to([n, HA, n]), start=True, stop=False)
        for h in range(HA):
            last = mm(out[:, h, :], F.g[:, h:h + 1].broadcast_to([n, n]), ut, start=False, stop=(h == HA - 1))
        last.then_inc(F.s_r, 1)

    def back():
        pe.wait_ge(F.s_sc, now(t))
        pe.wait_ge(F.s_dec, now(t))
        for h in range(HA):
            tr(bank(0)[:, h * n:(h + 1) * n], F.kk[:, 0, h, :], pn)
            tr(flat[:, 512 + 2 * h * n:512 + (2 * h + 1) * n], F.kk[:, 1, h, :], pn)
            tr(flat[:, 512 + (2 * h + 1) * n:512 + (2 * h + 2) * n], F.qq[:, 0, h, :], pn)
            last = tr(bank(3)[:, h * n:(h + 1) * n], F.qq[:, 1, h, :], pn)
        last.then_inc(F.s_bt, 1)

    def gram():
        pe.wait_ge(F.s_kt, now(t))
        for h in range(HA):
            last = mm(flat[0:n, 2 * h * n:2 * (h + 1) * n], F.knT[:, h, :], F.kqT[:, h], start=True, stop=True)
        last.then_inc(F.s_gm, 1)

    def level0():
        pe.wait_ge(F.s_c, now(t, L, 0))
        for h in range(HA):
            last = tr(bank(2)[0:n, h * n:(h + 1) * n], F.ct[:, 0, h, :], pn)
        last.then_inc(F.s_c1, 1)

    def level_y(lv):
        pe.wait_ge(F.s_c, now(t, L, lv))
        pe.wait_ge(F.s_x, now(t, L + 1, lv))
        for h in range(HA):
            last = mm(bank(0)[0:n, h * n:(h + 1) * n], F.ct[:, lv, h, :], F.xx[:, 0, h, :], start=True, stop=True)
        last.then_inc(F.s_y, 1)

    def level_z(lv):
        pe.wait_ge(F.s_ye, now(t, L - 1, lv - 1))
        for h in range(HA):
            at = slice(h * n, (h + 1) * n)
            if lv < L - 1:
                mm(bank(1)[0:n, at], F.xx[:, 1, h, :], F.ys[:, h, :], start=True, stop=True)
            last = mm(bank(2)[0:n, at], F.ys[:, h, :], F.xx[:, 1, h, :], start=True, stop=True)
        last.then_inc(F.s_z, 1)

    def w():
        pe.wait_ge(F.s_x, now(t, L + 1))
        for h in range(HA):
            last = mm(bank(0)[:, h * n:(h + 1) * n], F.kk[:, 2, h, :], F.xx[:, 1, h, :], start=True, stop=True)
        last.then_inc(F.s_w, 1)

    return turn, spread, back, gram, level0, level_y, level_z, w


def front_act(nc, act, F, t, negc, free_kt, free_nw, free_sq):
    n, L = F.n, F.levels
    a = nc.scalar

    def square():
        act.wait_ge(F.s_t1, now(t))
        free_sq()
        a.activation(F.sq[:].rearrange("p (b h) d -> p b (h d)", b=2), F.gp[0:n, 0:2, :], ACT.Square).then_inc(F.s_sq, 1)

    def decay():
        act.wait_ge(F.s_r, now(t))
        act.wait_ge(F.s_al, was(t))
        for h in range(HA):
            last = a.activation(F.dec[:, h, :], F.gp[0:n, 3, h * n:(h + 1) * n], ACT.Exp, bias=negc(h))
        last.then_inc(F.s_dec, 1)

    def read_back():
        act.wait_ge(F.s_bt, now(t))
        free_kt()
        flat = F.gp[:].rearrange("p b c -> p (b c)")
        a.copy(F.knT[:].rearrange("p h i -> p (h i)"), flat[:, 0:HA * n])
        a.copy(F.qgT[:].rearrange("p h i -> p (h i)"), flat[:, 3 * 512:3 * 512 + HA * n])
        a.copy(F.kqT[:].rearrange("p h v i -> p (h v i)"), flat[:, 512:512 + 2 * HA * n]).then_inc(F.s_kt, 1)

    def read_y(lv):
        act.wait_ge(F.s_y, now(t, L - 1, lv - 1))
        act.wait_ge(F.s_z, t * (L - 1) + lv)
        a.copy(F.ys[:].rearrange("p h i -> p (h i)"), F.gp[0:n, 0, 0:HA * n]).then_inc(F.s_ye, 1)

    def read_w():
        act.wait_ge(F.s_w, now(t))
        free_nw()
        a.mul(F.nwT[:].rearrange("p h i -> p (h i)"), F.gp[:, 0, 0:HA * n], -1.0).then_inc(F.s_nw, 1)

    return square, decay, read_back, read_y, read_w


def front_dve(nc, dve, F, k, t, table, beta, free_scaled, free_al):
    n, L = F.n, F.levels
    v = nc.vector
    wide = lambda x, d: x.unsqueeze(len(x.shape)).broadcast_to(list(x.shape) + [d])

    def norms():
        dve.wait_ge(F.s_sq, now(t))
        v.tensor_reduce(F.ss[:].rearrange("p a h -> p (a h)"), F.sq[:], AX.X, ALU.add).then_inc(F.s_ss, 1)
        dve.wait_ge(F.s_ss, now(t))
        v.tensor_scalar(F.ms[:], F.ss[:], EPS, None, ALU.add).then_inc(F.s_ms, 1)

    def scale():
        dve.wait_ge(F.s_rs, now(t))
        dve.wait_ge(F.s_sc, was(t))
        v.tensor_tensor(F.f[:, 0:2], table(0, 2), F.rs[:, 0:1, :].broadcast_to([n, 2, HA]), ALU.mult)
        v.tensor_tensor(F.f[:, 2:6], table(2, 6), F.rs[:, 1:2, :].broadcast_to([n, 4, HA]), ALU.mult).then_inc(F.s_f, 1)
        dve.wait_ge(F.s_f, now(t))
        free_scaled()
        src = lambda b, r: F.gp[0:n, b, :].rearrange("p (h d) -> p h d", h=HA).unsqueeze(1).broadcast_to([n, r, HA, P])
        v.tensor_tensor(F.kk[:], src(1, 4), wide(F.f[:, 2:6], P), ALU.mult)
        v.tensor_tensor(F.qq[:], src(0, 2), wide(F.f[:, 0:2], P), ALU.mult)
        v.tensor_tensor(F.vb[:], F.gp[0:n, 2, :].rearrange("p (h d) -> p h d", h=HA), beta, ALU.mult).then_inc(F.s_sc, 1)

    def decayed():
        dve.wait_ge(F.s_gm, now(t))
        dve.wait_ge(F.s_dec, now(t))
        free_al()
        flat = F.gp[:].rearrange("p b c -> p (b c)")
        v.tensor_tensor(F.al[:], flat[0:n, 0:2 * HA * n].rearrange("p (h v i) -> p h v i", h=HA, v=2),
                        F.dec[:].unsqueeze(2).broadcast_to([n, HA, 2, n]), ALU.mult).then_inc(F.s_al, 1)

    def start_x():
        eye = k["ident"][0:n, 0:n].unsqueeze(1).broadcast_to([n, HA, n])
        dve.wait_ge(F.s_c, now(t, L, 0))
        v.tensor_tensor(F.xx[:, 1], eye, F.ct[:, 0], ALU.subtract).then_inc(F.s_x, 1)
        dve.wait_ge(F.s_c1, now(t))
        v.tensor_tensor(F.xx[:, 0], eye, F.gp[0:n, 2, 0:HA * n].rearrange("p (h i) -> p h i", h=HA), ALU.subtract
                        ).then_inc(F.s_x, 1)

    def step_x(lv):
        dve.wait_ge(F.s_z, now(t, L - 1, lv - 1))
        dve.wait_ge(F.s_x, now(t, L + 1, lv))
        lo = 0 if lv < L - 1 else 1
        x = F.xx[:, lo:2].rearrange("p a h i -> p a (h i)")
        v.tensor_tensor(x, x, F.gp[0:n, 1 + lo:3, 0:HA * n], ALU.subtract).then_inc(F.s_x, 1)

    return norms, scale, decayed, start_x, step_x


def front_pool(nc, pool, F, k, t, g_src, lev):
    n, L = F.n, F.levels
    g = nc.gpsimd

    def place():
        pool.wait_ge(F.s_r, was(t))
        g.tensor_copy(F.g[:], g_src).then_inc(F.s_g, 1)

    def rsqrt():
        pool.wait_ge(F.s_ms, now(t))
        g.tensor_tensor(F.rs[:].rearrange("p a h -> p (a h)"), F.ms[:].rearrange("p a h -> p (a h)"),
                        k["nhalf"][0:n, 0:2 * HA], ALU.pow).then_inc(F.s_rs, 1)

    def cut():
        pool.wait_ge(F.s_w, was(t))
        pool.wait_ge(F.s_al, now(t))
        for lv in range(L):
            g.tensor_tensor(F.ct[:, lv], F.al[:, :, 0, :], lev(lv).unsqueeze(1).broadcast_to([n, HA, n]), ALU.mult
                            ).then_inc(F.s_c, 1)

    return place, rsqrt, cut


def mixer(nc, io, k):
    with ExitStack() as ctx:
        m = Mem(nc, ctx)
        F = Front(m, "", P, 7)
        L = F.levels
        th = m.sb("beta_tanh", [P, NT, HA])
        beta = m.sb("beta", [P, NT, HA])
        xa = m.sb("a_biased", [P, NT, HA])
        ax = m.sb("a_abs", [P, NT, HA])
        na = m.sb("a_neg", [P, NT, HA])
        ea = m.sb("decay_rate", [P, HA])
        gg = m.sb("g_all", [P, NT, HA])
        gc = m.sb("g_cumsum", [P, 2, NT, HA])
        negc = m.sb("minus_g_cumsum", [P, NT, HA])
        dk = m.sb("g_to_last", [P, NT, HA])
        gl = m.sb("g_last_exp", [P, NT, HA])
        tab = m.sb("factor_table", [P, NT, 6, HA])
        zT = m.sb("zT", [P, HA, P])
        vn = m.sb("v_new", [P, HA, P])
        osq = m.sb("o_squares", [P, HA, P])
        oss, oms, ors = (m.sb(x, [P, HA]) for x in ("o_sumsq", "o_meansq", "o_rrms"))
        on = m.sb("o_normed", [P, HA, P])
        oaT = m.sb("oaT", [P, HA, P])
        qT = m.sb("attn_qT", [P, 4, P])
        kvT = m.sb("attn_kT_vT", [P, 2, 2 * W])
        vt = m.sb("attn_v", [P, 2, P])
        sm = m.sb("scores", [P, HB, 2 * W])
        mx, nm, esk, dn, rc = (m.sb(x, [P, HB]) for x in ("score_max", "minus_max", "sink_exp", "prob_sum", "prob_recip"))
        pT = m.sb("probsT", [P, HB, 2, P])
        obT = m.sb("obT", [P, 4, P])
        kl = m.sb("k_last", [P, P])
        sp_ = m.ps("attn_ps", [P, 4, 512])
        s_pre = m.sem("tables_step")
        s_pe0, s_act0 = m.sem("cumsums_summed"), m.sem("tables_act_step")
        s_z, s_qk = m.sem("z_loaded"), m.sem("attn_loaded")
        s_v, s_vn, s_o, s_s, s_su = (m.sem(x) for x in ("v_new_done", "v_new_read", "o_done", "state_added", "state_updated"))
        s_osq, s_oss, s_oms, s_ors, s_on, s_ot, s_oa, s_ost = (m.sem(x) for x in (
            "o_squared", "o_sumsq_done", "o_meansq_done", "o_rrms_done", "o_normed_done", "o_turned", "oaT_done", "oaT_stored"))
        s_vT, s_vE, s_sc, s_msk, s_mx, s_nm, s_ex, s_es, s_dn, s_rc, s_pr, s_pt, s_pe, s_ov, s_ob, s_obst, s_bm, s_d8 = (m.sem(x) for x in (
            "attn_v_turned", "attn_v_read", "scores_done", "scores_masked", "max_done", "max_negated", "exp_done", "sink_exp_done",
            "prob_sum_done", "recip_done", "probs_done", "probs_turned", "probsT_read", "attn_out_done", "obT_done", "obT_stored",
            "band_set", "sink_less_max"))
        s_d9 = m.sem("max_with_sink")
        s_fin0, s_fin = m.sem("last_rows_read"), k["states_stored"]
        flat3 = lambda x: x[:].rearrange("p t h -> p (t h)")
        with nc.Block() as block:
            @block.sync
            def _(sp):
                for s in (F.s_in, s_z, s_qk):
                    sp.sem_inc(s, 16)
                with sp.Fori(0, NT) as t:
                    pT_ = io["projT"]
                    sp.wait_ge(F.s_t1, was(t))
                    sp.dma_start(F.qkv[:], pT_[0:CC, :, bass.ds(t * P + PAD, P)].rearrange("c p t -> p c t")).then_inc(F.s_in, 16)
                    sp.wait_ge(s_sc, was(t))
                    sp.wait_ge(s_vT, was(t))
                    for g in range(2):
                        sp.dma_start(qT[64 * g:64 * g + 64, :, :],
                                     pT_[16 + 2 * g:18 + 2 * g, :, bass.ds(t * P + PAD, P)]
                                     .rearrange("c (e d) t -> d (c e) t", e=2)).then_inc(s_qk, 16)
                    sp.dma_start(kvT[:], pT_[20:22, :, bass.ds(t * P, 2 * W)].rearrange("c p t -> p c t")).then_inc(s_qk, 16)
                    sp.wait_ge(s_oa, was(t))
                    sp.dma_start(zT[:], pT_[12:16, :, bass.ds(t * P + PAD, P)].rearrange("c p t -> p c t")).then_inc(s_z, 16)

            @block.tensor
            def _(pe):
                mm, tr, ident = nc.tensor.matmul, nc.tensor.transpose, k["ident"]
                pe.wait_ge(s_pre, 6)
                mm(F.gp[:, 0, 0:NT * HA], k["ut"][:], flat3(gg), start=True, stop=True)
                mm(F.gp[:, 0, NT * HA:2 * NT * HA], k["ones"][:], flat3(gg), start=True, stop=True).then_inc(s_pe0, 1)
                for s in F.credits_pe() + (s_v, s_o, s_s, s_ot, s_vT, s_sc, s_pt, s_ov):
                    pe.sem_inc(s, 1)
                pe.wait_ge(s_pre, 7)
                with pe.Fori(0, NT) as t:
                    turn, spread, back, gram, level0, level_y, level_z, w = front_pe(
                        nc, pe, F, k, t, k["ut"][:], k["neg"][:], lambda: pe.wait_ge(s_oa, was(t)))
                    turn()
                    spread()
                    pe.wait_ge(s_qk, t * 48 + 64)
                    pe.wait_ge(s_ob, was(t))
                    for j in range(2):
                        last = tr(sp_[:, 0, j * P:(j + 1) * P], kvT[:, 1, j * W:(j + 1) * W], ident[:])
                    last.then_inc(s_vT, 1)
                    back()
                    pe.wait_ge(s_vE, now(t))
                    for g in range(2):
                        for c in range(4):
                            at = slice(64 * g, 64 * g + 64)
                            last = mm(sp_[:, 2 * g + c // 2, (c % 2) * 256:(c % 2) * 256 + 256], qT[at, c, :], kvT[at, 0, :],
                                      start=True, stop=True)
                    last.then_inc(s_sc, 1)
                    gram()
                    level0()
                    for lv in range(1, L):
                        level_y(lv)
                        if lv == 4:
                            pe.wait_ge(s_pr, now(t))
                            for h in range(HB):
                                for j in range(2):
                                    last = tr(sp_[:, h // 2, (h % 2) * 256 + j * P:(h % 2) * 256 + (j + 1) * P],
                                              sm[:, h, j * W:(j + 1) * W], ident[:])
                            last.then_inc(s_pt, 1)
                        if lv == 6:
                            pe.wait_ge(s_pe, now(t))
                            for g in range(2):
                                for c in range(4):
                                    for j in range(2):
                                        last = mm(sp_[64 * g:64 * g + 64, 0, c * P:(c + 1) * P], vt[:, j, 64 * g:64 * g + 64],
                                                  pT[:, 4 * g + c, j, :], start=(j == 0), stop=(j == 1))
                            last.then_inc(s_ov, 1)
                        level_z(lv)
                    w()
                    pe.wait_ge(F.s_nw, now(t))
                    pe.wait_ge(s_su, was(t, HA))
                    for h in range(HA):
                        at = slice(h * P, (h + 1) * P)
                        mm(F.gp[:, 1, at], F.xx[:, 1, h, :], F.vb[:, h, :], start=True, stop=False)
                        last = mm(F.gp[:, 1, at], F.nwT[:, h, :], k["state"][:, h, :], start=False, stop=True)
                    last.then_inc(s_v, 1)
                    pe.wait_ge(s_vn, now(t))
                    for h in range(HA):
                        at = slice(h * P, (h + 1) * P)
                        mm(F.gp[:, 2, at], F.qgT[:, h, :], k["state"][:, h, :], start=True, stop=False)
                        last = mm(F.gp[:, 2, at], F.al[:, h, 1, :], vn[:, h, :], start=False, stop=True)
                    last.then_inc(s_o, 1)
                    for h in range(HA):
                        last = mm(F.gp[:, 3, h * P:(h + 1) * P], F.kk[:, 3, h, :], vn[:, h, :], start=True, stop=True)
                    last.then_inc(s_s, 1)
                    pe.wait_ge(s_on, now(t))
                    for h in range(HA):
                        last = tr(F.gp[:, 0, h * P:(h + 1) * P], on[:, h, :], ident[:])
                    last.then_inc(s_ot, 1)
                pe.wait_ge(s_ov, now(NT - 1))
                pe.wait_ge(s_ob, now(NT - 1))
                tr(sp_[:, 1, 0:P], kvT[:, 0, W:2 * W], ident[:])
                tr(sp_[0:36, 2, 0:P], k["xlast"][:].rearrange("p i c -> p (i c)"), ident[:]).then_inc(s_pe0, 1)

            @block.scalar
            def _(act):
                a = nc.scalar
                a.activation(th[:], k["ba"][:, :, 0:HA], ACT.Tanh, scale=0.5).then_inc(s_act0, 1)
                a.activation(ea[:], k["alog"][:], ACT.Exp).then_inc(s_act0, 1)
                act.wait_ge(s_pre, 3)
                a.activation(ax[:], ax[:], ACT.Exp, scale=-1.0).then_inc(s_act0, 1)
                act.wait_ge(s_act0, 3)
                a.activation(ax[:], ax[:], ACT.Ln, bias=1.0).then_inc(s_act0, 1)
                act.wait_ge(s_pre, 8)
                a.activation(gc[:, 0], gc[:, 0], ACT.Exp).then_inc(s_act0, 1)
                a.activation(gl[:], gc[:, 1], ACT.Exp).then_inc(s_act0, 1)
                a.activation(dk[:], dk[:], ACT.Exp).then_inc(s_act0, 1)
                for s in (s_ost, s_obst):
                    act.sem_inc(s, 16)
                for s in F.credits_act() + (s_vn, s_osq, s_vE, s_ex, s_es, s_pe, s_ob):
                    act.sem_inc(s, 1)
                with act.Fori(0, NT) as t:
                    square, decay, read_back, read_y, read_w = front_act(
                        nc, act, F, t, lambda h: negc[:, bass.ds(t, 1), h:h + 1].rearrange("p a h -> p (a h)"),
                        lambda: act.wait_ge(s_o, was(t)), lambda: act.wait_ge(s_v, was(t)), lambda: act.wait_ge(F.s_ss, was(t)))
                    square()
                    decay()
                    act.wait_ge(s_vT, now(t))
                    act.wait_ge(s_ov, was(t))
                    a.copy(vt[:].rearrange("p j d -> p (j d)"), sp_[:, 0, 0:2 * P]).then_inc(s_vE, 1)
                    read_back()
                    read_y(1)
                    act.wait_ge(s_nm, now(t))
                    act.wait_ge(s_ex, was(t))
                    act.wait_ge(s_dn, was(t))
                    for h in range(HB):
                        last = a.activation(sm[:, h, :], sm[:, h, :], ACT.Exp, bias=nm[:, h:h + 1], accum_out=dn[:, h:h + 1])
                    last.then_inc(s_ex, 1)
                    act.wait_ge(s_d8, now(t))
                    a.activation(esk[:], esk[:], ACT.Exp).then_inc(s_es, 1)
                    for lv in range(2, L):
                        read_y(lv)
                        if lv == 4 or lv == 5:
                            if lv == 4:
                                act.wait_ge(s_pt, now(t))
                            j = 2 * (lv - 4)
                            ins = a.copy(pT[:].rearrange("p (b e) j q -> p b (e j q)", b=4)[:, j:j + 2], sp_[:, j:j + 2, :])
                            if lv == 5:
                                ins.then_inc(s_pe, 1)
                    read_w()
                    act.wait_ge(s_ov, now(t))
                    act.wait_ge(s_obst, was(t) * 16)
                    a.copy(obT[:].rearrange("p c q -> p (c q)"), sp_[:, 0, :]).then_inc(s_ob, 1)
                    act.wait_ge(s_v, now(t))
                    a.copy(vn[:].rearrange("p h d -> p (h d)"), F.gp[:, 1, :]).then_inc(s_vn, 1)
                    act.wait_ge(s_o, now(t))
                    act.wait_ge(s_oss, was(t))
                    a.activation(osq[:].rearrange("p h d -> p (h d)"), F.gp[:, 2, :], ACT.Square).then_inc(s_osq, 1)
                    act.wait_ge(s_ob, now(t))
                    act.dma_start(io["oT"][4:8, :, bass.ds(t * P, P)].rearrange("c p t -> p c t"), obT[:]).then_inc(s_obst, 16)
                    act.wait_ge(s_oa, now(t))
                    act.dma_start(io["oT"][0:4, :, bass.ds(t * P, P)].rearrange("c p t -> p c t"), oaT[:]).then_inc(s_ost, 16)

            @block.vector
            def _(dve):
                v = nc.vector
                wide = lambda x, d: x.unsqueeze(len(x.shape)).broadcast_to(list(x.shape) + [d])
                per_head = lambda x: x[:].unsqueeze(1).broadcast_to([P, NT, HA])
                v.tensor_tensor(xa[:], k["ba"][:, :, HA:2 * HA], per_head(k["dtb"]), ALU.add).then_inc(s_pre, 1)
                dve.wait_ge(s_pre, 1)
                v.tensor_scalar(na[:], xa[:], -1.0, None, ALU.mult).then_inc(s_pre, 1)
                dve.wait_ge(s_pre, 2)
                v.tensor_tensor(ax[:], xa[:], na[:], ALU.max).then_inc(s_pre, 1)
                dve.wait_ge(s_act0, 4)
                v.scalar_tensor_tensor(xa[:], xa[:], 0.0, ax[:], ALU.max, ALU.add).then_inc(s_pre, 1)
                dve.wait_ge(s_pre, 4)
                v.tensor_scalar(xa[:], xa[:], -1.0, None, ALU.mult).then_inc(s_pre, 1)
                dve.wait_ge(s_pre, 5)
                v.tensor_tensor(gg[:], xa[:], per_head(ea), ALU.mult).then_inc(s_pre, 1)
                dve.wait_ge(s_pe0, 1)
                v.tensor_copy(gc[:].rearrange("p a t h -> p (a t h)"), F.gp[:, 0, 0:2 * NT * HA]).then_inc(s_pre, 1)
                dve.wait_ge(s_pre, 7)
                v.tensor_scalar(negc[:], gc[:, 0], -1.0, None, ALU.mult)
                v.tensor_tensor(dk[:], gc[:, 1], gc[:, 0], ALU.subtract).then_inc(s_pre, 1)
                v.tensor_scalar(beta[:], th[:], 0.5, 0.5, ALU.mult, ALU.add).then_inc(s_pre, 1)
                scale = float(P) ** -0.5
                v.memset(tab[:, :, 0, :], scale)
                v.memset(tab[:, :, 2, :], 1.0)
                dve.wait_ge(s_act0, 7)
                dve.wait_ge(s_pre, 9)
                v.tensor_scalar(tab[:, :, 1, :], gc[:, 0], scale, None, ALU.mult)
                v.tensor_copy(tab[:, :, 3, :], beta[:])
                v.tensor_tensor(tab[:, :, 4, :], beta[:], gc[:, 0], ALU.mult)
                v.tensor_copy(tab[:, :, 5, :], dk[:]).then_inc(s_pre, 1)
                dve.wait_ge(s_pre, 10)
                for s in F.credits_dve() + (s_oss, s_oms, s_on, s_oa, s_su, s_msk, s_mx, s_nm, s_dn, s_rc, s_pr, s_d8, s_d9):
                    dve.sem_inc(s, 1)
                with dve.Fori(0, NT) as t:
                    norms, scale_, decayed, start_x, step_x = front_dve(
                        nc, dve, F, k, t, lambda lo, hi: tab[:, bass.ds(t, 1), lo:hi, :].rearrange("p a f h -> p (a f) h"),
                        wide(beta[:, bass.ds(t, 1), :].rearrange("p a h -> p (a h)"), P),
                        lambda: dve.wait_ge(s_s, was(t)), lambda: dve.wait_ge(s_o, was(t)))
                    norms()
                    scale_()
                    dve.wait_ge(s_sc, now(t))
                    dve.wait_ge(s_bm, now(t))
                    dve.wait_ge(s_pt, was(t))
                    v.scalar_tensor_tensor(sm[:], sp_[:].rearrange("p b (h q) -> p (b h) q", h=2), float(DB) ** -0.5,
                                           k["band_now"][:].unsqueeze(1).broadcast_to([P, HB, 2 * W]), ALU.mult, ALU.add
                                           ).then_inc(s_msk, 1)
                    decayed()
                    start_x()
                    dve.wait_ge(s_msk, now(t))
                    dve.wait_ge(s_nm, was(t))
                    dve.wait_ge(s_es, was(t))
                    v.tensor_reduce(mx[:], sm[:], AX.X, ALU.max).then_inc(s_mx, 1)
                    dve.wait_ge(s_mx, now(t))
                    dve.wait_ge(s_ex, was(t))
                    dve.wait_ge(s_dn, was(t))
                    v.tensor_tensor(nm[:], mx[:], k["sink"][:], ALU.max).then_inc(s_d9, 1)
                    dve.wait_ge(s_d9, now(t))
                    v.tensor_tensor(esk[:], k["sink"][:], nm[:], ALU.subtract).then_inc(s_d8, 1)
                    dve.wait_ge(s_d8, now(t))
                    v.tensor_scalar(nm[:], nm[:], -1.0, None, ALU.mult).then_inc(s_nm, 1)
                    step_x(1)
                    step_x(2)
                    dve.wait_ge(s_ex, now(t))
                    dve.wait_ge(s_es, now(t))
                    dve.wait_ge(s_pr, was(t))
                    v.tensor_tensor(rc[:], dn[:], esk[:], ALU.add).then_inc(s_dn, 1)
                    dve.wait_ge(s_dn, now(t))
                    v.reciprocal(rc[:], rc[:]).then_inc(s_rc, 1)
                    dve.wait_ge(s_rc, now(t))
                    v.tensor_tensor(sm[:], sm[:], wide(rc[:], 2 * W), ALU.mult).then_inc(s_pr, 1)
                    for lv in range(3, L):
                        step_x(lv)
                    dve.wait_ge(s_s, now(t))
                    for h in range(HA):
                        v.scalar_tensor_tensor(k["state"][:, h, :], k["state"][:, h, :],
                                               gl[:, bass.ds(t, 1), h:h + 1].rearrange("p a h -> p (a h)"),
                                               F.gp[:, 3, h * P:(h + 1) * P], ALU.mult, ALU.add).then_inc(s_su, 1)
                    dve.wait_ge(s_osq, now(t))
                    v.tensor_reduce(oss[:], osq[:], AX.X, ALU.add).then_inc(s_oss, 1)
                    dve.wait_ge(s_oss, now(t))
                    v.tensor_scalar(oms[:], oss[:], 1.0 / P, EPS, ALU.mult, ALU.add).then_inc(s_oms, 1)
                    dve.wait_ge(s_ors, t + 1)
                    v.tensor_tensor(on[:], F.gp[:, 2, :].rearrange("p (h d) -> p h d", h=HA), wide(ors[:], P), ALU.mult
                                    ).then_inc(s_on, 1)
                    dve.wait_ge(s_ot, now(t))
                    dve.wait_ge(s_z, now(t) * 16)
                    dve.wait_ge(s_ost, was(t) * 16)
                    v.scalar_tensor_tensor(oaT[:].rearrange("p h q -> p (h q)"), F.gp[:, 0, :], k["vcol"][:, V_GDN:V_GDN + 1],
                                           zT[:].rearrange("p h q -> p (h q)"), ALU.mult, ALU.mult).then_inc(s_oa, 1)
                dve.wait_ge(s_pe0, 2)
                v.tensor_copy(kl[:], sp_[:, 1, 0:P])
                v.tensor_copy(k["xrow"][:], sp_[0:36, 2, 0:P]).then_inc(s_fin0, 1)

            @block.gpsimd
            def _(pool):
                g = nc.gpsimd
                for s in (F.s_g, F.s_rs, F.s_c, s_bm):
                    pool.sem_inc(s, 1)
                pool.wait_ge(s_pre, 10)
                pool.sem_inc(s_bm, 1)
                with pool.Fori(0, NT) as t:
                    place, rsqrt, cut = front_pool(nc, pool, F, k, t, gg[:, bass.ds(t, 1), :].rearrange("p a h -> p (a h)"),
                                                   lambda lv: k["lev"][:, lv, :])
                    place()
                    rsqrt()
                    pool.wait_ge(s_msk, now(t))
                    g.tensor_tensor(k["band_now"][:, 0:W], k["band"][:, 0:W], k["ones"][:], ALU.mult).then_inc(s_bm, 1)
                    cut()
                    pool.wait_ge(s_oms, now(t))
                    g.tensor_tensor(ors[:], oms[:], k["nhalf"][:, 0:HA], ALU.pow).then_inc(s_ors, 1)
                pool.wait_ge(s_obst, 16 * (NT + 1))
                pool.wait_ge(s_ost, 16 * (NT + 1))
                pool.wait_ge(s_su, now(NT - 1, HA))
                pool.dma_start(io["ssm_prompt"].rearrange("a b h k v -> k (a b h) v"), k["state"][:]).then_inc(s_fin, 16)
                pool.dma_start(io["swa_v_prompt"].rearrange("a b w g d -> (a b w) (g d)"), vt[:, 1, :]).then_inc(s_fin, 16)
                pool.wait_ge(s_fin0, 1)
                pool.dma_start(io["swa_k_prompt"].rearrange("a b w g d -> (a b w) (g d)"), kl[:]).then_inc(s_fin, 16)
                pool.wait_ge(s_fin, 48)
        m.clear_sems()


def sample_mixer(nc, io, k):
    with ExitStack() as ctx:
        m = Mem(nc, ctx)
        F = Front(m, "s_", TS, 2)
        L = F.levels
        cv = m.sb("s_conv", [P, CC, NB, NS])
        tp = m.sb("s_tap", [P, CC, NB, NS])
        zt = m.sb("s_z_tanh", [P, HA, TS])
        zs = m.sb("s_z_silu", [P, HA, TS])
        th, beta, xa, ax, na, gg, gc0, gcx, negc, dk = (m.sb("s_" + x, [TS, HA]) for x in (
            "beta_tanh", "beta", "a_biased", "a_abs", "a_neg", "g", "gc", "gc_exp", "gc_neg", "g_to_last"))
        ea = m.sb("s_decay_rate", [TS, HA])
        gt = m.sb("s_g_total", [TS, HA])
        gl = m.sb("s_g_last_exp", [P, HA, NB])
        tab = m.sb("s_factor_table", [TS, 6, HA])
        s0 = m.sb("s_state", [P, NB, HA, P])
        kgm = m.sb("s_kg_of_batch", [TS, NB, HA, P])
        vnT = m.sb("s_v_newT", [P, HA, TS])
        vn = m.sb("s_v_new", [TS, HA, P])
        oT = m.sb("s_oT", [P, HA, TS])
        osq = m.sb("s_o_squares", [TS, HA, P])
        oss, oms, ors = (m.sb("s_" + x, [TS, HA]) for x in ("o_sumsq", "o_meansq", "o_rrms"))
        on = m.sb("s_o_normed", [TS, HA, P])
        kc, vc = m.sb("s_cache_k", [P, NB, P]), m.sb("s_cache_v", [P, NB, P])
        kcT = m.sb("s_kT", [P, NB, W + NS])
        vnew = m.sb("s_v_rows", [NS, NB, P])
        qS = m.sb("s_q_heads", [P, 4, TS])
        qB = m.sb("s_q_rows", [P, NB, NS, 4])
        sc = m.sb("s_scores", [16, NB, 2, W + NS])
        mx, nm, esk, dn, rc = (m.sb("s_" + x, [16, NB, 2]) for x in ("max", "max_sink", "sink_exp", "prob_sum", "recip"))
        pcT = m.sb("s_probsT", [P, NB, 2, 16])
        pnT = m.sb("s_probsT_new", [NS, NB, 2, 16])
        rows = m.sb("s_rows", [TS, CC + 2, P])
        ap = m.ps("s_attn_ps", [P, 4, 512])
        s_ld, s_st0, s_q = m.sem("s_cache_loaded"), m.sem("s_state_loaded"), m.sem("s_q_moved")
        s_pre, s_cv, s_act, s_pes = m.sem("s_tables_step"), m.sem("s_conv_step"), m.sem("s_act_step"), m.sem("s_cumsums_summed")
        s_zz, s_gl = m.sem("s_z_done"), m.sem("s_g_last_done")
        s_kgm, s_v, s_ve, s_vt, s_vn = (m.sem(x) for x in ("s_kg_masked", "s_v_newT_done", "s_v_newT_read", "s_v_new_turned", "s_v_new_read"))
        s_o, s_oe, s_ot, s_osq, s_oss, s_oms, s_ors, s_on, s_o2, s_oa = (m.sem(x) for x in (
            "s_oT_done", "s_oT_read", "s_o_turned", "s_o_squared", "s_o_sumsq_done", "s_o_meansq_done", "s_o_rrms_done",
            "s_o_normed_done", "s_o_turned_back", "s_o_out"))
        s_add, s_new = m.sem("s_state_added"), m.sem("s_state_new")
        s_rt, s_rr, s_kt, s_ke, s_qb = (m.sem(x) for x in ("s_rows_turned", "s_rows_read", "s_kT_turned", "s_kT_read", "s_q_placed"))
        s_sc, s_mk, s_sm, s_pt, s_pe2, s_av, s_ob = (m.sem(x) for x in (
            "s_scores_done", "s_scores_masked", "s_softmax_step", "s_probs_turned", "s_probs_read", "s_attn_done", "s_attn_out"))
        s_out, s_rcp = m.sem("s_stored"), m.sem("s_recip_done")
        with nc.Block() as block:
            @block.sync
            def _(sp):
                sp.dma_start(kc[:], io["cache_swa_k"].rearrange("a b w g d -> w (a b) (g d)")).then_inc(s_ld, 16)
                sp.dma_start(vc[:], io["cache_swa_v"].rearrange("a b w g d -> w (a b) (g d)")).then_inc(s_ld, 16)
                for h in range(HB):
                    sp.dma_start(qS[64 * (h // 4):64 * (h // 4) + 64, h % 4, :],
                                 k["projS"][64 * (h % 2):64 * (h % 2) + 64, 16 + h // 2, :]).then_inc(s_q, 16)
                sp.dma_start(s0[:], io["state_ssm"].rearrange("a b h k v -> k (a b) h v")).then_inc(s_st0, 16)
                for name, cache in (("swa_k_sample", "cache_swa_k"), ("swa_v_sample", "cache_swa_v")):
                    sp.dma_start(io[name].rearrange("a b w g d -> (a b) (w g d)")[:, 0:(W - NS) * P],
                                 io[cache].rearrange("a b w g d -> (a b) (w g d)")[:, NS * P:W * P]).then_inc(s_out, 16)
                sp.dma_start(io["conv_prompt"].rearrange("a b i (c p) -> (a b i c) p", p=P), k["xrow"][:]).then_inc(s_out, 16)
                sp.wait_ge(s_rr, 1)
                for b in range(NB):
                    sp.dma_start(io["conv_sample"][0, b], rows[NS * b + 1:NS * b + NS, 0:CC, :].rearrange("t c p -> t (c p)")
                                 ).then_inc(s_out, 16)
                    for j, name in enumerate(("swa_k_sample", "swa_v_sample")):
                        sp.dma_start(io[name].rearrange("a b w g d -> (a b) w (g d)")[b, W - NS:W],
                                     rows[NS * b:NS * b + NS, CC + j, :]).then_inc(s_out, 16)
                for b in range(NB):
                    sp.wait_ge(s_new, HA * (b + 1))
                    sp.dma_start(io["ssm_sample"].rearrange("a b h k v -> k (a b) h v")[:, b], s0[:, b]).then_inc(s_out, 16)
                sp.wait_ge(s_out, 16 * (3 + 3 * NB + NB))

            @block.tensor
            def _(pe):
                mm, tr, ident = nc.tensor.matmul, nc.tensor.transpose, k["ident"]
                for s in F.credits_pe():
                    pe.sem_inc(s, 1)
                for c in range(CC + 2):
                    src = k["projS"][:, c if c < CC else c + 8, :]
                    last = tr(ap[0:TS, c // 4, (c % 4) * P:(c % 4) * P + P], src, ident[:])
                last.then_inc(s_rt, 1)
                pe.wait_ge(s_pre, 6)
                mm(F.gp[0:TS, 0, 0:HA], k["uts"][:], gg[:], start=True, stop=True)
                mm(F.gp[0:TS, 0, HA:2 * HA], k["same"][:], gg[:], start=True, stop=True)
                for h in range(HA):
                    last = mm(F.gp[:, 1, h * NB:(h + 1) * NB], gg[:, h:h + 1].broadcast_to([TS, P]), k["seg"][:], start=True, stop=True)
                last.then_inc(s_pes, 1)
                pe.wait_ge(s_pre, 7)
                pe.wait_ge(s_gl, 1)
                turn, spread, back, gram, level0, level_y, level_z, w = front_pe(
                    nc, pe, F, k, 0, k["uts"][:], k["negs"][:], lambda: None)
                turn()
                spread()
                pe.wait_ge(s_ld, 32)
                pe.wait_ge(s_rr, 1)
                for b in range(NB):
                    tr(ap[:, b // 4, (b % 4) * P:(b % 4) * P + P], kc[:, b, :], ident[:])
                    last = tr(ap[0:NS, 2 + b // 4, (b % 4) * P:(b % 4) * P + P], k["projS"][:, 21, NS * b:NS * b + NS], ident[:])
                last.then_inc(s_kt, 1)
                back()
                gram()
                level0()
                level_y(1)
                level_z(1)
                w()
                for half in range(2):
                    if half == 0:
                        pe.wait_ge(s_ke, 1)
                        pe.wait_ge(s_qb, 1)
                    else:
                        pe.wait_ge(s_mk, 4)
                    for j in range(4):
                        b = 4 * half + j
                        for g in range(2):
                            at = slice(64 * g, 64 * g + 64)
                            o = (j % 2) * 256
                            last = mm(ap[0:16, 2 * (j // 2) + g, o:o + W + NS], qB[at, b].rearrange("p s c -> p (s c)"),
                                      kcT[at, b, :], start=True, stop=True)
                    last.then_inc(s_sc, 1)
                pe.wait_ge(F.s_nw, now(0))
                pe.wait_ge(s_st0, 16)
                for h in range(HA):
                    at = F.gp[:, 1, h * TS:(h + 1) * TS]
                    mm(at, F.vb[:, h, :], F.xx[:, 1, h, :], start=True, stop=False)
                    for b in range(NB):
                        last = mm(F.gp[:, 1, h * TS + NS * b:h * TS + NS * b + NS], s0[:, b, h, :],
                                  F.nwT[:, h, NS * b:NS * b + NS], start=False, stop=(b == NB - 1))
                last.then_inc(s_v, 1)
                pe.wait_ge(s_ve, 1)
                for h in range(HA):
                    last = tr(F.gp[0:TS, 2, h * P:(h + 1) * P], vnT[:, h, :], ident[:])
                last.then_inc(s_vt, 1)
                pe.wait_ge(s_vn, 1)
                for h in range(HA):
                    mm(F.gp[:, 3, h * TS:(h + 1) * TS], vn[:, h, :], F.al[:, h, 1, :], start=True, stop=False)
                    for b in range(NB):
                        last = mm(F.gp[:, 3, h * TS + NS * b:h * TS + NS * b + NS], s0[:, b, h, :],
                                  F.qgT[:, h, NS * b:NS * b + NS], start=False, stop=(b == NB - 1))
                last.then_inc(s_o, 1)
                pe.wait_ge(s_oe, 1)
                for h in range(HA):
                    last = tr(F.gp[0:TS, 0, h * P:(h + 1) * P], oT[:, h, :], ident[:])
                last.then_inc(s_ot, 1)
                pe.wait_ge(s_sm, 8)
                for b in range(NB):
                    for g in range(2):
                        o = (2 * b + g) * 16
                        tr(ap[:, 0, o:o + 16], sc[:, b, g, 0:W], ident[0:16, 0:16])
                        last = tr(ap[0:NS, 1, o:o + 16], sc[:, b, g, W:W + NS], ident[0:16, 0:16])
                last.then_inc(s_pt, 1)
                pe.wait_ge(s_pe2, 1)
                for b in range(NB):
                    for g in range(2):
                        at = ap[64 * g:64 * g + 64, 2, b * 16:b * 16 + 16]
                        mm(at, vc[:, b, 64 * g:64 * g + 64], pcT[:, b, g, :], start=True, stop=False)
                        last = mm(at, vnew[:, b, 64 * g:64 * g + 64], pnT[:, b, g, :], start=False, stop=True)
                last.then_inc(s_av, 1)
                pe.wait_ge(s_on, 1)
                for h in range(HA):
                    last = tr(F.gp[:, 1, h * TS:(h + 1) * TS], on[:, h, :], ident[0:TS, 0:TS])
                last.then_inc(s_o2, 1)
                pe.wait_ge(s_kgm, 1)
                pe.wait_ge(s_ob, 1)
                for b in range(NB):
                    if b >= 4:
                        pe.wait_ge(s_new, HA * (b - 3))
                    for h in range(HA):
                        last = mm(ap[:, b % 4, h * P:(h + 1) * P], kgm[:, b, h, :], vn[:, h, :], start=True, stop=True)
                    last.then_inc(s_add, 1)

            @block.scalar
            def _(act):
                a = nc.scalar
                for s in F.credits_act():
                    act.sem_inc(s, 1)
                a.activation(th[:], k["ba_s"][:, 0:HA], ACT.Tanh, scale=0.5).then_inc(s_act, 1)
                a.activation(zt[:], k["projS"][:, 12:16, :], ACT.Tanh).then_inc(s_zz, 1)
                a.activation(ea[:], k["alog"][0:TS, :], ACT.Exp).then_inc(s_act, 1)
                act.wait_ge(s_pre, 3)
                a.activation(ax[:], ax[:], ACT.Exp, scale=-1.0).then_inc(s_act, 1)
                act.wait_ge(s_act, 3)
                a.activation(ax[:], ax[:], ACT.Ln, bias=1.0).then_inc(s_act, 1)
                act.wait_ge(s_cv, 7)
                a.activation(tp[:], cv[:], ACT.Tanh).then_inc(s_act, 1)
                act.wait_ge(s_rt, 1)
                a.copy(rows[:].rearrange("p c d -> p (c d)")[:, 0:1024], ap[0:TS, 0:2, :].rearrange("p b c -> p (b c)"))
                a.copy(rows[:].rearrange("p c d -> p (c d)")[:, 1024:14 * P], ap[0:TS, 2:4, :].rearrange("p b c -> p (b c)")[:, 0:768]
                       ).then_inc(s_rr, 1)
                act.wait_ge(s_pre, 8)
                a.activation(gcx[:], gc0[:], ACT.Exp)
                a.activation(dk[:], dk[:], ACT.Exp).then_inc(s_act, 1)
                a.activation(gl[:].rearrange("p h b -> p (h b)"), F.gp[:, 1, 0:HA * NB], ACT.Exp).then_inc(s_gl, 1)
                square, decay, read_back, read_y, read_w = front_act(
                    nc, act, F, 0, lambda h: negc[:, h:h + 1], lambda: None, lambda: None, lambda: None)
                square()
                decay()
                act.wait_ge(s_kt, 1)
                a.copy(kcT[:, :, 0:W], ap[:, 0:2, :].rearrange("p b (c w) -> p (b c) w", w=P))
                a.copy(vnew[:].rearrange("p b d -> p (b d)"), ap[0:NS, 2:4, :].rearrange("p b c -> p (b c)")).then_inc(s_ke, 1)
                read_back()
                read_y(1)
                read_w()
                act.wait_ge(s_v, 1)
                a.copy(vnT[:].rearrange("p h i -> p (h i)"), F.gp[:, 1, 0:P]).then_inc(s_ve, 1)
                act.wait_ge(s_vt, 1)
                a.copy(vn[:].rearrange("p h d -> p (h d)"), F.gp[0:TS, 2, :]).then_inc(s_vn, 1)
                act.wait_ge(s_sm, 4)
                a.activation(sc[:], sc[:], ACT.Exp)
                a.activation(esk[:], esk[:], ACT.Exp).then_inc(s_sm, 1)
                act.wait_ge(s_o, 1)
                a.copy(oT[:].rearrange("p h i -> p (h i)"), F.gp[:, 3, 0:P]).then_inc(s_oe, 1)
                act.wait_ge(s_ot, 1)
                a.activation(osq[:].rearrange("p h d -> p (h d)"), F.gp[0:TS, 0, :], ACT.Square).then_inc(s_osq, 1)
                act.wait_ge(s_pt, 1)
                a.copy(pcT[:].rearrange("p b g r -> p (b g r)"), ap[:, 0, 0:256])
                a.copy(pnT[:].rearrange("p b g r -> p (b g r)"), ap[0:NS, 1, 0:256]).then_inc(s_pe2, 1)

            @block.vector
            def _(dve):
                v = nc.vector
                wide = lambda x, d: x.unsqueeze(len(x.shape)).broadcast_to(list(x.shape) + [d])
                for s in F.credits_dve():
                    dve.sem_inc(s, 1)
                v.tensor_tensor(xa[:], k["ba_s"][:, HA:2 * HA], k["dtb"][0:TS, :], ALU.add).then_inc(s_pre, 1)
                dve.wait_ge(s_pre, 1)
                v.tensor_scalar(na[:], xa[:], -1.0, None, ALU.mult).then_inc(s_pre, 1)
                dve.wait_ge(s_pre, 2)
                v.tensor_tensor(ax[:], xa[:], na[:], ALU.max).then_inc(s_pre, 1)
                dve.wait_ge(s_act, 4)
                v.scalar_tensor_tensor(xa[:], xa[:], 0.0, ax[:], ALU.max, ALU.add).then_inc(s_pre, 1)
                dve.wait_ge(s_pre, 4)
                v.tensor_scalar(xa[:], xa[:], -1.0, None, ALU.mult).then_inc(s_pre, 1)
                dve.wait_ge(s_pre, 5)
                v.tensor_tensor(gg[:], xa[:], ea[:], ALU.mult).then_inc(s_pre, 1)
                v.tensor_copy(k["xs_pad"][:, :, :, CW - 1:], k["projS"][:, 0:CC, :].rearrange("p c (b s) -> p c b s", s=NS)
                              ).then_inc(s_cv, 1)
                dve.wait_ge(s_cv, 1)
                tap = lambda i: k["taps"][:, i * CC:(i + 1) * CC].unsqueeze(2).unsqueeze(3).broadcast_to([P, CC, NB, NS])
                step = 1
                v.tensor_tensor(cv[:], k["xs_pad"][:, :, :, 0:NS], tap(0), ALU.mult)
                for i in range(1, CW):
                    if i > 1:
                        dve.wait_ge(s_cv, step)
                    v.tensor_tensor(tp[:], k["xs_pad"][:, :, :, i:i + NS], tap(i), ALU.mult).then_inc(s_cv, 1)
                    step += 1
                    dve.wait_ge(s_cv, step)
                    v.tensor_tensor(cv[:], cv[:], tp[:], ALU.add).then_inc(s_cv, 1)
                    step += 1
                dve.wait_ge(s_act, 5)
                v.scalar_tensor_tensor(F.qkv[:].rearrange("p c t -> p (c t)"), tp[:].rearrange("p c b s -> p (c b s)"), 1.0,
                                       cv[:].rearrange("p c b s -> p (c b s)"), ALU.add, ALU.mult).then_inc(F.s_in, 32)
                dve.wait_ge(s_zz, 1)
                v.scalar_tensor_tensor(zs[:].rearrange("p h t -> p (h t)"), zt[:].rearrange("p h t -> p (h t)"), 1.0,
                                       k["projS"][:, 12:16, :].rearrange("p h t -> p (h t)"), ALU.add, ALU.mult).then_inc(s_zz, 1)
                dve.wait_ge(s_pes, 1)
                v.tensor_copy(gc0[:], F.gp[0:TS, 0, 0:HA])
                v.tensor_copy(gt[:], F.gp[0:TS, 0, HA:2 * HA]).then_inc(s_pre, 1)
                dve.wait_ge(s_pre, 7)
                v.tensor_scalar(negc[:], gc0[:], -1.0, None, ALU.mult)
                v.tensor_tensor(dk[:], gt[:], gc0[:], ALU.subtract).then_inc(s_pre, 1)
                v.tensor_scalar(beta[:], th[:], 0.5, 0.5, ALU.mult, ALU.add).then_inc(s_pre, 1)
                scale = float(P) ** -0.5
                v.memset(tab[:, 0, :], scale)
                v.memset(tab[:, 2, :], 1.0)
                dve.wait_ge(s_act, 6)
                dve.wait_ge(s_pre, 9)
                v.tensor_scalar(tab[:, 1, :], gcx[:], scale, None, ALU.mult)
                v.tensor_copy(tab[:, 3, :], beta[:])
                v.tensor_tensor(tab[:, 4, :], beta[:], gcx[:], ALU.mult)
                v.tensor_copy(tab[:, 5, :], dk[:]).then_inc(s_pre, 1)
                dve.wait_ge(s_pre, 10)
                norms, scale_, decayed, start_x, step_x = front_dve(
                    nc, dve, F, k, 0, lambda lo, hi: tab[:, lo:hi, :], wide(beta[:], P), lambda: None, lambda: None)
                norms()
                v.tensor_copy(kcT[:, :, W:W + NS], k["projS"][:, 20, :].rearrange("p (b s) -> p b s", s=NS))
                dve.wait_ge(s_q, 16 * HB)
                v.tensor_copy(qB[:], qS[:].rearrange("p c (b s) -> p b s c", s=NS)).then_inc(s_qb, 1)
                scale_()
                decayed()
                start_x()
                step_x(1)
                dve.wait_ge(F.s_sc, now(0))
                v.tensor_tensor(kgm[:].rearrange("t b h d -> t b (h d)"),
                                F.kk[:, 3].rearrange("t h d -> t (h d)").unsqueeze(1).broadcast_to([TS, NB, HA * P]),
                                wide(k["seg"][:], HA * P), ALU.mult).then_inc(s_kgm, 1)
                for half in range(2):
                    dve.wait_ge(s_sc, half + 1)
                    for bank in range(4):
                        j, g = bank // 2, bank % 2
                        b = 4 * half + 2 * j
                        v.scalar_tensor_tensor(sc[:, b:b + 2, g, :], ap[0:16, bank, :].rearrange("p (e q) -> p e q", e=2)[:, :, 0:W + NS],
                                               float(DB) ** -0.5, k["masks"][:].unsqueeze(1).broadcast_to([16, 2, W + NS]),
                                               ALU.mult, ALU.add).then_inc(s_mk, 1)
                dve.wait_ge(s_mk, 8)
                v.tensor_reduce(mx[:], sc[:], AX.X, ALU.max).then_inc(s_sm, 1)
                dve.wait_ge(s_sm, 1)
                sink = k["sink_s"][:].unsqueeze(1).broadcast_to([16, NB, 2])
                v.tensor_tensor(nm[:], mx[:], sink, ALU.max).then_inc(s_sm, 1)
                dve.wait_ge(s_sm, 2)
                v.tensor_tensor(esk[:], sink, nm[:], ALU.subtract).then_inc(s_sm, 1)
                v.tensor_tensor(sc[:], sc[:], wide(nm[:], W + NS), ALU.subtract).then_inc(s_sm, 1)
                dve.wait_ge(s_sm, 5)
                v.tensor_reduce(dn[:], sc[:], AX.X, ALU.add).then_inc(s_sm, 1)
                dve.wait_ge(s_sm, 6)
                v.tensor_tensor(dn[:], dn[:], esk[:], ALU.add).then_inc(s_sm, 1)
                dve.wait_ge(s_sm, 7)
                v.reciprocal(rc[:], dn[:]).then_inc(s_rcp, 1)
                dve.wait_ge(s_rcp, 1)
                v.tensor_tensor(sc[:], sc[:], wide(rc[:], W + NS), ALU.mult).then_inc(s_sm, 1)
                dve.wait_ge(s_osq, 1)
                v.tensor_reduce(oss[:], osq[:], AX.X, ALU.add).then_inc(s_oss, 1)
                dve.wait_ge(s_oss, 1)
                v.tensor_scalar(oms[:], oss[:], 1.0 / P, EPS, ALU.mult, ALU.add).then_inc(s_oms, 1)
                dve.wait_ge(s_ors, 1)
                v.tensor_tensor(on[:], F.gp[0:TS, 0, :].rearrange("p (h d) -> p h d", h=HA), wide(ors[:], P), ALU.mult).then_inc(s_on, 1)
                dve.wait_ge(s_av, 1)
                v.tensor_copy(k["oS"][:, 4:8, :].rearrange("p c (b s) -> p c b s", s=NS),
                              ap[:, 2, 0:P].rearrange("p (b s c) -> p c b s", b=NB, s=NS)).then_inc(s_ob, 1)
                dve.wait_ge(s_o2, 1)
                dve.wait_ge(s_zz, 2)
                v.scalar_tensor_tensor(k["oS"][:, 0:4, :].rearrange("p h t -> p (h t)"), F.gp[:, 1, 0:P], k["vcol"][:, V_GDN:V_GDN + 1],
                                       zs[:].rearrange("p h t -> p (h t)"), ALU.mult, ALU.mult).then_inc(s_oa, 1)
                for b in range(NB):
                    dve.wait_ge(s_add, b + 1)
                    for h in range(HA):
                        v.scalar_tensor_tensor(s0[:, b, h, :], s0[:, b, h, :], gl[:, h, b:b + 1], ap[:, b % 4, h * P:(h + 1) * P],
                                               ALU.mult, ALU.add).then_inc(s_new, 1)

            @block.gpsimd
            def _(pool):
                g = nc.gpsimd
                for s in (F.s_g, F.s_rs, F.s_c):
                    pool.sem_inc(s, 1)
                pool.wait_ge(s_pre, 6)
                place, rsqrt, cut = front_pool(nc, pool, F, k, 0, gg[:], lambda lv: k["lev"][0:TS, lv, 0:TS])
                place()
                rsqrt()
                cut()
                pool.wait_ge(s_oms, 1)
                g.tensor_tensor(ors[:], oms[:], k["nhalf"][0:TS, 0:HA], ALU.pow).then_inc(s_ors, 1)
        m.clear_sems()


def spread_gate(nc, pe, k, which, rows, at, sample, out):
    for c in range(KD):
        o = out[at:at + rows, c // 4, (c % 4) * P:(c % 4) * P + P]
        if sample:
            last = nc.tensor.matmul(o, k["gate_col_s"][:, which, c].rearrange("p b s -> p (b s)"), k["ident"][:],
                                    start=True, stop=True)
        else:
            last = nc.tensor.matmul(o, k["gate_col"][:, which, c:c + 1].broadcast_to([P, P]), k["ident"][:], start=True, stop=True)
    return last


def out_projection(nc, io, k):
    with ExitStack() as ctx:
        m = Mem(nc, ctx)
        wr = m.sb("w_o_raw", [P, D])
        whi = m.sb("w_o_hi", [P, KD, D], FR)
        wlo = m.sb("w_o_lo", [P, KD, D], FR)
        gate = m.sb("gate_rows", [P, 2, 512])
        gate_s = m.sb("gate_rows_s", [TS, 2, 512])
        ot = m.sb("mixed_T", [P, 2, KD, P])
        ohi = m.sb("mixed_hi", [P, 2, KD, P], FR)
        olo = m.sb("mixed_lo", [P, 2, KD, P], FR)
        xt = m.sb("x_in", [P, 2, D])
        x1 = m.sb("x_mid", [P, 2, D])
        xn = m.sb("x_mid_normed", [P, 2, D])
        sq = m.sb("out_squares", [P, D])
        h2 = m.sb("h2_tile", [P, 2, KD, P])
        sm = m.sb("out_scalars", [P, 2, 2, 4])
        po = m.ps("out_ps", [P, 2, 2, 512])
        pt = m.ps("turn_ps", [P, 2, 2, 512])
        s_w, s_wh, s_wl = m.sem("w_o_loaded"), m.sem("w_o_hi_split"), m.sem("w_o_lo_split")
        s_gt, s_gr = m.sem("gates_spread"), m.sem("gates_read")
        s_o = [m.sem(f"mixed_loaded_{p}") for p in range(2)]
        s_x = [m.sem(f"x_in_loaded_{p}") for p in range(2)]
        s_x1s = [m.sem(f"x_mid_stored_{p}") for p in range(2)]
        s_h2s = [m.sem(f"h2_stored_{p}") for p in range(2)]
        s_oh, s_ol, s_mm = m.sem("mixed_hi_split"), m.sem("mixed_lo_split"), m.sem("out_summed")
        s_sa, s_ma, s_ra, s_t, s_x1 = (m.sem(x) for x in ("mix_sumsq", "mix_meansq", "mix_rrms", "mix_gated", "x_mid_done"))
        s_sb, s_mb, s_rb, s_xn = (m.sem(x) for x in ("mid_sumsq", "mid_meansq", "mid_rrms", "mid_normed"))
        s_tr, s_ht, s_h2 = m.sem("mid_turned"), m.sem("h2_scaled"), m.sem("h2_done")
        h2T = io["h2T"]

        def skeleton(eng, pre, post):
            pre(0, 0, 0)
            with eng.Fori(0, NT // 2 - 1) as i:
                pre(i * 2 + 1, 1, i)
                post(i * 2, 0, i)
                pre(i * 2 + 2, 0, i + 1)
                post(i * 2 + 1, 1, i)
            last = NT // 2 - 1
            pre(NT - 1, 1, last)
            post(NT - 2, 0, last)
            pre(NT, 0, last + 1)
            post(NT - 1, 1, last)
            post(NT, 0, last + 1)

        is_sample = lambda t: isinstance(t, int) and t == NT
        rows = lambda t: TS if is_sample(t) else P
        with nc.Block() as block:
            @block.sync
            def _(sp):
                for c in range(KD):
                    sp.wait_ge(s_wl, c)
                    for g in range(2):
                        r = c * P + g * DB if c < 4 else HA * P + (4 * g + c - 4) * DB
                        sp.dma_start(wr[64 * g:64 * g + 64, :], io["w_o"][r:r + DB, :]).then_inc(s_w, 16)
                for p in range(2):
                    sp.sem_inc(s_x1s[p], 16)
                    sp.sem_inc(s_h2s[p], 16)

                def load(t, p, u):
                    sp.wait_ge(s_ol, t + 1)
                    if not is_sample(t):
                        sp.dma_start(ot[:, p], io["oT"][:, :, bass.ds(t * P, P)].rearrange("c p t -> p c t")).then_inc(s_o[p], 16)
                    sp.wait_ge(s_x1, t + 1)
                    src = io["xs"] if is_sample(t) else io["x"][bass.ds(t * P, P), :]
                    sp.dma_start(xt[0:rows(t), p], src).then_inc(s_x[p], 16)

                def store(t, p, u):
                    n = rows(t)
                    sp.wait_ge(s_x1, t + 3)
                    sp.dma_start(io["x1"][bass.ds(t * P, n), :], x1[0:n, p]).then_inc(s_x1s[p], 16)
                    sp.wait_ge(s_h2, t + 3)
                    sp.dma_start(h2T[bass.ds(t, 1), :, :, 0:n].rearrange("a p c t -> (a p) c t"), h2[:, p, :, 0:n]).then_inc(s_h2s[p], 16)

                load(0, 0, 0)
                load(1, 1, 0)
                with sp.Fori(0, NT // 2 - 1) as i:
                    for p in range(2):
                        load(i * 2 + p + 2, p, i + 1)
                        store(i * 2 + p, p, i)
                load(NT, 0, NT // 2)
                store(NT - 2, 0, NT // 2 - 1)
                store(NT - 1, 1, NT // 2 - 1)
                store(NT, 0, NT // 2)
                for p in range(2):
                    n = (NT // 2 + 1 + (p == 0)) * 16
                    sp.wait_ge(s_x1s[p], n)
                    sp.wait_ge(s_h2s[p], n)

            @block.tensor
            def _(pe):
                for s in (s_mm, s_tr):
                    pe.sem_inc(s, 2)
                spread_gate(nc, pe, k, 0, P, 0, False, pt[:, 0]).then_inc(s_gt, 1)
                spread_gate(nc, pe, k, 0, TS, 0, True, pt[:, 1]).then_inc(s_gt, 1)

                def pre(t, p, u):
                    if isinstance(t, int) and t == 0:
                        pe.wait_ge(s_wl, KD)
                        pe.wait_ge(s_gr, 2)
                    pe.wait_ge(s_oh, t + 3)
                    pe.wait_ge(s_ol, t + 3)
                    pe.wait_ge(s_t, t + 1)
                    for kk in range(KD):
                        for h in range(2):
                            at = slice(h * 512, (h + 1) * 512)
                            last = three_pass(nc, po[:, p, h, :], ohi[:, p, kk, :], olo[:, p, kk, :],
                                              whi[:, kk, at], wlo[:, kk, at], kk == 0, kk == KD - 1)
                    last.then_inc(s_mm, 1)

                def post(t, p, u):
                    n = rows(t)
                    pe.wait_ge(s_xn, t + 3)
                    pe.wait_ge(s_ht, t + 1)
                    for c in range(KD):
                        last = nc.tensor.transpose(pt[:, p, c // 4, (c % 4) * P:(c % 4) * P + n], xn[0:n, p, c * P:(c + 1) * P],
                                                   k["ident"][0:n, 0:n])
                    last.then_inc(s_tr, 1)
                skeleton(pe, pre, post)

            @block.scalar
            def _(act):
                a = nc.scalar
                for s in (s_oh, s_sa, s_sb, s_xn):
                    act.sem_inc(s, 2)
                for c in range(KD):
                    act.wait_ge(s_w, 32 * (c + 1))
                    a.copy(whi[:, c], wr[:]).then_inc(s_wh, 1)
                act.wait_ge(s_gt, 1)
                a.copy(gate[:], pt[:, 0]).then_inc(s_gr, 1)
                act.wait_ge(s_gt, 2)
                a.copy(gate_s[:], pt[0:TS, 1]).then_inc(s_gr, 1)

                def pre(t, p, u):
                    act.wait_ge(s_mm, t + 1)
                    if is_sample(t):
                        a.copy(ohi[:, p, :, 0:TS], k["oS"][:]).then_inc(s_oh, 1)
                    else:
                        act.wait_ge(s_o[p], u * 16 + 16)
                        a.copy(ohi[:, p], ot[:, p]).then_inc(s_oh, 1)

                def post(t, p, u):
                    n = rows(t)
                    act.wait_ge(s_mm, t + 3)
                    act.wait_ge(s_sb, t + 2)
                    a.activation(sq[0:n].rearrange("p (b c) -> p b c", b=2), po[0:n, p], ACT.Square, accum_out=sm[0:n, p, 0, 0:1]
                                 ).then_inc(s_sa, 1)
                    act.wait_ge(s_x1, t + 3)
                    act.wait_ge(s_sa, t + 3)
                    a.activation(sq[0:n], x1[0:n, p], ACT.Square, accum_out=sm[0:n, p, 1, 0:1]).then_inc(s_sb, 1)
                    act.wait_ge(s_rb, t + 1)
                    act.wait_ge(s_tr, t + 1)
                    a.mul(xn[0:n, p], x1[0:n, p], sm[0:n, p, 1, 2:3]).then_inc(s_xn, 1)
                skeleton(act, pre, post)

            @block.gpsimd
            def _(pool):
                g = nc.gpsimd

                def rrms(t, p, norm, ready, done):
                    n = rows(t)
                    pool.wait_ge(ready, t + 3)
                    g.tensor_tensor(sm[0:n, p, norm, 2:3], sm[0:n, p, norm, 1:2], k["nhalf"][0:n, 0:1], ALU.pow).then_inc(done, 1)

                def post(t, p, u):
                    rrms(t, p, 0, s_ma, s_ra)
                    rrms(t, p, 1, s_mb, s_rb)
                skeleton(pool, lambda t, p, u: None, post)

            @block.vector
            def _(dve):
                v = nc.vector
                for s in (s_ol, s_ma, s_t, s_x1, s_mb, s_ht, s_h2):
                    dve.sem_inc(s, 2)
                for c in range(KD):
                    dve.wait_ge(s_wh, c + 1)
                    v.tensor_tensor(wlo[:, c], wr[:], whi[:, c].bitcast(F32), ALU.subtract).then_inc(s_wl, 1)

                def pre(t, p, u):
                    dve.wait_ge(s_oh, t + 3)
                    if is_sample(t):
                        v.tensor_tensor(olo[:, p, :, 0:TS], k["oS"][:], ohi[:, p, :, 0:TS].bitcast(F32), ALU.subtract).then_inc(s_ol, 1)
                    else:
                        v.tensor_tensor(olo[:, p], ot[:, p], ohi[:, p].bitcast(F32), ALU.subtract).then_inc(s_ol, 1)

                def post(t, p, u):
                    n = rows(t)
                    gr = gate_s if is_sample(t) else gate
                    dve.wait_ge(s_sa, t + 3)
                    v.tensor_scalar(sm[0:n, p, 0, 1:2], sm[0:n, p, 0, 0:1], 1.0 / D, EPS, ALU.mult, ALU.add).then_inc(s_ma, 1)
                    dve.wait_ge(s_ra, t + 1)
                    dve.wait_ge(s_x1s[p], u * 16 + 16)
                    x1v = x1[0:n, p].rearrange("p (b c) -> p b c", b=2)
                    v.scalar_tensor_tensor(x1v, po[0:n, p], sm[0:n, p, 0, 2:3], gr[0:n], ALU.mult, ALU.mult).then_inc(s_t, 1)
                    dve.wait_ge(s_t, t + 3)
                    dve.wait_ge(s_x[p], u * 16 + 16)
                    v.tensor_tensor(x1[0:n, p], x1[0:n, p], xt[0:n, p], ALU.add).then_inc(s_x1, 1)
                    dve.wait_ge(s_sb, t + 3)
                    v.tensor_scalar(sm[0:n, p, 1, 1:2], sm[0:n, p, 1, 0:1], 1.0 / D, EPS, ALU.mult, ALU.add).then_inc(s_mb, 1)
                    dve.wait_ge(s_tr, t + 3)
                    dve.wait_ge(s_h2s[p], u * 16 + 16)
                    if is_sample(t):
                        src = pt[:, p].rearrange("p a (b q) -> p (a b) q", q=P)[:, :, 0:TS].rearrange("p c (b s) -> p c b s", s=NS)
                        dst = h2[:, p, :, 0:TS].rearrange("p c (b s) -> p c b s", s=NS)
                        spread = lambda x: x[:, 1, :, 1:9].unsqueeze(3).broadcast_to([P, KD, NB, NS])
                        scale, shift = spread(k["mscale"]), spread(k["mshift"])
                    else:
                        src = pt[:, p].rearrange("p a (b q) -> p (a b) q", q=P)
                        dst = h2[:, p]
                        scale, shift = (k[x][:, 1].unsqueeze(2).broadcast_to([P, KD, P]) for x in ("pscale", "pshift"))
                    v.tensor_tensor(dst, src, scale, ALU.mult).then_inc(s_ht, 1)
                    dve.wait_ge(s_ht, t + 3)
                    v.tensor_tensor(dst, dst, shift, ALU.add).then_inc(s_h2, 1)
                skeleton(dve, pre, post)
        m.clear_sems()


def mlp(nc, io, k, half):
    with ExitStack() as ctx:
        m = Mem(nc, ctx)
        tiles = NT // 2 + (1 if half == 0 else 0)
        n = NT // 2 * P + (TS if half == 0 else 0)
        Q = 4
        qn = n // Q
        NG = FF // P // 2
        last0 = n - P
        tag = f"h{half}_"
        hhi, hlo = (m.sb(tag + x, [P, KD, n], FR) for x in ("h2_hi", "h2_lo"))
        ru = m.sb(tag + "relu", [P, 2, n])
        uhi, ulo = (m.sb(tag + x, [P, 2, 2, n], FR) for x in ("u_hi", "u_lo"))
        y = m.sb(tag + "y", [P, tiles, D])
        ur = m.sb(tag + "w_up_raw", [P, 2, KD, P])
        uwh, uwl = (m.sb(tag + x, [P, 2, KD, P], FR) for x in ("w_up_hi", "w_up_lo"))
        dr = m.sb(tag + "w_down_raw", [P, 2, D])
        dwh, dwl = (m.sb(tag + x, [P, 2, D], FR) for x in ("w_down_hi", "w_down_lo"))
        gate = m.sb(tag + "gate_rows", [P, 2, 512])
        gate_s = m.sb(tag + "gate_rows_s", [P, 2, 512]) if half == 0 else None
        ss, ms, rr = (m.sb(tag + x, [P, tiles]) for x in ("y_sumsq", "y_meansq", "y_rrms"))
        pu = m.ps(tag + "up_ps", [P, Q, 512])
        pd = m.ps(tag + "down_ps", [P, 2, 2, 512])
        sem = lambda x: m.sem(tag + x)
        s_h = [sem(f"h2_loaded_{q}") for q in range(2)]
        s_hh, s_hl = sem("h2_hi_split"), sem("h2_lo_split")
        s_ur = [sem(f"w_up_loaded_{q}") for q in range(2)]
        s_dr = [sem(f"w_down_loaded_{q}") for q in range(2)]
        s_uwh, s_uwl, s_dwh, s_dwl = (sem(x) for x in ("w_up_hi_split", "w_up_lo_split", "w_down_hi_split", "w_down_lo_split"))
        s_up, s_re, s_u, s_uh, s_ul = (sem(x) for x in ("up_summed", "relu_done", "squared", "u_hi_split", "u_lo_split"))
        s_dn, s_y, s_y0 = sem("down_summed"), sem("y_added"), sem("y_cleared")
        s_gt, s_gr = sem("gates_spread"), sem("gates_read")
        s_ss, s_ms, s_rr, s_yg, s_yo = (sem(x) for x in ("y_sumsq_done", "y_meansq_done", "y_rrms_done", "y_gated", "y_out"))
        s_x = [sem(f"x_mid_loaded_{q}") for q in range(2)]
        s_st = sem("y_stored")

        def skeleton(eng, up, down, split_down):
            up(0, 0, 0)
            with eng.Fori(0, NG // 2 - 1) as i:
                split_down(i * 2)
                up(i * 2 + 1, 1, i)
                down(i * 2, 0, i)
                split_down(i * 2 + 1)
                up(i * 2 + 2, 0, i + 1)
                down(i * 2 + 1, 1, i)
            split_down(NG - 2)
            up(NG - 1, 1, NG // 2 - 1)
            down(NG - 2, 0, NG // 2 - 1)
            split_down(NG - 1)
            down(NG - 1, 1, NG // 2 - 1)

        nothing = lambda *_: None
        def place(t):
            if half == 0 and t == tiles - 1:
                return slice(P - TS, P), slice(T, T + TS)
            return slice(0, P), slice((half * 8 + t) * P, (half * 8 + t + 1) * P)

        with nc.Block() as block:
            @block.sync
            def _(sp):
                def finish(sp, t):
                    r, rows = place(t)
                    sp.wait_ge(s_yo, t + 1)
                    dst = io["ys"] if rows.start == T else io["y"][rows, :]
                    sp.dma_start(dst, y[r, t]).then_inc(s_st, 16)

                def h_slice(kk):
                    q = kk % 2
                    if kk >= 2:
                        sp.wait_ge(s_hl, kk - 1)
                    sp.dma_start(ru[:, q, 0:NT // 2 * P].rearrange("p (t n) -> p t n", n=P),
                                 io["h2T"][half * NT // 2:(half + 1) * NT // 2, :, kk, :].rearrange("t p n -> p t n")).then_inc(s_h[q], 16)
                    if half == 0:
                        sp.dma_start(ru[:, q, NT // 2 * P:n], io["h2T"][NT, :, kk, 0:TS]).then_inc(s_h[q], 16)
                for kk in range(KD):
                    h_slice(kk)

                def load_up(f, c):
                    sp.wait_ge(s_uwl, f + 1)
                    sp.dma_start(ur[:, c], io["w_up"][:, bass.ds(f * P, P)].rearrange("(k p) n -> p k n", p=P)).then_inc(s_ur[c], 16)

                def load_down(G):
                    for c in range(2):
                        sp.wait_ge(s_dwl, G * 2 + c + 1)
                        sp.dma_start(dr[:, c], io["w_down"][bass.ds((G * 2 + c) * P, P), :]).then_inc(s_dr[c], 16)
                with sp.Fori(0, NG) as G:
                    for c in range(2):
                        load_up(G * 2 + c, c)
                    load_down(G)
                for c in range(2):
                    sp.wait_ge(s_uwl, 2 * NG + c + 1)
                    sp.dma_start(ur[:, c], io["w_up"][:, c * P:(c + 1) * P].rearrange("(k p) n -> p k n", p=P)).then_inc(s_ur[c], 16)
                for t in range(tiles):
                    r, rows = place(t)
                    sp.wait_ge(s_dwl, 2 * NG + 2)
                    if t >= 2:
                        sp.wait_ge(s_yo, t - 1)
                    sp.dma_start(dr[r, t % 2], io["x1"][rows, :]).then_inc(s_x[t % 2], 16)
                    if t >= 1:
                        finish(sp, t - 1)
                finish(sp, tiles - 1)
                sp.wait_ge(s_st, 16 * tiles)

            @block.tensor
            def _(pe):
                pe.sem_inc(s_dn, tiles + 1)
                spread_gate(nc, pe, k, 1, P, 0, False, pd[:, 0]).then_inc(s_gt, 1)
                if half == 0:
                    spread_gate(nc, pe, k, 1, TS, P - TS, True, pd[:, 1]).then_inc(s_gt, 1)
                pe.wait_ge(s_hl, KD)
                pe.wait_ge(s_hh, KD)

                def up(G, par, i):
                    for c in range(2):
                        f = G * 2 + c
                        pe.wait_ge(s_uwh, f + 1)
                        pe.wait_ge(s_uwl, f + 3)
                        for j in range(Q):
                            pe.wait_ge(s_re, f * Q + j + 1)
                            at = slice(j * qn, (j + 1) * qn)
                            for kk in range(KD):
                                last = three_pass(nc, pu[:, j, 0:qn], uwh[:, c, kk, :], uwl[:, c, kk, :],
                                                  hhi[:, kk, at], hlo[:, kk, at], kk == 0, kk == KD - 1)
                            last.then_inc(s_up, 1)

                def down(G, par, i):
                    pe.wait_ge(s_gr, 2 if half == 0 else 1)
                    pe.wait_ge(s_dwh, G * 2 + 2)
                    pe.wait_ge(s_dwl, G * 2 + 4)
                    pe.wait_ge(s_uh, G * 2 + 2)
                    pe.wait_ge(s_ul, G * 2 + 4)
                    for t in range(tiles):
                        b = (par * tiles + t) % 2
                        at = slice(t * P, (t + 1) * P) if t < NT // 2 else slice(last0, n)
                        pe.wait_ge(s_y, G * tiles + t + 1)
                        for c in range(2):
                            for h in range(2):
                                ha = slice(h * 512, (h + 1) * 512)
                                last = three_pass(nc, pd[:, b, h, :], uhi[:, par, c, at], ulo[:, par, c, at],
                                                  dwh[:, c, ha], dwl[:, c, ha], c == 0, c == 1)
                        last.then_inc(s_dn, 1)
                skeleton(pe, up, down, nothing)

            @block.scalar
            def _(act):
                a = nc.scalar
                act.sem_inc(s_re, Q)
                for kk in range(KD):
                    q = kk % 2
                    act.wait_ge(s_h[q], (kk // 2 + 1) * (32 if half == 0 else 16))
                    a.copy(hhi[:, kk], ru[:, q]).then_inc(s_hh, 1)
                    if kk == 0:
                        act.wait_ge(s_gt, 1)
                        a.copy(gate[:], pd[:, 0]).then_inc(s_gr, 1)
                        if half == 0:
                            act.wait_ge(s_gt, 2)
                            a.copy(gate_s[P - TS:P], pd[P - TS:P, 1]).then_inc(s_gr, 1)

                def split_up(f, c, count):
                    act.wait_ge(s_ur[c], count * 16)
                    a.copy(uwh[:, c], ur[:, c]).then_inc(s_uwh, 1)
                split_up(0, 0, 1)
                split_up(1, 1, 1)

                def up(G, par, i):
                    for c in range(2):
                        f = G * 2 + c
                        act.wait_ge(s_ul, f + 1)
                        for j in range(Q):
                            at = slice(j * qn, (j + 1) * qn)
                            act.wait_ge(s_up, f * Q + j + 1)
                            a.activation(ru[:, c, at], pu[:, j, 0:qn], ACT.Relu).then_inc(s_re, 1)
                        split_up(f + 2, c, G + 2)
                        act.wait_ge(s_u, f + 1)
                        act.wait_ge(s_dn, G * tiles + 1)
                        a.copy(uhi[:, par, c], ru[:, c]).then_inc(s_uh, 1)

                def split_down(G):
                    for c in range(2):
                        act.wait_ge(s_dr[c], G * 16 + 16)
                        act.wait_ge(s_dn, G * tiles + tiles + 1)
                        a.copy(dwh[:, c], dr[:, c]).then_inc(s_dwh, 1)
                skeleton(act, up, nothing, split_down)
                act.wait_ge(s_y, NG * tiles + 2)
                for t in range(tiles):
                    r, _ = place(t)
                    act.wait_ge(s_ss, t + 1)
                    a.activation(ru[r, 0, 0:D], y[r, t], ACT.Square, accum_out=ss[r, t:t + 1]).then_inc(s_ss, 1)

            @block.gpsimd
            def _(pool):
                g = nc.gpsimd
                g.memset(y[:], 0.0).then_inc(s_y0, 1)
                g.memset(ss[:], 1.0).then_inc(s_ss, 1)
                pool.wait_ge(s_ms, 1)
                g.tensor_tensor(rr[:], ms[:], k["nhalf"][:, 0:tiles], ALU.pow).then_inc(s_rr, 1)

            @block.vector
            def _(dve):
                v = nc.vector
                for s in (s_uwl, s_dwl, s_ul, s_y):
                    dve.sem_inc(s, 2)
                for kk in range(KD):
                    dve.wait_ge(s_hh, kk + 1)
                    v.tensor_tensor(hlo[:, kk], ru[:, kk % 2], hhi[:, kk].bitcast(F32), ALU.subtract).then_inc(s_hl, 1)

                def split_up(f, c):
                    dve.wait_ge(s_uwh, f + 1)
                    v.tensor_tensor(uwl[:, c], ur[:, c], uwh[:, c].bitcast(F32), ALU.subtract).then_inc(s_uwl, 1)
                split_up(0, 0)
                split_up(1, 1)
                dve.wait_ge(s_y0, 1)

                def up(G, par, i):
                    for c in range(2):
                        f = G * 2 + c
                        dve.wait_ge(s_re, f * Q + 2 * Q)
                        v.tensor_tensor(ru[:, c], ru[:, c], ru[:, c], ALU.mult).then_inc(s_u, 1)
                        split_up(f + 2, c)
                        dve.wait_ge(s_uh, f + 1)
                        v.tensor_tensor(ulo[:, par, c], ru[:, c], uhi[:, par, c].bitcast(F32), ALU.subtract).then_inc(s_ul, 1)

                def down(G, par, i):
                    for t in range(tiles):
                        r, _ = place(t)
                        b = (par * tiles + t) % 2
                        dve.wait_ge(s_dn, G * tiles + t + tiles + 2)
                        acc = y[r, t].rearrange("p (b c) -> p b c", b=2)
                        v.tensor_tensor(acc, acc, pd[r, b], ALU.add).then_inc(s_y, 1)

                def split_down(G):
                    for c in range(2):
                        dve.wait_ge(s_dwh, G * 2 + c + 1)
                        v.tensor_tensor(dwl[:, c], dr[:, c], dwh[:, c].bitcast(F32), ALU.subtract).then_inc(s_dwl, 1)
                skeleton(dve, up, down, split_down)
                dve.wait_ge(s_ss, tiles + 1)
                v.tensor_scalar(ms[:], ss[:], 1.0 / D, EPS, ALU.mult, ALU.add).then_inc(s_ms, 1)
                dve.wait_ge(s_rr, 1)
                for t in range(tiles):
                    r, _ = place(t)
                    yt = y[r, t].rearrange("p (b c) -> p b c", b=2)
                    gr = gate_s if half == 0 and t == tiles - 1 else gate
                    v.scalar_tensor_tensor(yt, yt, rr[r, t:t + 1], gr[r], ALU.mult, ALU.mult).then_inc(s_yg, 1)
                    dve.wait_ge(s_yg, t + 1)
                    dve.wait_ge(s_x[t % 2], 16 * (t // 2 + 1))
                    v.tensor_tensor(y[r, t], y[r, t], dr[r, t % 2], ALU.add).then_inc(s_yo, 1)
        m.clear_sems()


def decoder_layer(nc, io):
    io["projT"] = nc.dram_tensor("proj_scratch", (NCH, P, PAD + T), F32, kind="Internal").ap()
    io["oT"] = nc.dram_tensor("mixed_scratch", (KD, P, T), F32, kind="Internal").ap()
    io["x1"] = nc.dram_tensor("x_mid_scratch", (T + TS, D), F32, kind="Internal").ap()
    io["h2T"] = nc.dram_tensor("h2_scratch", (NT + 1, P, KD, P), F32, kind="Internal").ap()
    with ExitStack() as whole, ExitStack() as ctx:
        k = {}
        k["chunk_stored"] = [Mem(nc, whole).sem(f"chunk_stored_{q}") for q in range(2)]
        k["states_stored"] = Mem(nc, whole).sem("states_stored")
        for name, shape in (("ident", [P, P]), ("nhalf", [P, 16]), ("mscale", [P, 2, KD, 9]), ("mshift", [P, 2, KD, 9]),
                            ("pscale", [P, 2, KD]), ("pshift", [P, 2, KD]), ("gate_col", [P, 2, KD]),
                            ("gate_col_s", [P, 2, KD, NB, NS]), ("oS", [P, KD, TS])):
            k[name] = Mem(nc, whole).sb(name, shape)
        m = Mem(nc, ctx)
        for name, shape in (("vcol", [P, NV]), ("alog", [P, HA]), ("dtb", [P, HA]), ("sink", [P, HB]), ("sink_s", [16, 2]),
                            ("zeros", [P, 1, P]), ("ones", [P, P]), ("ut", [P, P]), ("neg", [P, P]),
                            ("band", [P, 2 * W]), ("band_now", [P, 2 * W]), ("lev", [P, 7, P]), ("state", [P, HA, P]),
                            ("same", [TS, TS]), ("seg", [TS, NB]), ("uts", [TS, TS]), ("negs", [TS, TS]),
                            ("masks", [16, W + NS]), ("taps", [P, CW * CC]),
                            ("xs_pad", [P, CC, NB, CW - 1 + NS]), ("scT", [P, KD, 9]), 
                            ("projS", [P, NCH, TS]), ("xlast", [P, 3, CC]), ("xrow", [CC * 3, P]),
                            ("ba", [P, NT, 2 * HA]), ("ba_s", [TS, 2 * HA])):
            k[name] = m.sb(name, shape)
        with ExitStack() as front:
            k["xnT"] = Mem(nc, front).sb("xnT", [P, KD, LEAD + T + TS])
            constants(nc, io, k)
            modulation(nc, io, k)
            projection(nc, io, k)
        mixer(nc, io, k)
        sample_mixer(nc, io, k)
        ctx.close()
        out_projection(nc, io, k)
        mlp(nc, io, k, 0)
        mlp(nc, io, k, 1)
        if "dbg" in io:
            io["dbg"](nc, io, k)


_INS = ["x_prompt", "x_sample", "state_conv", "state_ssm", "cache_swa_k", "cache_swa_v", "c_prompt", "c_sample",
        "g_pre_mix", "g_post_mix", "g_pre_ffn", "g_post_ffn", "w_ada", "b_ada", "w_in", "conv_w", "a_log", "dt_bias",
        "gdn_norm_w", "sinks", "w_o", "w_up", "w_down"]
_OUTS = [("y_prompt", (1, T, D)), ("y_sample", (NB, NS, D)), ("conv_prompt", (1, 1, 3, CC * P)),
         ("ssm_prompt", (1, 1, HA, P, P)), ("swa_k_prompt", (1, 1, W, 2, DB)), ("swa_v_prompt", (1, 1, W, 2, DB)),
         ("conv_sample", (1, NB, 3, CC * P)), ("ssm_sample", (1, NB, HA, P, P)), ("swa_k_sample", (1, NB, W, 2, DB)),
         ("swa_v_sample", (1, NB, W, 2, DB))]


def kernel(**inputs):
    import numpy as _np
    import concourse.bacc as _bacc
    from concourse import mybir as _mybir
    from concourse.bass_utils import run_bass_kernel_spmd as _run

    nc = _bacc.Bacc("TRN2", target_bir_lowering=False, num_devices=1)
    arrays, io = {}, {}
    for name in _INS:
        a = _np.ascontiguousarray(inputs[name])
        arrays["in_" + name] = a
        io[name] = nc.dram_tensor("in_" + name, a.shape, _mybir.dt.from_np(a.dtype), kind="ExternalInput").ap()
    for name, shape in _OUTS:
        io[name] = nc.dram_tensor("out_" + name, shape, _mybir.dt.float32, kind="ExternalOutput").ap()
    io["x"] = io["x_prompt"].rearrange("a t d -> (a t) d")
    io["y"] = io["y_prompt"].rearrange("a t d -> (a t) d") if "y_prompt" in io else None
    io["ys"] = io["y_sample"].rearrange("b s d -> (b s) d") if "y_sample" in io else None
    io["xs"] = io["x_sample"].rearrange("b s d -> (b s) d")
    for name in ("w_ada", "w_in", "w_o", "w_up", "w_down"):
        io[name] = io[name].rearrange("a k n -> (a k) n")
    decoder_layer(nc, io)
    r = _run(nc, [arrays], core_ids=[0])
    return tuple(r.results[0]["out_" + name] for name, _ in _OUTS)
```

```python
from contextlib import ExitStack

import concourse.bass as bass
import numpy as np
from concourse import mybir

F32 = mybir.dt.float32
FR = mybir.dt.float32r
ALU = mybir.AluOpType
ACT = mybir.ActivationFunctionType
AX = mybir.AxisListType

P = 128
D = 1024
KD = D // P
T = 2048
NT = T // P
NB = 8
NS = 4
TS = NB * NS
HA = 4
CC = 12
CW = 4
NCH = 22
HB = 8
DB = 64
W = 128
FF = 4 * D
EPS = 1e-6
NEG = -1e30
BLK = 512
NBLK = T // BLK
SB = TS // NBLK
LEAD = 4
BT = LEAD + BLK + SB
PAD = W
V_BADA, V_GPM, V_GQM, V_GPF, V_GQF, V_GDN = 0, 48, 56, 64, 72, 80
NV = 81


class Mem:

    def __init__(self, nc, ctx):
        self.nc, self.ctx, self.sems = nc, ctx, []

    def sb(self, name, shape, dt=F32):
        return self.ctx.enter_context(self.nc.sbuf_tensor(name, shape, dt))

    def ps(self, name, shape):
        return self.ctx.enter_context(self.nc.psum_tensor(name, shape, F32))

    def sem(self, name):
        self.sems.append(self.nc.alloc_semaphore(name=name))
        return self.sems[-1]

    def clear_sems(self):
        self.nc.clear_and_free_semaphores(self.sems)
        self.nc.all_engine_barrier()


def three_pass(nc, out, whi, wlo, mhi, mlo, first, last):
    nc.tensor.matmul(out, whi, mhi, start=first, stop=False)
    nc.tensor.matmul(out, whi, mlo, start=False, stop=False)
    return nc.tensor.matmul(out, wlo, mhi, start=False, stop=last)


def constants(nc, io, k):
    with ExitStack() as ctx:
        m = Mem(nc, ctx)
        vec = m.sb("vec_rows", [NV, P])
        cwr = m.sb("conv_rows", [CW * CC, P])
        cin = m.sb("c_rows", [1 + NB, D])
        cth = m.sb("c_tanh", [1 + NB, D])
        csl = m.sb("c_silu", [1 + NB, D])
        scr = m.sb("cache_rows", [NB * (CW - 1), CC * P])
        pc = m.ps("const_ps", [P, 4, 512])
        s_vec, s_c = m.sem("vectors_loaded"), m.sem("c_loaded")
        s_set, s_sel, s_th, s_si = m.sem("masks_set"), m.sem("masks_cut"), m.sem("c_tanh_done"), m.sem("c_silu_done")
        s_tr, s_der, s_nap = m.sem("columns_turned"), m.sem("derived"), m.sem("tap_halved")
        with nc.Block() as block:
            @block.sync
            def _(sp):
                rows = lambda v, n: v.rearrange("a (c p) -> (a c) p", p=P)
                for src, at, n in ((io["b_ada"], V_BADA, 48), (io["g_pre_mix"], V_GPM, 8), (io["g_post_mix"], V_GQM, 8),
                                   (io["g_pre_ffn"], V_GPF, 8), (io["g_post_ffn"], V_GQF, 8), (io["gdn_norm_w"], V_GDN, 1)):
                    sp.dma_start(vec[at:at + n, :], rows(src, n)).then_inc(s_vec, 16)
                sp.dma_start(cwr[:], io["conv_w"].rearrange("a i (c p) -> (a i c) p", p=P)).then_inc(s_vec, 16)
                sp.dma_start(scr[:], io["state_conv"].rearrange("a b i c -> (a b i) c")).then_inc(s_vec, 16)
                sp.dma_start(cin[0:1, :], io["c_prompt"]).then_inc(s_c, 16)
                sp.dma_start(cin[1:1 + NB, :], io["c_sample"]).then_inc(s_c, 16)
                for src, dst in ((io["a_log"], k["alog"]), (io["dt_bias"], k["dtb"]), (io["sinks"], k["sink"])):
                    sp.dma_start(dst[:], src.partition_broadcast(P).rearrange("p a h -> p (a h)")).then_inc(s_vec, 16)
                for s in range(NS):
                    sp.dma_start(k["sink_s"][s * 4:s * 4 + 4, :], io["sinks"].rearrange("a (g c) -> (a c) g", g=2), allow_slow_non_contiguous=True
                                 ).then_inc(s_vec, 16)
                sp.wait_ge(s_vec, 16 * (8 + 3 + NS))

            @block.gpsimd
            def _(pool):
                g = nc.gpsimd
                g.memset(k["zeros"][:], 0.0).then_inc(s_set, 1)
                g.memset(k["ones"][:], 1.0).then_inc(s_set, 1)
                g.memset(k["ident"][:], 0.0).then_inc(s_set, 1)
                g.memset(k["ut"][:], 1.0).then_inc(s_set, 1)
                g.memset(k["neg"][:], 0.0).then_inc(s_set, 1)
                g.memset(k["band"][:], 0.0).then_inc(s_set, 1)
                g.memset(k["band_now"][:, 0:W], NEG).then_inc(s_set, 1)
                g.memset(k["band_now"][:, W:2 * W], 0.0).then_inc(s_set, 1)
                g.memset(k["lev"][:], 0.0).then_inc(s_set, 1)
                g.memset(k["state"][:], 0.0).then_inc(s_set, 1)
                g.memset(k["xnT"][:, :, 0:LEAD], 0.0).then_inc(s_set, 1)
                g.memset(k["same"][:], 1.0).then_inc(s_set, 1)
                g.memset(k["seg"][:], 1.0).then_inc(s_set, 1)
                g.memset(k["uts"][:], 1.0).then_inc(s_set, 1)
                g.memset(k["negs"][:], 0.0).then_inc(s_set, 1)
                g.memset(k["masks"][:], 0.0).then_inc(s_set, 1)
                g.memset(k["nhalf"][:], -0.5).then_inc(s_set, 1)
                n = 17
                pool.wait_ge(s_set, n)
                for lv in range(7):
                    b = 1 << lv
                    g.memset(k["lev"][:, lv, :].rearrange("p (m r) -> p m r", r=2 * b)[:, :, b:2 * b], 1.0).then_inc(s_set, 1)
                    n += 1
                pool.wait_ge(s_set, n)
                cut = 0

                def sel(ap, op, fill, base, pattern, mul, after=True):
                    nonlocal cut
                    if after:
                        pool.wait_ge(s_sel, cut)
                    g.affine_select(out=ap, in_=ap, pattern=pattern, compare_op=op, fill=fill, base=base,
                                    channel_multiplier=mul).then_inc(s_sel, 1)
                    cut += 1

                sel(k["ident"][:], ALU.not_equal, 1.0, 0, [[-1, P]], 1, False)
                sel(k["ut"][:], ALU.is_ge, 0.0, 0, [[1, P]], -1)
                sel(k["neg"][:], ALU.is_ge, NEG, 0, [[1, P]], -1)
                sel(k["band"][:], ALU.is_gt, NEG, 0, [[1, 2 * W]], -1)
                sel(k["band"][:], ALU.is_ge, NEG, W, [[-1, 2 * W]], 1)
                sel(k["band_now"][:, W:2 * W], ALU.is_ge, NEG, 0, [[-1, W]], 1)
                for lv in range(7):
                    b = 1 << lv
                    v = k["lev"][:, lv, :].rearrange("p (m r) -> p m r", r=2 * b)
                    sel(v, ALU.is_ge, 0.0, 0, [[-2 * b, P // (2 * b)], [0, 2 * b]], 1)
                    sel(v, ALU.is_ge, 0.0, b - 1, [[2 * b, P // (2 * b)], [0, 2 * b]], -1)
                sv = k["same"][:].rearrange("p (m r) -> p m r", r=NS)
                sel(sv, ALU.is_ge, 0.0, 0, [[-NS, NB], [0, NS]], 1)
                sel(sv, ALU.is_ge, 0.0, NS - 1, [[NS, NB], [0, NS]], -1)
                sel(k["seg"][:], ALU.is_ge, 0.0, 0, [[-NS, NB]], 1)
                sel(k["seg"][:], ALU.is_ge, 0.0, NS - 1, [[NS, NB]], -1)
                uv = k["uts"][:].rearrange("p (m r) -> p m r", r=NS)
                sel(k["uts"][:], ALU.is_ge, 0.0, 0, [[1, TS]], -1)
                sel(uv, ALU.is_ge, 0.0, 0, [[-NS, NB], [0, NS]], 1)
                sel(uv, ALU.is_ge, 0.0, NS - 1, [[NS, NB], [0, NS]], -1)
                nv = k["negs"][:].rearrange("p (m r) -> p m r", r=NS)
                sel(k["negs"][:], ALU.is_ge, NEG, 0, [[1, TS]], -1)
                sel(nv, ALU.is_ge, NEG, 0, [[-NS, NB], [0, NS]], 1)
                sel(nv, ALU.is_ge, NEG, NS - 1, [[NS, NB], [0, NS]], -1)
                sel(k["masks"][:], ALU.is_gt, NEG, 0, [[NS, W + NS]], -1)
                sel(k["masks"][:], ALU.is_ge, NEG, NS * W, [[-NS, W + NS]], 1)

            @block.scalar
            def _(act):
                act.wait_ge(s_c, 32)
                nc.scalar.activation(cth[:], cin[:], ACT.Tanh, scale=0.5).then_inc(s_th, 1)

            @block.vector
            def _(dve):
                v = nc.vector
                dve.wait_ge(s_th, 1)
                v.scalar_tensor_tensor(csl[:], cth[:], 1.0, cin[:], ALU.add, ALU.mult).then_inc(s_si, 1)
                dve.wait_ge(s_tr, 1)
                v.tensor_copy(k["vcol"][:], pc[:, 0, 0:NV]).then_inc(s_der, 1)
                v.tensor_scalar(k["taps"][:], pc[:, 1, 0:CW * CC], 0.5, None, ALU.mult).then_inc(s_der, 1)
                v.tensor_copy(k["xs_pad"][:, :, :, 0:CW - 1],
                              pc[:, 2, 0:CC * 24].rearrange("p (c b i) -> p c b i", c=CC, b=NB)).then_inc(s_der, 1)
                dve.wait_ge(s_tr, 2)
                v.tensor_scalar(k["scT"][:], pc[:, 3, 0:KD * 9].rearrange("p (k n) -> p k n", n=9), 0.5, None,
                                ALU.mult).then_inc(s_der, 1)

            @block.tensor
            def _(pe):
                pe.wait_ge(s_vec, 16 * (8 + 3 + NS))
                pe.wait_ge(s_sel, 1)
                nc.tensor.transpose(pc[:, 0, 0:NV], vec[:], k["ident"][0:NV, 0:NV])
                nc.tensor.transpose(pc[:, 1, 0:CW * CC], cwr[:], k["ident"][0:CW * CC, 0:CW * CC])
                for c in range(CC):
                    last = nc.tensor.transpose(pc[:, 2, c * 24:c * 24 + 24], scr[:, c * P:(c + 1) * P], k["ident"][0:24, 0:24])
                last.then_inc(s_tr, 1)
                pe.wait_ge(s_si, 1)
                for c in range(KD):
                    last = nc.tensor.transpose(pc[:, 3, c * 9:c * 9 + 9], csl[:, c * P:(c + 1) * P], k["ident"][0:9, 0:9])
                last.then_inc(s_tr, 1)
        m.clear_sems()


def modulation(nc, io, k):
    GC = 3
    with ExitStack() as ctx:
        m = Mem(nc, ctx)
        xt = m.sb("x_tile", [P, 2, D])
        xn = m.sb("x_normed", [P, 2, D])
        sq = m.sb("x_squares", [P, D])
        ss = m.sb("x_sumsq", [P, 2])
        ms = m.sb("x_meansq", [P, 2])
        rr = m.sb("x_rrms", [P, 2])
        wa = m.sb("w_ada_cols", [P, 2, KD, GC * P])
        modT = m.sb("modT", [P, 6 * KD, 9])
        gcol, gcs = k["gate_col"], k["gate_col_s"]
        one = m.sb("one_plus", [P, 2, KD, 9])
        pt = m.ps("xT_ps", [P, 2, 2, 512])
        pm = m.ps("mod_ps", [P, 2, 512])
        pb = m.ps("mod_turned_ps", [P, 2, 512])
        mrow = m.sb("mod_rows", [9, 2, GC * P])
        s_x = [m.sem(f"x_loaded_{p}") for p in range(2)]
        s_wa = [m.sem(f"w_ada_loaded_{p}") for p in range(2)]
        s_ss, s_ms, s_rr, s_xn = m.sem("x_sumsq_done"), m.sem("x_meansq_done"), m.sem("x_rrms_done"), m.sem("x_normed_done")
        s_xT, s_ev = m.sem("x_turned"), m.sem("xnT_written")
        s_mod, s_me = m.sem("mod_summed"), m.sem("mod_written")
        s_mr, s_mt, s_free = m.sem("mod_rows_read"), m.sem("mod_turned"), m.sem("mod_columns_read")
        s_d, s_c = m.sem("mod_derived"), m.sem("mod_chain")
        N = NT + 1
        with nc.Block() as block:
            @block.sync
            def _(sp):
                with sp.Fori(0, NT // 2) as i:
                    for p in range(2):
                        t = i * 2 + p
                        sp.wait_ge(s_mr, t + 1)
                        sp.dma_start(wa[:, p], io["w_ada"][:, bass.ds(t * (GC * P), GC * P)]
                                     .rearrange("(k p) n -> p k n", p=P)).then_inc(s_wa[p], 16)
                        sp.wait_ge(s_xn, t + 1)
                        sp.dma_start(xt[:, p], io["x"][bass.ds(t * P, P), :]).then_inc(s_x[p], 16)
                sp.wait_ge(s_xn, NT + 1)
                sp.dma_start(xt[0:TS, 0], io["xs"]).then_inc(s_x[0], 16)

            @block.scalar
            def _(act):
                a = nc.scalar

                def square(i, t, p, n):
                    act.wait_ge(s_x[p], i * 16 + 16)
                    a.activation(sq[0:n], xt[0:n, p], ACT.Square, accum_out=ss[0:n, p:p + 1]).then_inc(s_ss, 1)

                def evac(t, p, n, dst):
                    act.wait_ge(s_xT, t + 1)
                    src = pt[:, p].rearrange("p a (b t) -> p (a b) t", t=P)[:, :, 0:n]
                    a.copy(dst, src).then_inc(s_ev, 1)

                with act.Fori(0, NT // 2) as i:
                    for p in range(2):
                        t = i * 2 + p
                        square(i, t, p, P)
                        evac(t, p, P, k["xnT"][:, :, bass.ds(t * P + LEAD, P)])
                square(NT // 2, NT, 0, TS)
                evac(NT, 0, TS, k["xnT"][:, :, LEAD + T:LEAD + T + TS])

            @block.gpsimd
            def _(pool):
                g = nc.gpsimd

                def rrms(t, p, n):
                    pool.wait_ge(s_ms, t + 1)
                    g.tensor_tensor(rr[0:n, p:p + 1], ms[0:n, p:p + 1], k["nhalf"][0:n, 0:1], ALU.pow).then_inc(s_rr, 1)

                with pool.Fori(0, NT // 2) as i:
                    for p in range(2):
                        rrms(i * 2 + p, p, P)
                rrms(NT, 0, TS)

            @block.vector
            def _(dve):
                v = nc.vector

                def norm(i, t, p, n):
                    dve.wait_ge(s_ss, t + 1)
                    v.tensor_scalar(ms[0:n, p:p + 1], ss[0:n, p:p + 1], 1.0 / D, EPS, ALU.mult, ALU.add).then_inc(s_ms, 1)
                    dve.wait_ge(s_rr, t + 1)
                    dve.wait_ge(s_x[p], i * 16 + 16)
                    v.tensor_scalar(xn[0:n, p], xt[0:n, p], rr[0:n, p:p + 1], None, ALU.mult).then_inc(s_xn, 1)

                for x in (s_xn, s_mr, s_free):
                    dve.sem_inc(x, 2)
                with dve.Fori(0, NT // 2) as i:
                    for p in range(2):
                        t = i * 2 + p
                        norm(i, t, p, P)
                        dve.wait_ge(s_mod, t + 1)
                        v.tensor_copy(mrow[:, p], pm[0:9, p, 0:GC * P]).then_inc(s_mr, 1)
                        dve.wait_ge(s_mt, t + 1)
                        v.tensor_copy(modT[:, bass.ds(t * GC, GC), :],
                                      pb[:, p, 0:GC * 9].rearrange("p (c n) -> p c n", n=9)).then_inc(s_free, 1)
                norm(NT // 2, NT, 0, TS)
                dve.wait_ge(s_free, NT + 2)
                v.tensor_tensor(modT[:], modT[:], k["vcol"][:, V_BADA:V_BADA + 48].unsqueeze(2).broadcast_to([P, 48, 9]),
                                ALU.add).then_inc(s_c, 1)
                dve.wait_ge(s_c, 1)
                mo = modT[:].rearrange("p (m k) n -> p m k n", m=6)
                for f, (gate, post) in enumerate(((2, V_GQM), (5, V_GQF))):
                    v.tensor_tensor(gcol[:, f], mo[:, gate, :, 0], k["vcol"][:, post:post + KD], ALU.mult).then_inc(s_d, 1)
                    v.tensor_tensor(gcs[:, f], mo[:, gate, :, 1:9].unsqueeze(3).broadcast_to([P, KD, NB, NS]),
                                    k["vcol"][:, post:post + KD].unsqueeze(2).unsqueeze(3).broadcast_to([P, KD, NB, NS]),
                                    ALU.mult).then_inc(s_d, 1)
                for f, (shift, scale, pre) in enumerate(((0, 1, V_GPM), (3, 4, V_GPF))):
                    v.tensor_scalar(one[:, f], mo[:, scale], 1.0, None, ALU.add).then_inc(s_c, 1)
                    dve.wait_ge(s_c, 2 + f)
                    v.tensor_tensor(k["mscale"][:, f], one[:, f], k["vcol"][:, pre:pre + KD].unsqueeze(2)
                                    .broadcast_to([P, KD, 9]), ALU.mult).then_inc(s_d, 1)
                    v.tensor_copy(k["mshift"][:, f], mo[:, shift]).then_inc(s_d, 1)
                    v.tensor_tensor(k["pscale"][:, f], one[:, f, :, 0], k["vcol"][:, pre:pre + KD], ALU.mult).then_inc(s_d, 1)
                    v.tensor_copy(k["pshift"][:, f], mo[:, shift, :, 0]).then_inc(s_d, 1)

            @block.tensor
            def _(pe):
                def turn(t, p, n):
                    pe.wait_ge(s_xn, t + 3)
                    pe.wait_ge(s_ev, t + 1)
                    for c in range(KD):
                        if c == KD // 2 and n == P:
                            pe.wait_ge(s_free, t + 1)
                            pe.wait_ge(s_mr, t + 3)
                        last = nc.tensor.transpose(pt[:, p, c // 4, (c % 4) * P:(c % 4) * P + n],
                                                   xn[0:n, p, c * P:(c + 1) * P], k["ident"][0:n, 0:n])
                    last.then_inc(s_xT, 1)

                pe.sem_inc(s_ev, 2)
                with pe.Fori(0, NT // 2) as i:
                    for p in range(2):
                        t = i * 2 + p
                        pe.wait_ge(s_wa[p], i * 16 + 16)
                        pe.wait_ge(s_mr, t + 1)
                        for kk in range(KD):
                            last = nc.tensor.matmul(pm[0:9, p, 0:GC * P], k["scT"][:, kk, :], wa[:, p, kk, :],
                                                    start=(kk == 0), stop=(kk == KD - 1))
                        last.then_inc(s_mod, 1)
                        turn(t, p, P)
                        for c in range(GC):
                            last = nc.tensor.transpose(pb[:, p, c * 9:c * 9 + 9], mrow[:, p, c * P:(c + 1) * P], k["ident"][0:9, 0:9])
                        last.then_inc(s_mt, 1)
                turn(NT, 0, TS)
        m.clear_sems()


def projection(nc, io, k):
    with ExitStack() as ctx:
        m = Mem(nc, ctx)
        raw = m.sb("w_in_raw", [P, 2, KD, P])
        whi = m.sb("w_in_hi", [P, 2, KD, P], FR)
        wlo = m.sb("w_in_lo", [P, 2, KD, P], FR)
        hf = m.sb("h_slice", [P, 2, LEAD + BLK])
        hhi = m.sb("h_hi", [P, 2, KD, BT], FR)
        hlo = m.sb("h_lo", [P, 2, KD, BT], FR)
        hsf = m.sb("hs_full", [P, KD, TS])
        hshi = m.sb("hs_hi", [P, KD, TS], FR)
        hslo = m.sb("hs_lo", [P, KD, TS], FR)
        wbh = m.sb("w_ba_hi", [P, KD, P], FR)
        wbl = m.sb("w_ba_lo", [P, KD, P], FR)
        wba = raw[:, 0]
        bar = m.sb("ba_rows", [2 * HA, BT])
        xb = m.sb("chunk_read", [P, 2, BT])
        yb = m.sb("chunk_convolved", [P, 2, BLK])
        so = m.sb("chunk_out", [P, 2, BLK])
        pp = m.ps("proj_ps", [P, 2, 2, 512])
        pb = m.ps("ba_ps", [P, 2, 512])
        s_raw = [m.sem(f"w_in_loaded_{q}") for q in range(2)]
        s_hi, s_lo = m.sem("w_in_hi_split"), m.sem("w_in_lo_split")
        s_h, s_hh, s_hl = m.sem("h_modulated"), m.sem("h_hi_split"), m.sem("h_lo_split")
        s_mm, s_ev = m.sem("chunk_summed"), m.sem("chunk_evacuated")
        s_tap, s_y, s_th, s_so = m.sem("tap_added"), m.sem("chunk_conv_done"), m.sem("chunk_tanh_done"), m.sem("chunk_out_done")
        s_st = k["chunk_stored"]
        s_keep = m.sem("chunk_tails_kept")
        s_wb, s_wbs, s_ba, s_be = m.sem("w_ba_loaded"), m.sem("w_ba_split"), m.sem("ba_turned"), m.sem("ba_read")
        s_bp, s_br = m.sem("ba_rows_summed"), m.sem("ba_rows_read")
        s_hs0, s_hs = m.sem("hs_scaled"), m.sem("hs_full_then_hi_then_lo")
        half = BT // 2
        PARTS = KD + 1
        SEG = (("conv", 0, 6), ("silu", 12, 2), ("plain", 16, 3))

        def pairs(eng, b, body):
            for kind, c0, n in SEG:
                with eng.Fori(0, n) as j:
                    for q in range(2):
                        body(kind, j * 2 + (c0 + q), q, b * NCH + j * 2 + (c0 + q), j + c0 // 2)

        with nc.Block() as block:
            @block.sync
            def _(sp):
                sp.dma_start(wba, io["w_in"][:, 2048:2048 + P].rearrange("(k p) n -> p k n", p=P)).then_inc(s_wb, 16)
                sp.wait_ge(s_ba, 1)
                sp.wait_ge(s_wbs, 2)

                def load(kind, c, q, n, j):
                    sp.wait_ge(s_lo, n + 1)
                    col = c * P + (2 * HA if kind == "plain" else 0)
                    sp.dma_start(raw[:, q], io["w_in"][:, bass.ds(col, P)].rearrange("(k p) n -> p k n", p=P)
                                 ).then_inc(s_raw[q], 16)
                with sp.Fori(0, NBLK) as b:
                    pairs(sp, b, load)
                for q in range(2):
                    sp.wait_ge(s_lo, NBLK * NCH + q + 1)
                    sp.dma_start(raw[:, q], io["w_in"][:, q * P:(q + 1) * P].rearrange("(k p) n -> p k n", p=P)
                                 ).then_inc(s_raw[q], 16)

            @block.tensor
            def _(pe):
                pe.wait_ge(s_hs, 1)
                pe.wait_ge(s_wb, 16)
                for kk in range(KD):
                    last = nc.tensor.matmul(pb[0:TS, 1, 0:8], hsf[:, kk, :], wba[:, kk, 0:2 * HA], start=(kk == 0), stop=(kk == KD - 1))
                last.then_inc(s_ba, 1)
                pe.wait_ge(s_wbs, 2)

                def block_of(b, q2):
                    def chunk(kind, c, q, n, j):
                        pe.wait_ge(s_hh, (b + 1) * PARTS)
                        pe.wait_ge(s_hl, (b + 1) * PARTS)
                        pe.wait_ge(s_hi, n + 1)
                        pe.wait_ge(s_lo, n + 3)
                        pe.wait_ge(s_ev, n + 1)
                        if kind == "plain":
                            pe.wait_ge(s_br, b + 1)
                        for kk in range(KD):
                            for h in range(2):
                                at = slice(h * half, (h + 1) * half)
                                last = three_pass(nc, pp[:, q, h, 0:half], whi[:, q, kk, :], wlo[:, q, kk, :],
                                                  hhi[:, q2, kk, at], hlo[:, q2, kk, at], kk == 0, kk == KD - 1)
                        last.then_inc(s_mm, 1)
                    pe.wait_ge(s_hh, (b + 1) * PARTS)
                    pe.wait_ge(s_hl, (b + 1) * PARTS)
                    pe.wait_ge(s_be, b + 1)
                    for kk in range(KD):
                        for h in range(2):
                            at = slice(h * half, (h + 1) * half)
                            last = three_pass(nc, pb[:, h, 0:half], wbh[:, kk, :], wbl[:, kk, :],
                                              hhi[:, q2, kk, at], hlo[:, q2, kk, at], kk == 0, kk == KD - 1)
                    last.then_inc(s_bp, 1)
                    pairs(pe, b, chunk)
                    for jj in range(BLK // P):
                        last = nc.tensor.transpose(pb[:, 0, jj * 8:jj * 8 + 8], bar[:, LEAD + jj * P:LEAD + (jj + 1) * P],
                                                   k["ident"][0:2 * HA, 0:2 * HA])
                    last.then_inc(s_ba, 1)

                with pe.Fori(0, NBLK // 2) as i:
                    for q2 in range(2):
                        block_of(i * 2 + q2, q2)

            @block.scalar
            def _(act):
                a = nc.scalar
                act.sem_inc(s_ev, 2)
                act.wait_ge(s_hs, 1)
                a.copy(hshi[:], hsf[:]).then_inc(s_hs, 1)
                act.wait_ge(s_wb, 16)
                a.copy(wbh[:], wba).then_inc(s_wbs, 1)

                def split(pair, q):
                    act.wait_ge(s_raw[q], pair * 16 + 16)
                    a.copy(whi[:, q], raw[:, q]).then_inc(s_hi, 1)

                def slice_hi(count, q2, kk, lead, w=0):
                    act.wait_ge(s_h, count + 1)
                    a.copy(hhi[:, q2, kk, lead:LEAD + BLK], hf[:, w, lead:]).then_inc(s_hh, 1)

                def samples_hi(b, q2):
                    act.wait_ge(s_hs, 2)
                    a.copy(hhi[:, q2, :, LEAD + BLK:BT], hshi[:, :, bass.ds(b * SB, SB)].bitcast(F32)).then_inc(s_hh, 1)

                for kk in range(KD):
                    slice_hi(kk, 0, kk, LEAD, kk % 2)
                samples_hi(0, 0)
                split(0, 0)
                split(0, 1)
                with act.Fori(0, NBLK // 2) as i:
                    for q2 in range(2):
                        b = i * 2 + q2
                        following = i * 2 + 1 if q2 == 0 else 2 - i * 2

                        def chunk(kind, c, q, n, j):
                            act.wait_ge(s_mm, n + 1)
                            act.wait_ge(s_so, n + 1)
                            act.wait_ge(s_keep, n + 1)
                            a.mul(xb[:, q, :].rearrange("p (h t) -> p h t", h=2), pp[:, q, :, 0:half],
                                  0.5 if kind == "silu" else 1.0).then_inc(s_ev, 1)
                            split(b * (NCH // 2) + j + 1, q)
                            if kind != "plain":
                                if q == 0:
                                    slice_hi((b + 1) * KD + j, 1 - q2, bass.ds(j, 1), 0)
                                if kind == "conv":
                                    act.wait_ge(s_y, b * CC + c + 1)
                                else:
                                    act.wait_ge(s_ev, n + 3)
                                act.wait_ge(s_st[q], (b * (NCH // 2) + j) * 16 + 16)
                                src = yb[:, q] if kind == "conv" else xb[:, q, LEAD:LEAD + BLK]
                                a.activation(so[:, q], src, ACT.Tanh).then_inc(s_th, 1)

                        act.wait_ge(s_bp, b + 1)
                        a.copy(bar[:].rearrange("p (h t) -> p h t", h=2), pb[0:2 * HA, :, 0:half]).then_inc(s_br, 1)
                        samples_hi(following, 1 - q2)
                        pairs(act, b, chunk)

            @block.vector
            def _(dve):
                v = nc.vector
                dve.sem_inc(s_lo, 2)
                dve.sem_inc(s_so, 2)
                xs = k["xnT"][:, :, LEAD + T:LEAD + T + TS].rearrange("p k (b s) -> p k b s", s=NS)
                hv = hsf[:].rearrange("p k (b s) -> p k b s", s=NS)
                for kk in range(KD):
                    v.tensor_tensor(hv[:, kk], xs[:, kk], k["mscale"][:, 0, kk, 1:9].unsqueeze(2).broadcast_to([P, NB, NS]),
                                    ALU.mult).then_inc(s_hs0, 1)
                dve.wait_ge(s_hs0, KD)
                for kk in range(KD):
                    last = v.tensor_tensor(hv[:, kk], hv[:, kk], k["mshift"][:, 0, kk, 1:9].unsqueeze(2)
                                           .broadcast_to([P, NB, NS]), ALU.add)
                last.then_inc(s_hs, 1)
                dve.wait_ge(s_hs, 2)
                v.tensor_tensor(hslo[:], hsf[:], hshi[:].bitcast(F32), ALU.subtract).then_inc(s_hs, 1)
                dve.wait_ge(s_wbs, 1)
                v.tensor_tensor(wbl[:], wba, wbh[:].bitcast(F32), ALU.subtract).then_inc(s_wbs, 1)
                v.memset(hhi[:, 0, :, 0:LEAD].bitcast(F32), 0.0)
                v.memset(hlo[:, 0, :, 0:LEAD].bitcast(F32), 0.0)
                dve.wait_ge(s_ba, 1)
                v.tensor_copy(k["ba_s"][:], pb[0:TS, 1, 0:8]).then_inc(s_be, 1)

                def split(n, q):
                    dve.wait_ge(s_hi, n + 1)
                    v.tensor_tensor(wlo[:, q], raw[:, q], whi[:, q].bitcast(F32), ALU.subtract).then_inc(s_lo, 1)

                def modulate(block0, kk, lead, w=0):
                    cols = bass.ds(block0 * BLK + lead, LEAD + BLK - lead)
                    one = slice(kk, kk + 1) if isinstance(kk, int) else bass.ds(kk, 1)
                    v.tensor_scalar(hf[:, w, lead:], k["xnT"][:, one, cols].rearrange("p a t -> p (a t)"),
                                    k["pscale"][:, 0, one], k["pshift"][:, 0, one], ALU.mult, ALU.add).then_inc(s_h, 1)

                def slice_lo(count, q2, kk, lead, w=0):
                    dve.wait_ge(s_hh, count + 1)
                    one = slice(kk, kk + 1) if isinstance(kk, int) else bass.ds(kk, 1)
                    v.tensor_tensor(hlo[:, q2, one, lead:LEAD + BLK].rearrange("p a t -> p (a t)"), hf[:, w, lead:],
                                    hhi[:, q2, one, lead:LEAD + BLK].rearrange("p a t -> p (a t)").bitcast(F32),
                                    ALU.subtract).then_inc(s_hl, 1)

                def samples_lo(b, q2):
                    dve.wait_ge(s_hs, 3)
                    v.tensor_copy(hlo[:, q2, :, LEAD + BLK:BT], hslo[:, :, bass.ds(b * SB, SB)].bitcast(F32)).then_inc(s_hl, 1)

                modulate(0, 0, LEAD, 0)
                for kk in range(KD):
                    if kk + 1 < KD:
                        if kk > 0:
                            dve.wait_ge(s_hl, kk)
                        modulate(0, kk + 1, LEAD, (kk + 1) % 2)
                    slice_lo(kk, 0, kk, LEAD, kk % 2)
                samples_lo(0, 0)
                split(0, 0)
                split(1, 1)
                with dve.Fori(0, NBLK // 2) as i:
                    for q2 in range(2):
                        b = i * 2 + q2
                        following = i * 2 + 1 if q2 == 0 else 2 - i * 2

                        def chunk(kind, c, q, n, j):
                            fresh = kind != "plain" and q == 0
                            if fresh:
                                dve.wait_ge(s_hl, (b + 1) * PARTS + j + 1)
                                modulate(following, j, 0)
                            dve.wait_ge(s_ev, n + 3)
                            if kind == "conv":
                                taps = (b * CC + c) * (CW - 1)
                                for t in range(CW):
                                    src = xb[:, q, t + 1:t + 1 + BLK]
                                    tap = k["taps"][:, bass.ds(t * CC + c, 1)]
                                    if t == 0:
                                        ins = v.tensor_scalar(yb[:, q], src, tap, None, ALU.mult)
                                    else:
                                        dve.wait_ge(s_tap, taps + t)
                                        ins = v.scalar_tensor_tensor(yb[:, q], src, tap, yb[:, q], ALU.mult, ALU.add)
                                    ins.then_inc(s_tap if t < CW - 1 else s_y, 1)
                            split(n + 2, q)
                            if fresh:
                                slice_lo((b + 1) * PARTS + j + 1, 1 - q2, j, 0)
                            if kind == "plain":
                                dve.wait_ge(s_st[q], (b * (NCH // 2) + j) * 16 + 16)
                                v.tensor_copy(so[:, q], xb[:, q, LEAD:LEAD + BLK]).then_inc(s_so, 1)
                            else:
                                dve.wait_ge(s_th, b * 16 + c + 1)
                                src = yb[:, q] if kind == "conv" else xb[:, q, LEAD:LEAD + BLK]
                                v.scalar_tensor_tensor(so[:, q], so[:, q], 1.0, src, ALU.add, ALU.mult).then_inc(s_so, 1)

                        samples_lo(following, 1 - q2)
                        pairs(dve, b, chunk)
                        dve.wait_ge(s_ba, b + 2)
                        v.tensor_copy(k["ba"][:, bass.ds(b * 4, 4), :], pb[:, 0, 0:32].rearrange("p (j n) -> p j n", n=8)
                                      ).then_inc(s_be, 1)

            @block.gpsimd
            def _(pool):
                g = nc.gpsimd
                pool.sem_inc(s_keep, 2)
                for q in range(2):
                    pool.dma_start(io["projT"][q * 11:q * 11 + 11, :, 0:PAD].rearrange("c p t -> p c t"),
                                   k["zeros"][:].broadcast_to([P, 11, P])).then_inc(s_st[q], 16)
                with pool.Fori(0, NBLK) as b:
                    def chunk(kind, c, q, n, j):
                        pool.wait_ge(s_ev, n + 3)
                        if kind == "conv":
                            g.tensor_copy(k["xlast"][:, :, bass.ds(c, 1)], xb[:, q, LEAD + BLK - 3:LEAD + BLK].unsqueeze(2))
                        g.tensor_copy(k["projS"][:, bass.ds(c, 1), bass.ds(b * SB, SB)], xb[:, q:q + 1, LEAD + BLK:BT]
                                      ).then_inc(s_keep, 1)
                        pool.wait_ge(s_so, n + 3)
                        pool.dma_start(io["projT"][bass.ds(c, 1), :, bass.ds(b * BLK + PAD, BLK)].rearrange("c p t -> (c p) t"),
                                       so[:, q]).then_inc(s_st[q], 16)
                    pairs(pool, b, chunk)
                for q in range(2):
                    pool.wait_ge(s_st[q], NBLK * NCH // 2 * 16 + 16)
        m.clear_sems()


class Front:

    def __init__(self, m, tag, n, levels, elsewhere=None):
        sem = lambda name: m.sem(tag + name)
        self.n, self.levels = n, levels
        self.qkv = m.sb(tag + "qkv", [P, CC, n])
        self.sq = m.sb(tag + "squares", [n, 2 * HA, P])
        self.ss, self.ms, self.rs = (m.sb(tag + x, [n, 2, HA]) for x in ("sumsq", "sumsq_eps", "rnorm"))
        self.f = m.sb(tag + "factors", [n, 6, HA])
        self.g = m.sb(tag + "g_now", [n, HA])
        self.qq = m.sb(tag + "q_scaled", [n, 2, HA, P])
        self.kk = m.sb(tag + "k_scaled", [n, 4, HA, P])
        self.vb = m.sb(tag + "v_beta", [n, HA, P])
        self.knT = m.sb(tag + "knT", [P, HA, n])
        self.kqT = m.sb(tag + "kbT_qnT", [P, HA, 2, n])
        self.qgT = m.sb(tag + "qgT", [P, HA, n])
        self.dec = m.sb(tag + "decay", [n, HA, n])
        self.al = m.sb(tag + "LT_attnT", [n, HA, 2, n])
        self.ct = m.sb(tag + "CT", [n, levels, HA, n])
        self.xx = m.sb(tag + "X_XT", [n, 2, HA, n])
        self.ys = m.sb(tag + "Y", [n, HA, n])
        self.nwT = m.sb(tag + "minus_wT", [P, HA, n])
        self.gp = m.ps(tag + "delta_ps", [P, 4, 512])
        self.qkv_ps, self.cs_ps = (self.gp[:, 0:3, :], self.gp[:, 3, :]) if elsewhere is None else elsewhere
        self.s_in = sem("qkv_loaded")
        self.s_g = sem("g_placed")
        self.s_t1, self.s_r = sem("qkv_turned"), sem("cumsum_spread")
        self.s_sq, self.s_ss, self.s_ms, self.s_rs, self.s_f = (sem(x) for x in ("squared", "sumsq_done", "sumsq_eps_done", "rnorm_done", "factors_done"))
        self.s_sc, self.s_sk, self.s_dec, self.s_bt, self.s_kt = (sem(x) for x in (
            "qk_scaled", "kg_v_scaled", "decay_done", "turned_back", "turned_read"))
        self.s_gm, self.s_al, self.s_c, self.s_c1 = (sem(x) for x in ("gram_done", "gram_decayed", "level_cut", "level0_turned"))
        self.s_x, self.s_y, self.s_ye, self.s_z = ([sem(f"{x}_{g}") for g in range(2)] for x in ("X_done", "Y_done", "Y_read", "Z_done"))
        self.s_w, self.s_nw, self.s_qg = sem("wT_done"), sem("wT_read"), sem("qgT_read")

    def credits_pe(self):
        return (self.s_t1, self.s_r, self.s_bt, self.s_gm, self.s_c1, *self.s_y, *self.s_z, self.s_w)

    def credits_act(self):
        return (self.s_sq, self.s_dec, self.s_kt, *self.s_ye, self.s_nw, self.s_qg)

    def credits_dve(self):
        return (self.s_ss, self.s_ms, self.s_f, self.s_sc, self.s_sk, self.s_al, *self.s_x)


def was(t, per=1):
    return t * per + 1


def now(t, per=1, step=None):
    return t * per + 2 + (per - 1 if step is None else step)


def front_pe(nc, pe, F, k, t, ut, neg, free_turn, free_spread, free_back):
    n, L = F.n, F.levels
    mm, tr, ident = nc.tensor.matmul, nc.tensor.transpose, k["ident"]
    pn = ident[0:n, 0:n]
    bank = lambda b: F.gp[:, b, :]
    flat = F.gp[:].rearrange("p b c -> p (b c)")

    def turn():
        pe.wait_ge(F.s_in, now(t) * 16)
        free_turn()
        for c in range(CC):
            last = tr(F.qkv_ps[0:n, c // HA, (c % HA) * P:(c % HA) * P + P], F.qkv[:, c, :], ident[:])
        last.then_inc(F.s_t1, 1)

    def spread():
        pe.wait_ge(F.s_g, now(t))
        free_spread()
        out = F.cs_ps[0:n, 0:HA * n].rearrange("p (h i) -> p h i", h=HA)
        mm(out, pn, neg.unsqueeze(1).broadcast_to([n, HA, n]), start=True, stop=False)
        for h in range(HA):
            last = mm(out[:, h, :], F.g[:, h:h + 1].broadcast_to([n, n]), ut, start=False, stop=(h == HA - 1))
        last.then_inc(F.s_r, 1)

    def back():
        pe.wait_ge(F.s_sc, now(t))
        free_back()
        for h in range(HA):
            tr(bank(0)[:, h * n:(h + 1) * n], F.kk[:, 0, h, :], pn)
            tr(flat[:, 512 + 2 * h * n:512 + (2 * h + 1) * n], F.kk[:, 1, h, :], pn)
            tr(flat[:, 512 + (2 * h + 1) * n:512 + (2 * h + 2) * n], F.qq[:, 0, h, :], pn)
            last = tr(bank(3)[:, h * n:(h + 1) * n], F.qq[:, 1, h, :], pn)
        last.then_inc(F.s_bt, 1)

    def gram():
        pe.wait_ge(F.s_kt, now(t))
        for h in range(HA):
            last = mm(flat[0:n, 2 * h * n:2 * (h + 1) * n], F.knT[:, h, :], F.kqT[:, h], start=True, stop=True)
        last.then_inc(F.s_gm, 1)

    def level0():
        pe.wait_ge(F.s_c, now(t, L, 0))
        pe.wait_ge(F.s_qg, now(t))
        for h in range(HA):
            at = h % 2 * n
            last = tr(bank(2 * (h // 2) + 1)[0:n, at:at + n], F.ct[:, 0, h, :], pn)
        last.then_inc(F.s_c1, 1)

    def level_y(lv, g):
        pe.wait_ge(F.s_c, now(t, L, lv))
        pe.wait_ge(F.s_x[g], now(t, L + 1, lv))
        for e in range(2):
            last = mm(bank(2 * g)[0:n, e * n:(e + 1) * n], F.ct[:, lv, 2 * g + e, :], F.xx[:, 0, 2 * g + e, :], start=True, stop=True)
        last.then_inc(F.s_y[g], 1)

    def level_z(lv, g):
        pe.wait_ge(F.s_ye[g], now(t, L - 1, lv - 1))
        for e in range(2):
            h = 2 * g + e
            if lv < L - 1:
                mm(bank(2 * g + 1)[0:n, e * n:(e + 1) * n], F.xx[:, 1, h, :], F.ys[:, h, :], start=True, stop=True)
            last = mm(bank(2 * g + 1)[0:n, (2 + e) * n:(3 + e) * n], F.ys[:, h, :], F.xx[:, 1, h, :], start=True, stop=True)
        last.then_inc(F.s_z[g], 1)

    def w():
        for g in range(2):
            pe.wait_ge(F.s_x[g], now(t, L + 1))
        for h in range(HA):
            last = mm(bank(0)[:, h * n:(h + 1) * n], F.kk[:, 2, h, :], F.xx[:, 1, h, :], start=True, stop=True)
        last.then_inc(F.s_w, 1)

    return turn, spread, back, gram, level0, level_y, level_z, w


def front_act(nc, act, F, t, negc, free_kt, free_nw, free_sq):
    n, L = F.n, F.levels
    a = nc.scalar

    def square():
        act.wait_ge(F.s_t1, now(t))
        free_sq()
        a.activation(F.sq[:].rearrange("p (b h) d -> p b (h d)", b=2), F.qkv_ps[0:n, 0:2, :], ACT.Square).then_inc(F.s_sq, 1)

    def decay():
        act.wait_ge(F.s_r, now(t))
        act.wait_ge(F.s_al, was(t))
        for h in range(HA):
            last = a.activation(F.dec[:, h, :], F.cs_ps[0:n, h * n:(h + 1) * n], ACT.Exp, bias=negc(h))
        last.then_inc(F.s_dec, 1)

    def read_back():
        act.wait_ge(F.s_bt, now(t))
        free_kt()
        flat = F.gp[:].rearrange("p b c -> p (b c)")
        a.copy(F.knT[:].rearrange("p h i -> p (h i)"), flat[:, 0:HA * n])
        a.copy(F.kqT[:].rearrange("p h v i -> p (h v i)"), flat[:, 512:512 + 2 * HA * n]).then_inc(F.s_kt, 1)
        a.copy(F.qgT[:].rearrange("p h i -> p (h i)"), flat[:, 3 * 512:3 * 512 + HA * n]).then_inc(F.s_qg, 1)

    def read_y(lv, g):
        act.wait_ge(F.s_y[g], now(t, L - 1, lv - 1))
        act.wait_ge(F.s_z[g], t * (L - 1) + lv)
        a.copy(F.ys[:, 2 * g:2 * g + 2].rearrange("p h i -> p (h i)"), F.gp[0:n, 2 * g, 0:2 * n]).then_inc(F.s_ye[g], 1)

    def read_w():
        act.wait_ge(F.s_w, now(t))
        free_nw()
        a.mul(F.nwT[:].rearrange("p h i -> p (h i)"), F.gp[:, 0, 0:HA * n], -1.0).then_inc(F.s_nw, 1)

    return square, decay, read_back, read_y, read_w


def front_dve(nc, dve, F, k, t, table, beta, free_scaled, free_al):
    n, L = F.n, F.levels
    v = nc.vector
    wide = lambda x, d: x.unsqueeze(len(x.shape)).broadcast_to(list(x.shape) + [d])

    def norms():
        dve.wait_ge(F.s_sq, now(t))
        v.tensor_reduce(F.ss[:].rearrange("p a h -> p (a h)"), F.sq[:], AX.X, ALU.add).then_inc(F.s_ss, 1)
        dve.wait_ge(F.s_ss, now(t))
        v.tensor_scalar(F.ms[:], F.ss[:], EPS, None, ALU.add).then_inc(F.s_ms, 1)

    src = lambda b, r: F.qkv_ps[0:n, b, :].rearrange("p (h d) -> p h d", h=HA).unsqueeze(1).broadcast_to([n, r, HA, P])

    def scale():
        dve.wait_ge(F.s_rs, now(t))
        dve.wait_ge(F.s_sk, was(t))
        v.tensor_tensor(F.f[:, 0:2], table(0, 2), F.rs[:, 0:1, :].broadcast_to([n, 2, HA]), ALU.mult)
        v.tensor_tensor(F.f[:, 2:6], table(2, 6), F.rs[:, 1:2, :].broadcast_to([n, 4, HA]), ALU.mult).then_inc(F.s_f, 1)
        dve.wait_ge(F.s_f, now(t))
        dve.wait_ge(F.s_bt, was(t))
        v.tensor_tensor(F.kk[:, 0:2], src(1, 2), wide(F.f[:, 2:4], P), ALU.mult)
        v.tensor_tensor(F.qq[:], src(0, 2), wide(F.f[:, 0:2], P), ALU.mult).then_inc(F.s_sc, 1)

    def scale_rest():
        free_scaled()
        v.tensor_tensor(F.kk[:, 2:4], src(1, 2), wide(F.f[:, 4:6], P), ALU.mult)
        v.tensor_tensor(F.vb[:], F.qkv_ps[0:n, 2, :].rearrange("p (h d) -> p h d", h=HA), beta, ALU.mult).then_inc(F.s_sk, 1)

    def decayed():
        dve.wait_ge(F.s_gm, now(t))
        dve.wait_ge(F.s_dec, now(t))
        free_al()
        flat = F.gp[:].rearrange("p b c -> p (b c)")
        v.tensor_tensor(F.al[:], flat[0:n, 0:2 * HA * n].rearrange("p (h v i) -> p h v i", h=HA, v=2),
                        F.dec[:].unsqueeze(2).broadcast_to([n, HA, 2, n]), ALU.mult).then_inc(F.s_al, 1)

    def start_x():
        eye = k["ident"][0:n, 0:n].unsqueeze(1).broadcast_to([n, 2, n])
        dve.wait_ge(F.s_c, now(t, L, 0))
        for g in range(2):
            v.tensor_tensor(F.xx[:, 1, 2 * g:2 * g + 2], eye, F.ct[:, 0, 2 * g:2 * g + 2], ALU.subtract).then_inc(F.s_x[g], 1)
        dve.wait_ge(F.s_c1, now(t))
        for g in range(2):
            v.tensor_tensor(F.xx[:, 0, 2 * g:2 * g + 2], eye, F.gp[0:n, 2 * g + 1, 0:2 * n].rearrange("p (h i) -> p h i", h=2),
                            ALU.subtract).then_inc(F.s_x[g], 1)

    def step_x(lv, g):
        dve.wait_ge(F.s_z[g], now(t, L - 1, lv - 1))
        dve.wait_ge(F.s_x[g], now(t, L + 1, lv))
        lo = 0 if lv < L - 1 else 1
        x = F.xx[:, lo:2, 2 * g:2 * g + 2].rearrange("p a h i -> p a (h i)")
        z = F.gp[0:n, 2 * g + 1, 2 * lo * n:4 * n].rearrange("p (a q) -> p a q", q=2 * n)
        v.tensor_tensor(x, x, z, ALU.subtract).then_inc(F.s_x[g], 1)

    return norms, scale, scale_rest, decayed, start_x, step_x


def front_pool(nc, pool, F, k, t, g_src, lev):
    n, L = F.n, F.levels
    g = nc.gpsimd

    def place():
        pool.wait_ge(F.s_r, was(t))
        g.tensor_copy(F.g[:], g_src).then_inc(F.s_g, 1)

    def rsqrt():
        pool.wait_ge(F.s_ms, now(t))
        g.tensor_tensor(F.rs[:].rearrange("p a h -> p (a h)"), F.ms[:].rearrange("p a h -> p (a h)"),
                        k["nhalf"][0:n, 0:2 * HA], ALU.pow).then_inc(F.s_rs, 1)

    def cut():
        pool.wait_ge(F.s_w, was(t))
        pool.wait_ge(F.s_al, now(t))
        for lv in range(L):
            g.tensor_tensor(F.ct[:, lv], F.al[:, :, 0, :], lev(lv).unsqueeze(1).broadcast_to([n, HA, n]), ALU.mult
                            ).then_inc(F.s_c, 1)

    return place, rsqrt, cut


def mixer(nc, io, k):
    with ExitStack() as ctx:
        m = Mem(nc, ctx)
        sp_ = m.ps("attn_ps", [P, 4, 512])
        F = Front(m, "", P, 7, (sp_[:, 1:4, :], sp_[:, 0, :]))
        L = F.levels
        th = m.sb("beta_tanh", [P, NT, HA])
        beta = m.sb("beta", [P, NT, HA])
        xa = m.sb("a_biased", [P, NT, HA])
        ax = m.sb("a_abs", [P, NT, HA])
        na = m.sb("a_neg", [P, NT, HA])
        ea = m.sb("decay_rate", [P, HA])
        gg = m.sb("g_all", [P, NT, HA])
        gc = m.sb("g_cumsum", [P, 2, NT, HA])
        negc = m.sb("minus_g_cumsum", [P, NT, HA])
        dk = m.sb("g_to_last", [P, NT, HA])
        gl = m.sb("g_last_exp", [P, NT, HA])
        tab = m.sb("factor_table", [P, NT, 6, HA])
        zT = m.sb("zT", [P, HA, P])
        vn = m.sb("v_new", [P, HA, P])
        osq = m.sb("o_squares", [P, HA, P])
        oss, oms, ors = (m.sb(x, [P, HA]) for x in ("o_sumsq", "o_meansq", "o_rrms"))
        on = m.sb("o_normed", [P, HA, P])
        oaT = m.sb("oaT", [P, HA, P])
        qT = m.sb("attn_qT", [P, 4, P])
        kvT = m.sb("attn_kT_vT", [P, 2, 2 * W])
        vt = m.sb("attn_v", [P, 2, P])
        sm = m.sb("scores", [P, HB, 2 * W])
        mx, nm, esk, dn, rc = (m.sb(x, [P, HB]) for x in ("score_max", "minus_max", "sink_exp", "prob_sum", "prob_recip"))
        pT = m.sb("probsT", [P, HB, 2, P])
        obT = m.sb("obT", [P, 4, P])
        kl = m.sb("k_last", [P, P])
        s_pre = m.sem("tables_step")
        s_pe0, s_act0 = m.sem("cumsums_summed"), m.sem("tables_act_step")
        s_z, s_qk = m.sem("z_loaded"), m.sem("attn_loaded")
        s_v, s_vn, s_o, s_s, s_su = (m.sem(x) for x in ("v_new_done", "v_new_read", "o_done", "state_added", "state_updated"))
        s_osq, s_oss, s_oms, s_ors, s_on, s_ot, s_oa, s_ost = (m.sem(x) for x in (
            "o_squared", "o_sumsq_done", "o_meansq_done", "o_rrms_done", "o_normed_done", "o_turned", "oaT_done", "oaT_stored"))
        s_vT, s_vE, s_sc, s_msk, s_mx, s_nm, s_ex, s_es, s_dn, s_rc, s_pr, s_pt, s_pe, s_ov, s_ob, s_obst, s_bm, s_d8 = (m.sem(x) for x in (
            "attn_v_turned", "attn_v_read", "scores_done", "scores_masked", "max_done", "max_negated", "exp_done", "sink_exp_done",
            "prob_sum_done", "recip_done", "probs_done", "probs_turned", "probsT_read", "attn_out_done", "obT_done", "obT_stored",
            "band_set", "sink_less_max"))
        s_d9 = m.sem("max_with_sink")
        s_fin0, s_fin = m.sem("last_rows_read"), k["states_stored"]
        flat3 = lambda x: x[:].rearrange("p t h -> p (t h)")

        def tiles(eng, tile):
            with eng.Fori(0, NT - 1) as t:
                tile(t, True)
            tile(NT - 1, False)

        with nc.Block() as block:
            @block.sync
            def _(sp):
                for s in (F.s_in, s_z, s_qk):
                    sp.sem_inc(s, 16)
                with sp.Fori(0, NT) as t:
                    pT_ = io["projT"]
                    sp.wait_ge(F.s_t1, was(t))
                    sp.dma_start(F.qkv[:], pT_[0:CC, :, bass.ds(t * P + PAD, P)].rearrange("c p t -> p c t")).then_inc(F.s_in, 16)
                    sp.wait_ge(s_sc, was(t))
                    sp.wait_ge(s_vT, was(t))
                    for g in range(2):
                        sp.dma_start(qT[64 * g:64 * g + 64, :, :],
                                     pT_[16 + 2 * g:18 + 2 * g, :, bass.ds(t * P + PAD, P)]
                                     .rearrange("c (e d) t -> d (c e) t", e=2)).then_inc(s_qk, 16)
                    sp.dma_start(kvT[:], pT_[20:22, :, bass.ds(t * P, 2 * W)].rearrange("c p t -> p c t")).then_inc(s_qk, 16)
                    sp.wait_ge(s_oa, was(t))
                    sp.dma_start(zT[:], pT_[12:16, :, bass.ds(t * P + PAD, P)].rearrange("c p t -> p c t")).then_inc(s_z, 16)
                for c in range(KD):
                    for g in range(2):
                        r = c * P + g * DB if c < 4 else HA * P + (4 * g + c - 4) * DB
                        sp.dma_start(k["w_o_raw"][64 * g:64 * g + 64, c, :], io["w_o"][r:r + DB, :]).then_inc(k["w_o_loaded"], 16)

            @block.tensor
            def _(pe):
                mm, tr, ident = nc.tensor.matmul, nc.tensor.transpose, k["ident"]
                pe.wait_ge(s_pre, 6)
                mm(F.gp[:, 0, 0:NT * HA], k["ut"][:], flat3(gg), start=True, stop=True)
                mm(F.gp[:, 0, NT * HA:2 * NT * HA], k["ones"][:], flat3(gg), start=True, stop=True).then_inc(s_pe0, 1)
                for s in F.credits_pe() + (s_v, s_o, s_s, s_ot, s_vT, s_sc, s_pt, s_ov):
                    pe.sem_inc(s, 1)
                pe.wait_ge(s_pre, 7)

                def front(t):
                    return front_pe(nc, pe, F, k, t, k["ut"][:], k["neg"][:],
                                    lambda: pe.wait_ge(s_pe, was(t)),
                                    lambda: pe.wait_ge(s_ob, was(t)),
                                    lambda: (pe.wait_ge(s_on, was(t)), pe.wait_ge(s_su, was(t, HA))))

                def turn_out(t):
                    pe.wait_ge(s_on, now(t))
                    for h in range(HA):
                        last = tr(sp_[:, 1, h * P:(h + 1) * P], on[:, h, :], ident[:])
                    last.then_inc(s_ot, 1)

                def begin(t, tile_before):
                    turn, spread, back, gram, level0, level_y, level_z, w = front(t)
                    back()
                    if tile_before is not None:
                        turn_out(tile_before)
                    pe.wait_ge(s_qk, t * 48 + 64)
                    pe.wait_ge(F.s_dec, now(t))
                    for j in range(2):
                        last = tr(sp_[:, 0, j * P:(j + 1) * P], kvT[:, 1, j * W:(j + 1) * W], ident[:])
                    last.then_inc(s_vT, 1)
                    gram()
                    pe.wait_ge(s_vE, now(t))
                    pe.wait_ge(F.s_sk, now(t))
                    pe.wait_ge(s_oa, was(t))
                    for g in range(2):
                        for c in range(4):
                            at = slice(64 * g, 64 * g + 64)
                            last = mm(sp_[:, 2 * g + c // 2, (c % 2) * 256:(c % 2) * 256 + 256], qT[at, c, :], kvT[at, 0, :],
                                      start=True, stop=True)
                    last.then_inc(s_sc, 1)
                    level0()

                def tile(t, more):
                    turn, spread, back, gram, level0, level_y, level_z, w = front(t)
                    for lv in range(1, L):
                        level_y(lv, 0)
                        level_y(lv, 1)
                        if lv == L - 1:
                            pe.wait_ge(s_pr, now(t))
                            for h in range(HB):
                                for j in range(2):
                                    last = tr(sp_[:, h // 2, (h % 2) * 256 + j * P:(h % 2) * 256 + (j + 1) * P],
                                              sm[:, h, j * W:(j + 1) * W], ident[:])
                            last.then_inc(s_pt, 1)
                        level_z(lv, 0)
                        level_z(lv, 1)
                    w()
                    if more:
                        next_turn, next_spread, *_ = front(t + 1)
                        next_turn()
                    pe.wait_ge(s_pe, now(t))
                    for g in range(2):
                        for c in range(4):
                            for j in range(2):
                                last = mm(sp_[64 * g:64 * g + 64, 0, c * P:(c + 1) * P], vt[:, j, 64 * g:64 * g + 64],
                                          pT[:, 4 * g + c, j, :], start=(j == 0), stop=(j == 1))
                    last.then_inc(s_ov, 1)
                    pe.wait_ge(F.s_nw, now(t))
                    pe.wait_ge(s_su, was(t, HA))
                    for h in range(HA):
                        at = slice(h * P, (h + 1) * P)
                        mm(F.gp[:, 1, at], F.xx[:, 1, h, :], F.vb[:, h, :], start=True, stop=False)
                        last = mm(F.gp[:, 1, at], F.nwT[:, h, :], k["state"][:, h, :], start=False, stop=True)
                    last.then_inc(s_v, 1)
                    if more:
                        next_spread()
                    pe.wait_ge(s_vn, now(t))
                    for h in range(HA):
                        at = slice(h * P, (h + 1) * P)
                        mm(F.gp[:, 2, at], F.qgT[:, h, :], k["state"][:, h, :], start=True, stop=False)
                        last = mm(F.gp[:, 2, at], F.al[:, h, 1, :], vn[:, h, :], start=False, stop=True)
                    last.then_inc(s_o, 1)
                    for h in range(HA):
                        last = mm(F.gp[:, 3, h * P:(h + 1) * P], F.kk[:, 3, h, :], vn[:, h, :], start=True, stop=True)
                    last.then_inc(s_s, 1)
                    if more:
                        begin(t + 1, t)
                    else:
                        turn_out(t)

                turn, spread, *_ = front(0)
                turn()
                spread()
                begin(0, None)
                tiles(pe, tile)
                pe.wait_ge(s_ov, now(NT - 1))
                pe.wait_ge(s_ob, now(NT - 1))
                pe.wait_ge(s_oa, now(NT - 1))
                tr(sp_[:, 1, 0:P], kvT[:, 0, W:2 * W], ident[:])
                tr(sp_[0:36, 2, 0:P], k["xlast"][:].rearrange("p i c -> p (i c)"), ident[:]).then_inc(s_pe0, 1)

            @block.scalar
            def _(act):
                a = nc.scalar
                a.activation(th[:], k["ba"][:, :, 0:HA], ACT.Tanh, scale=0.5).then_inc(s_act0, 1)
                a.activation(ea[:], k["alog"][:], ACT.Exp).then_inc(s_act0, 1)
                act.wait_ge(s_pre, 3)
                a.activation(ax[:], ax[:], ACT.Exp, scale=-1.0).then_inc(s_act0, 1)
                act.wait_ge(s_act0, 3)
                a.activation(ax[:], ax[:], ACT.Ln, bias=1.0).then_inc(s_act0, 1)
                act.wait_ge(s_pre, 8)
                a.activation(gc[:, 0], gc[:, 0], ACT.Exp).then_inc(s_act0, 1)
                a.activation(gl[:], gc[:, 1], ACT.Exp).then_inc(s_act0, 1)
                a.activation(dk[:], dk[:], ACT.Exp).then_inc(s_act0, 1)
                for s in (s_ost, s_obst):
                    act.sem_inc(s, 16)
                for s in F.credits_act() + (s_vn, s_osq, s_vE, s_ex, s_es, s_pe, s_ob):
                    act.sem_inc(s, 1)

                def front(t):
                    return front_act(nc, act, F, t, lambda h: negc[:, bass.ds(t, 1), h:h + 1].rearrange("p a h -> p (a h)"),
                                     lambda: act.wait_ge(s_o, was(t)), lambda: act.wait_ge(s_v, was(t)),
                                     lambda: act.wait_ge(F.s_ss, was(t)))

                def begin(t):
                    square, decay, read_back, read_y, read_w = front(t)
                    read_back()
                    act.wait_ge(s_vT, now(t))
                    act.wait_ge(s_ov, was(t))
                    a.copy(vt[:].rearrange("p j d -> p (j d)"), sp_[:, 0, 0:2 * P]).then_inc(s_vE, 1)

                def tile(t, more):
                    square, decay, read_back, read_y, read_w = front(t)

                    def exps(lo):
                        for h in range(lo, lo + 2):
                            last = a.activation(sm[:, h, :], sm[:, h, :], ACT.Exp, bias=nm[:, h:h + 1], accum_out=dn[:, h:h + 1])
                        return last

                    for lv in range(1, L):
                        for g in range(2):
                            read_y(lv, g)
                            step = 2 * lv + g
                            if step == 5:
                                act.wait_ge(s_nm, now(t))
                                act.wait_ge(s_ex, was(t))
                                act.wait_ge(s_dn, was(t))
                            if 5 <= step < 8:
                                exps(2 * (step - 5))
                            if step == 8:
                                exps(HB - 2).then_inc(s_ex, 1)
                                act.wait_ge(s_d8, now(t))
                                a.activation(esk[:], esk[:], ACT.Exp).then_inc(s_es, 1)
                    act.wait_ge(s_pt, now(t))
                    for j in (0, 2):
                        ins = a.copy(pT[:].rearrange("p (b e) j q -> p b (e j q)", b=4)[:, j:j + 2], sp_[:, j:j + 2, :])
                    ins.then_inc(s_pe, 1)
                    read_w()
                    if more:
                        next_square, next_decay, *_ = front(t + 1)
                        next_square()
                    act.wait_ge(s_ov, now(t))
                    act.wait_ge(s_obst, was(t) * 16)
                    a.copy(obT[:].rearrange("p c q -> p (c q)"), sp_[:, 0, :]).then_inc(s_ob, 1)
                    act.wait_ge(s_v, now(t))
                    a.copy(vn[:].rearrange("p h d -> p (h d)"), F.gp[:, 1, :]).then_inc(s_vn, 1)
                    if more:
                        next_decay()
                    act.wait_ge(s_o, now(t))
                    act.wait_ge(s_oss, was(t))
                    a.activation(osq[:].rearrange("p h d -> p (h d)"), F.gp[:, 2, :], ACT.Square).then_inc(s_osq, 1)
                    act.wait_ge(s_ob, now(t))
                    act.dma_start(io["oT"][4:8, :, bass.ds(t * P, P)].rearrange("c p t -> p c t"), obT[:]).then_inc(s_obst, 16)
                    if more:
                        begin(t + 1)
                    act.wait_ge(s_oa, now(t))
                    act.dma_start(io["oT"][0:4, :, bass.ds(t * P, P)].rearrange("c p t -> p c t"), oaT[:]).then_inc(s_ost, 16)

                square, decay, *_ = front(0)
                square()
                decay()
                begin(0)
                tiles(act, tile)

            @block.vector
            def _(dve):
                v = nc.vector
                wide = lambda x, d: x.unsqueeze(len(x.shape)).broadcast_to(list(x.shape) + [d])
                per_head = lambda x: x[:].unsqueeze(1).broadcast_to([P, NT, HA])
                v.tensor_tensor(xa[:], k["ba"][:, :, HA:2 * HA], per_head(k["dtb"]), ALU.add).then_inc(s_pre, 1)
                dve.wait_ge(s_pre, 1)
                v.tensor_scalar(na[:], xa[:], -1.0, None, ALU.mult).then_inc(s_pre, 1)
                dve.wait_ge(s_pre, 2)
                v.tensor_tensor(ax[:], xa[:], na[:], ALU.max).then_inc(s_pre, 1)
                dve.wait_ge(s_act0, 4)
                v.scalar_tensor_tensor(xa[:], xa[:], 0.0, ax[:], ALU.max, ALU.add).then_inc(s_pre, 1)
                dve.wait_ge(s_pre, 4)
                v.tensor_scalar(xa[:], xa[:], -1.0, None, ALU.mult).then_inc(s_pre, 1)
                dve.wait_ge(s_pre, 5)
                v.tensor_tensor(gg[:], xa[:], per_head(ea), ALU.mult).then_inc(s_pre, 1)
                dve.wait_ge(s_pe0, 1)
                v.tensor_copy(gc[:].rearrange("p a t h -> p (a t h)"), F.gp[:, 0, 0:2 * NT * HA]).then_inc(s_pre, 1)
                dve.wait_ge(s_pre, 7)
                v.tensor_scalar(negc[:], gc[:, 0], -1.0, None, ALU.mult)
                v.tensor_tensor(dk[:], gc[:, 1], gc[:, 0], ALU.subtract).then_inc(s_pre, 1)
                v.tensor_scalar(beta[:], th[:], 0.5, 0.5, ALU.mult, ALU.add).then_inc(s_pre, 1)
                q_scale = float(P) ** -0.5
                v.memset(tab[:, :, 0, :], q_scale)
                v.memset(tab[:, :, 2, :], 1.0)
                dve.wait_ge(s_act0, 7)
                dve.wait_ge(s_pre, 9)
                v.tensor_scalar(tab[:, :, 1, :], gc[:, 0], q_scale, None, ALU.mult)
                v.tensor_copy(tab[:, :, 3, :], beta[:])
                v.tensor_tensor(tab[:, :, 4, :], beta[:], gc[:, 0], ALU.mult)
                v.tensor_copy(tab[:, :, 5, :], dk[:]).then_inc(s_pre, 1)
                dve.wait_ge(s_pre, 10)
                for s in F.credits_dve() + (s_oss, s_oms, s_on, s_oa, s_su, s_msk, s_mx, s_nm, s_dn, s_rc, s_pr, s_d8, s_d9):
                    dve.sem_inc(s, 1)

                def front(t):
                    return front_dve(nc, dve, F, k, t, lambda lo, hi: tab[:, bass.ds(t, 1), lo:hi, :].rearrange("p a f h -> p (a f) h"),
                                     wide(beta[:, bass.ds(t, 1), :].rearrange("p a h -> p (a h)"), P),
                                     lambda: dve.wait_ge(s_s, was(t)), lambda: dve.wait_ge(s_o, was(t)))

                def begin(t):
                    norms, scale, scale_rest, decayed, start_x, step_x = front(t)
                    decayed()
                    start_x()
                    dve.wait_ge(s_sc, now(t))
                    dve.wait_ge(s_bm, now(t))
                    dve.wait_ge(s_pt, was(t))
                    v.scalar_tensor_tensor(sm[:], sp_[:].rearrange("p b (h q) -> p (b h) q", h=2), float(DB) ** -0.5,
                                           k["band_now"][:].unsqueeze(1).broadcast_to([P, HB, 2 * W]), ALU.mult, ALU.add
                                           ).then_inc(s_msk, 1)

                def tile(t, more):
                    norms, scale, scale_rest, decayed, start_x, step_x = front(t)

                    def maxes(lo):
                        dve.wait_ge(s_msk, now(t))
                        dve.wait_ge(s_nm, was(t))
                        return v.tensor_reduce(mx[:, lo:lo + HB // 2], sm[:, lo:lo + HB // 2], AX.X, ALU.max)

                    def probs(lo):
                        at = slice(lo, lo + HB // 2)
                        return v.tensor_tensor(sm[:, at], sm[:, at], wide(rc[:, at], 2 * W), ALU.mult)

                    for lv in range(1, L):
                        for g in range(2):
                            step_x(lv, g)
                            if lv == 1 and g == 0:
                                maxes(0)
                            if lv == 1 and g == 1:
                                maxes(HB // 2).then_inc(s_mx, 1)
                                dve.wait_ge(s_mx, now(t))
                                dve.wait_ge(s_ex, was(t))
                                dve.wait_ge(s_dn, was(t))
                                v.tensor_tensor(nm[:], mx[:], k["sink"][:], ALU.max).then_inc(s_d9, 1)
                                dve.wait_ge(s_d9, now(t))
                                v.tensor_tensor(esk[:], k["sink"][:], nm[:], ALU.subtract).then_inc(s_d8, 1)
                                dve.wait_ge(s_d8, now(t))
                                v.tensor_scalar(nm[:], nm[:], -1.0, None, ALU.mult).then_inc(s_nm, 1)
                            if lv == 4 and g == 1:
                                dve.wait_ge(s_ex, now(t))
                                dve.wait_ge(s_es, now(t))
                                dve.wait_ge(s_pr, was(t))
                                v.tensor_tensor(rc[:], dn[:], esk[:], ALU.add).then_inc(s_dn, 1)
                                dve.wait_ge(s_dn, now(t))
                                v.reciprocal(rc[:], rc[:]).then_inc(s_rc, 1)
                                dve.wait_ge(s_rc, now(t))
                                probs(0)
                            if lv == 5 and g == 1:
                                probs(HB // 2).then_inc(s_pr, 1)
                    if more:
                        next_norms, next_scale, next_rest, *_ = front(t + 1)
                        next_norms()
                        next_scale()
                    dve.wait_ge(s_osq, now(t))
                    v.tensor_reduce(oss[:], osq[:], AX.X, ALU.add).then_inc(s_oss, 1)
                    dve.wait_ge(s_oss, now(t))
                    v.tensor_scalar(oms[:], oss[:], 1.0 / P, EPS, ALU.mult, ALU.add).then_inc(s_oms, 1)
                    dve.wait_ge(s_s, now(t))
                    for h in range(HA):
                        v.scalar_tensor_tensor(k["state"][:, h, :], k["state"][:, h, :],
                                               gl[:, bass.ds(t, 1), h:h + 1].rearrange("p a h -> p (a h)"),
                                               F.gp[:, 3, h * P:(h + 1) * P], ALU.mult, ALU.add).then_inc(s_su, 1)
                    dve.wait_ge(s_ors, t + 1)
                    v.tensor_tensor(on[:], F.gp[:, 2, :].rearrange("p (h d) -> p h d", h=HA), wide(ors[:], P), ALU.mult
                                    ).then_inc(s_on, 1)
                    if more:
                        next_rest()
                    dve.wait_ge(s_ot, now(t))
                    dve.wait_ge(s_z, now(t) * 16)
                    dve.wait_ge(s_ost, was(t) * 16)
                    v.scalar_tensor_tensor(oaT[:].rearrange("p h q -> p (h q)"), sp_[:, 1, :], k["vcol"][:, V_GDN:V_GDN + 1],
                                           zT[:].rearrange("p h q -> p (h q)"), ALU.mult, ALU.mult).then_inc(s_oa, 1)
                    if more:
                        begin(t + 1)

                norms, scale, scale_rest, *_ = front(0)
                norms()
                scale()
                scale_rest()
                begin(0)
                tiles(dve, tile)
                dve.wait_ge(s_pe0, 2)
                v.tensor_copy(kl[:], sp_[:, 1, 0:P])
                v.tensor_copy(k["xrow"][:], sp_[0:36, 2, 0:P]).then_inc(s_fin0, 1)

            @block.gpsimd
            def _(pool):
                g = nc.gpsimd
                for s in (F.s_g, F.s_rs, F.s_c, s_bm):
                    pool.sem_inc(s, 1)
                pool.wait_ge(s_pre, 10)
                pool.sem_inc(s_bm, 1)

                def front(t):
                    return front_pool(nc, pool, F, k, t, gg[:, bass.ds(t, 1), :].rearrange("p a h -> p (a h)"),
                                      lambda lv: k["lev"][:, lv, :])

                def tile(t, more):
                    pool.wait_ge(s_msk, now(t))
                    g.tensor_tensor(k["band_now"][:, 0:W], k["band"][:, 0:W], k["ones"][:], ALU.mult).then_inc(s_bm, 1)
                    if more:
                        next_place, next_rsqrt, next_cut = front(t + 1)
                        next_place()
                        next_rsqrt()
                    pool.wait_ge(s_oms, now(t))
                    g.tensor_tensor(ors[:], oms[:], k["nhalf"][:, 0:HA], ALU.pow).then_inc(s_ors, 1)
                    if more:
                        next_cut()

                for step in front(0):
                    step()
                tiles(pool, tile)
                pool.wait_ge(s_obst, 16 * (NT + 1))
                pool.wait_ge(s_ost, 16 * (NT + 1))
                pool.wait_ge(s_su, now(NT - 1, HA))
                pool.dma_start(io["ssm_prompt"].rearrange("a b h k v -> k (a b h) v"), k["state"][:]).then_inc(s_fin, 16)
                pool.dma_start(io["swa_v_prompt"].rearrange("a b w g d -> (a b w) (g d)"), vt[:, 1, :]).then_inc(s_fin, 16)
                pool.wait_ge(s_fin0, 1)
                pool.dma_start(io["swa_k_prompt"].rearrange("a b w g d -> (a b w) (g d)"), kl[:]).then_inc(s_fin, 16)
                pool.wait_ge(s_fin, 48)
        m.clear_sems()


def sample_mixer(nc, io, k):
    with ExitStack() as ctx:
        m = Mem(nc, ctx)
        F = Front(m, "s_", TS, 2)
        L = F.levels
        cv = m.sb("s_conv", [P, CC, NB, NS])
        tp = m.sb("s_tap", [P, CC, NB, NS])
        zt = m.sb("s_z_tanh", [P, HA, TS])
        zs = m.sb("s_z_silu", [P, HA, TS])
        th, beta, xa, ax, na, gg, gc0, gcx, negc, dk = (m.sb("s_" + x, [TS, HA]) for x in (
            "beta_tanh", "beta", "a_biased", "a_abs", "a_neg", "g", "gc", "gc_exp", "gc_neg", "g_to_last"))
        ea = m.sb("s_decay_rate", [TS, HA])
        gt = m.sb("s_g_total", [TS, HA])
        gl = m.sb("s_g_last_exp", [P, HA, NB])
        tab = m.sb("s_factor_table", [TS, 6, HA])
        s0 = m.sb("s_state", [P, NB, HA, P])
        kgm = m.sb("s_kg_of_batch", [TS, NB, HA, P])
        vnT = m.sb("s_v_newT", [P, HA, TS])
        vn = m.sb("s_v_new", [TS, HA, P])
        oT = m.sb("s_oT", [P, HA, TS])
        osq = m.sb("s_o_squares", [TS, HA, P])
        oss, oms, ors = (m.sb("s_" + x, [TS, HA]) for x in ("o_sumsq", "o_meansq", "o_rrms"))
        on = m.sb("s_o_normed", [TS, HA, P])
        kc, vc = m.sb("s_cache_k", [P, NB, P]), m.sb("s_cache_v", [P, NB, P])
        kcT = m.sb("s_kT", [P, NB, W + NS])
        vnew = m.sb("s_v_rows", [NS, NB, P])
        qS = m.sb("s_q_heads", [P, 4, TS])
        qB = m.sb("s_q_rows", [P, NB, NS, 4])
        sc = m.sb("s_scores", [16, NB, 2, W + NS])
        mx, nm, esk, dn, rc = (m.sb("s_" + x, [16, NB, 2]) for x in ("max", "max_sink", "sink_exp", "prob_sum", "recip"))
        pcT = m.sb("s_probsT", [P, NB, 2, 16])
        pnT = m.sb("s_probsT_new", [NS, NB, 2, 16])
        rows = m.sb("s_rows", [TS, CC + 2, P])
        ap = m.ps("s_attn_ps", [P, 4, 512])
        s_ld, s_st0, s_q = m.sem("s_cache_loaded"), m.sem("s_state_loaded"), m.sem("s_q_moved")
        s_pre, s_cv, s_act, s_pes = m.sem("s_tables_step"), m.sem("s_conv_step"), m.sem("s_act_step"), m.sem("s_cumsums_summed")
        s_zz, s_gl = m.sem("s_z_done"), m.sem("s_g_last_done")
        s_kgm, s_v, s_ve, s_vt, s_vn = (m.sem(x) for x in ("s_kg_masked", "s_v_newT_done", "s_v_newT_read", "s_v_new_turned", "s_v_new_read"))
        s_o, s_oe, s_ot, s_osq, s_oss, s_oms, s_ors, s_on, s_o2, s_oa = (m.sem(x) for x in (
            "s_oT_done", "s_oT_read", "s_o_turned", "s_o_squared", "s_o_sumsq_done", "s_o_meansq_done", "s_o_rrms_done",
            "s_o_normed_done", "s_o_turned_back", "s_o_out"))
        s_add, s_new = m.sem("s_state_added"), m.sem("s_state_new")
        s_rt, s_rr, s_kt, s_ke, s_qb = (m.sem(x) for x in ("s_rows_turned", "s_rows_read", "s_kT_turned", "s_kT_read", "s_q_placed"))
        s_sc, s_mk, s_sm, s_pt, s_pe2, s_av, s_ob = (m.sem(x) for x in (
            "s_scores_done", "s_scores_masked", "s_softmax_step", "s_probs_turned", "s_probs_read", "s_attn_done", "s_attn_out"))
        s_out, s_rcp = m.sem("s_stored"), m.sem("s_recip_done")
        with nc.Block() as block:
            @block.sync
            def _(sp):
                sp.dma_start(kc[:], io["cache_swa_k"].rearrange("a b w g d -> w (a b) (g d)")).then_inc(s_ld, 16)
                sp.dma_start(vc[:], io["cache_swa_v"].rearrange("a b w g d -> w (a b) (g d)")).then_inc(s_ld, 16)
                for h in range(HB):
                    sp.dma_start(qS[64 * (h // 4):64 * (h // 4) + 64, h % 4, :],
                                 k["projS"][64 * (h % 2):64 * (h % 2) + 64, 16 + h // 2, :]).then_inc(s_q, 16)
                sp.dma_start(s0[:], io["state_ssm"].rearrange("a b h k v -> k (a b) h v")).then_inc(s_st0, 16)
                for name, cache in (("swa_k_sample", "cache_swa_k"), ("swa_v_sample", "cache_swa_v")):
                    sp.dma_start(io[name].rearrange("a b w g d -> (a b) (w g d)")[:, 0:(W - NS) * P],
                                 io[cache].rearrange("a b w g d -> (a b) (w g d)")[:, NS * P:W * P]).then_inc(s_out, 16)
                sp.dma_start(io["conv_prompt"].rearrange("a b i (c p) -> (a b i c) p", p=P), k["xrow"][:]).then_inc(s_out, 16)
                sp.wait_ge(s_rr, 1)
                for b in range(NB):
                    sp.dma_start(io["conv_sample"][0, b], rows[NS * b + 1:NS * b + NS, 0:CC, :].rearrange("t c p -> t (c p)")
                                 ).then_inc(s_out, 16)
                    for j, name in enumerate(("swa_k_sample", "swa_v_sample")):
                        sp.dma_start(io[name].rearrange("a b w g d -> (a b) w (g d)")[b, W - NS:W],
                                     rows[NS * b:NS * b + NS, CC + j, :]).then_inc(s_out, 16)
                for b in range(NB):
                    sp.wait_ge(s_new, HA * (b + 1))
                    sp.dma_start(io["ssm_sample"].rearrange("a b h k v -> k (a b) h v")[:, b], s0[:, b]).then_inc(s_out, 16)
                sp.wait_ge(s_out, 16 * (3 + 3 * NB + NB))

            @block.tensor
            def _(pe):
                mm, tr, ident = nc.tensor.matmul, nc.tensor.transpose, k["ident"]
                for s in F.credits_pe():
                    pe.sem_inc(s, 1)
                for c in range(CC + 2):
                    src = k["projS"][:, c if c < CC else c + 8, :]
                    last = tr(ap[0:TS, c // 4, (c % 4) * P:(c % 4) * P + P], src, ident[:])
                last.then_inc(s_rt, 1)
                pe.wait_ge(s_pre, 6)
                mm(F.gp[0:TS, 0, 0:HA], k["uts"][:], gg[:], start=True, stop=True)
                mm(F.gp[0:TS, 0, HA:2 * HA], k["same"][:], gg[:], start=True, stop=True)
                for h in range(HA):
                    last = mm(F.gp[:, 1, h * NB:(h + 1) * NB], gg[:, h:h + 1].broadcast_to([TS, P]), k["seg"][:], start=True, stop=True)
                last.then_inc(s_pes, 1)
                pe.wait_ge(s_pre, 7)
                pe.wait_ge(s_gl, 1)
                turn, spread, back, gram, level0, level_y, level_z, w = front_pe(
                    nc, pe, F, k, 0, k["uts"][:], k["negs"][:], lambda: None, lambda: None,
                    lambda: (pe.wait_ge(F.s_sk, now(0)), pe.wait_ge(F.s_dec, now(0))))
                turn()
                spread()
                pe.wait_ge(s_ld, 32)
                pe.wait_ge(s_rr, 1)
                for b in range(NB):
                    tr(ap[:, b // 4, (b % 4) * P:(b % 4) * P + P], kc[:, b, :], ident[:])
                    last = tr(ap[0:NS, 2 + b // 4, (b % 4) * P:(b % 4) * P + P], k["projS"][:, 21, NS * b:NS * b + NS], ident[:])
                last.then_inc(s_kt, 1)
                back()
                gram()
                level0()
                for g in range(2):
                    level_y(1, g)
                for g in range(2):
                    level_z(1, g)
                w()
                for half in range(2):
                    if half == 0:
                        pe.wait_ge(s_ke, 1)
                        pe.wait_ge(s_qb, 1)
                    else:
                        pe.wait_ge(s_mk, 4)
                    for j in range(4):
                        b = 4 * half + j
                        for g in range(2):
                            at = slice(64 * g, 64 * g + 64)
                            o = (j % 2) * 256
                            last = mm(ap[0:16, 2 * (j // 2) + g, o:o + W + NS], qB[at, b].rearrange("p s c -> p (s c)"),
                                      kcT[at, b, :], start=True, stop=True)
                    last.then_inc(s_sc, 1)
                pe.wait_ge(F.s_nw, now(0))
                pe.wait_ge(s_st0, 16)
                for h in range(HA):
                    at = F.gp[:, 1, h * TS:(h + 1) * TS]
                    mm(at, F.vb[:, h, :], F.xx[:, 1, h, :], start=True, stop=False)
                    for b in range(NB):
                        last = mm(F.gp[:, 1, h * TS + NS * b:h * TS + NS * b + NS], s0[:, b, h, :],
                                  F.nwT[:, h, NS * b:NS * b + NS], start=False, stop=(b == NB - 1))
                last.then_inc(s_v, 1)
                pe.wait_ge(s_ve, 1)
                for h in range(HA):
                    last = tr(F.gp[0:TS, 2, h * P:(h + 1) * P], vnT[:, h, :], ident[:])
                last.then_inc(s_vt, 1)
                pe.wait_ge(s_vn, 1)
                for h in range(HA):
                    mm(F.gp[:, 3, h * TS:(h + 1) * TS], vn[:, h, :], F.al[:, h, 1, :], start=True, stop=False)
                    for b in range(NB):
                        last = mm(F.gp[:, 3, h * TS + NS * b:h * TS + NS * b + NS], s0[:, b, h, :],
                                  F.qgT[:, h, NS * b:NS * b + NS], start=False, stop=(b == NB - 1))
                last.then_inc(s_o, 1)
                pe.wait_ge(s_oe, 1)
                for h in range(HA):
                    last = tr(F.gp[0:TS, 0, h * P:(h + 1) * P], oT[:, h, :], ident[:])
                last.then_inc(s_ot, 1)
                pe.wait_ge(s_sm, 8)
                for b in range(NB):
                    for g in range(2):
                        o = (2 * b + g) * 16
                        tr(ap[:, 0, o:o + 16], sc[:, b, g, 0:W], ident[0:16, 0:16])
                        last = tr(ap[0:NS, 1, o:o + 16], sc[:, b, g, W:W + NS], ident[0:16, 0:16])
                last.then_inc(s_pt, 1)
                pe.wait_ge(s_pe2, 1)
                for b in range(NB):
                    for g in range(2):
                        at = ap[64 * g:64 * g + 64, 2, b * 16:b * 16 + 16]
                        mm(at, vc[:, b, 64 * g:64 * g + 64], pcT[:, b, g, :], start=True, stop=False)
                        last = mm(at, vnew[:, b, 64 * g:64 * g + 64], pnT[:, b, g, :], start=False, stop=True)
                last.then_inc(s_av, 1)
                pe.wait_ge(s_on, 1)
                for h in range(HA):
                    last = tr(F.gp[:, 1, h * TS:(h + 1) * TS], on[:, h, :], ident[0:TS, 0:TS])
                last.then_inc(s_o2, 1)
                pe.wait_ge(s_kgm, 1)
                pe.wait_ge(s_ob, 1)
                for b in range(NB):
                    if b >= 4:
                        pe.wait_ge(s_new, HA * (b - 3))
                    for h in range(HA):
                        last = mm(ap[:, b % 4, h * P:(h + 1) * P], kgm[:, b, h, :], vn[:, h, :], start=True, stop=True)
                    last.then_inc(s_add, 1)

            @block.scalar
            def _(act):
                a = nc.scalar
                for s in F.credits_act():
                    act.sem_inc(s, 1)
                a.activation(th[:], k["ba_s"][:, 0:HA], ACT.Tanh, scale=0.5).then_inc(s_act, 1)
                a.activation(zt[:], k["projS"][:, 12:16, :], ACT.Tanh).then_inc(s_zz, 1)
                a.activation(ea[:], k["alog"][0:TS, :], ACT.Exp).then_inc(s_act, 1)
                act.wait_ge(s_pre, 3)
                a.activation(ax[:], ax[:], ACT.Exp, scale=-1.0).then_inc(s_act, 1)
                act.wait_ge(s_act, 3)
                a.activation(ax[:], ax[:], ACT.Ln, bias=1.0).then_inc(s_act, 1)
                act.wait_ge(s_cv, 7)
                a.activation(tp[:], cv[:], ACT.Tanh).then_inc(s_act, 1)
                act.wait_ge(s_rt, 1)
                a.copy(rows[:].rearrange("p c d -> p (c d)")[:, 0:1024], ap[0:TS, 0:2, :].rearrange("p b c -> p (b c)"))
                a.copy(rows[:].rearrange("p c d -> p (c d)")[:, 1024:14 * P], ap[0:TS, 2:4, :].rearrange("p b c -> p (b c)")[:, 0:768]
                       ).then_inc(s_rr, 1)
                act.wait_ge(s_pre, 8)
                a.activation(gcx[:], gc0[:], ACT.Exp)
                a.activation(dk[:], dk[:], ACT.Exp).then_inc(s_act, 1)
                a.activation(gl[:].rearrange("p h b -> p (h b)"), F.gp[:, 1, 0:HA * NB], ACT.Exp).then_inc(s_gl, 1)
                square, decay, read_back, read_y, read_w = front_act(
                    nc, act, F, 0, lambda h: negc[:, h:h + 1], lambda: None, lambda: None, lambda: None)
                square()
                decay()
                act.wait_ge(s_kt, 1)
                a.copy(kcT[:, :, 0:W], ap[:, 0:2, :].rearrange("p b (c w) -> p (b c) w", w=P))
                a.copy(vnew[:].rearrange("p b d -> p (b d)"), ap[0:NS, 2:4, :].rearrange("p b c -> p (b c)")).then_inc(s_ke, 1)
                read_back()
                for half in range(2):
                    read_y(1, half)
                read_w()
                act.wait_ge(s_v, 1)
                a.copy(vnT[:].rearrange("p h i -> p (h i)"), F.gp[:, 1, 0:P]).then_inc(s_ve, 1)
                act.wait_ge(s_vt, 1)
                a.copy(vn[:].rearrange("p h d -> p (h d)"), F.gp[0:TS, 2, :]).then_inc(s_vn, 1)
                act.wait_ge(s_sm, 4)
                a.activation(sc[:], sc[:], ACT.Exp)
                a.activation(esk[:], esk[:], ACT.Exp).then_inc(s_sm, 1)
                act.wait_ge(s_o, 1)
                a.copy(oT[:].rearrange("p h i -> p (h i)"), F.gp[:, 3, 0:P]).then_inc(s_oe, 1)
                act.wait_ge(s_ot, 1)
                a.activation(osq[:].rearrange("p h d -> p (h d)"), F.gp[0:TS, 0, :], ACT.Square).then_inc(s_osq, 1)
                act.wait_ge(s_pt, 1)
                a.copy(pcT[:].rearrange("p b g r -> p (b g r)"), ap[:, 0, 0:256])
                a.copy(pnT[:].rearrange("p b g r -> p (b g r)"), ap[0:NS, 1, 0:256]).then_inc(s_pe2, 1)

            @block.vector
            def _(dve):
                v = nc.vector
                wide = lambda x, d: x.unsqueeze(len(x.shape)).broadcast_to(list(x.shape) + [d])
                for s in F.credits_dve():
                    dve.sem_inc(s, 1)
                v.tensor_tensor(xa[:], k["ba_s"][:, HA:2 * HA], k["dtb"][0:TS, :], ALU.add).then_inc(s_pre, 1)
                dve.wait_ge(s_pre, 1)
                v.tensor_scalar(na[:], xa[:], -1.0, None, ALU.mult).then_inc(s_pre, 1)
                dve.wait_ge(s_pre, 2)
                v.tensor_tensor(ax[:], xa[:], na[:], ALU.max).then_inc(s_pre, 1)
                dve.wait_ge(s_act, 4)
                v.scalar_tensor_tensor(xa[:], xa[:], 0.0, ax[:], ALU.max, ALU.add).then_inc(s_pre, 1)
                dve.wait_ge(s_pre, 4)
                v.tensor_scalar(xa[:], xa[:], -1.0, None, ALU.mult).then_inc(s_pre, 1)
                dve.wait_ge(s_pre, 5)
                v.tensor_tensor(gg[:], xa[:], ea[:], ALU.mult).then_inc(s_pre, 1)
                v.tensor_copy(k["xs_pad"][:, :, :, CW - 1:], k["projS"][:, 0:CC, :].rearrange("p c (b s) -> p c b s", s=NS)
                              ).then_inc(s_cv, 1)
                dve.wait_ge(s_cv, 1)
                tap = lambda i: k["taps"][:, i * CC:(i + 1) * CC].unsqueeze(2).unsqueeze(3).broadcast_to([P, CC, NB, NS])
                step = 1
                v.tensor_tensor(cv[:], k["xs_pad"][:, :, :, 0:NS], tap(0), ALU.mult)
                for i in range(1, CW):
                    if i > 1:
                        dve.wait_ge(s_cv, step)
                    v.tensor_tensor(tp[:], k["xs_pad"][:, :, :, i:i + NS], tap(i), ALU.mult).then_inc(s_cv, 1)
                    step += 1
                    dve.wait_ge(s_cv, step)
                    v.tensor_tensor(cv[:], cv[:], tp[:], ALU.add).then_inc(s_cv, 1)
                    step += 1
                dve.wait_ge(s_act, 5)
                v.scalar_tensor_tensor(F.qkv[:].rearrange("p c t -> p (c t)"), tp[:].rearrange("p c b s -> p (c b s)"), 1.0,
                                       cv[:].rearrange("p c b s -> p (c b s)"), ALU.add, ALU.mult).then_inc(F.s_in, 32)
                dve.wait_ge(s_zz, 1)
                v.scalar_tensor_tensor(zs[:].rearrange("p h t -> p (h t)"), zt[:].rearrange("p h t -> p (h t)"), 1.0,
                                       k["projS"][:, 12:16, :].rearrange("p h t -> p (h t)"), ALU.add, ALU.mult).then_inc(s_zz, 1)
                dve.wait_ge(s_pes, 1)
                v.tensor_copy(gc0[:], F.gp[0:TS, 0, 0:HA])
                v.tensor_copy(gt[:], F.gp[0:TS, 0, HA:2 * HA]).then_inc(s_pre, 1)
                dve.wait_ge(s_pre, 7)
                v.tensor_scalar(negc[:], gc0[:], -1.0, None, ALU.mult)
                v.tensor_tensor(dk[:], gt[:], gc0[:], ALU.subtract).then_inc(s_pre, 1)
                v.tensor_scalar(beta[:], th[:], 0.5, 0.5, ALU.mult, ALU.add).then_inc(s_pre, 1)
                scale = float(P) ** -0.5
                v.memset(tab[:, 0, :], scale)
                v.memset(tab[:, 2, :], 1.0)
                dve.wait_ge(s_act, 6)
                dve.wait_ge(s_pre, 9)
                v.tensor_scalar(tab[:, 1, :], gcx[:], scale, None, ALU.mult)
                v.tensor_copy(tab[:, 3, :], beta[:])
                v.tensor_tensor(tab[:, 4, :], beta[:], gcx[:], ALU.mult)
                v.tensor_copy(tab[:, 5, :], dk[:]).then_inc(s_pre, 1)
                dve.wait_ge(s_pre, 10)
                norms, scale_, scale_rest, decayed, start_x, step_x = front_dve(
                    nc, dve, F, k, 0, lambda lo, hi: tab[:, lo:hi, :], wide(beta[:], P), lambda: None, lambda: None)
                norms()
                v.tensor_copy(kcT[:, :, W:W + NS], k["projS"][:, 20, :].rearrange("p (b s) -> p b s", s=NS))
                dve.wait_ge(s_q, 16 * HB)
                v.tensor_copy(qB[:], qS[:].rearrange("p c (b s) -> p b s c", s=NS)).then_inc(s_qb, 1)
                scale_()
                scale_rest()
                decayed()
                start_x()
                for half in range(2):
                    step_x(1, half)
                dve.wait_ge(F.s_sk, now(0))
                v.tensor_tensor(kgm[:].rearrange("t b h d -> t b (h d)"),
                                F.kk[:, 3].rearrange("t h d -> t (h d)").unsqueeze(1).broadcast_to([TS, NB, HA * P]),
                                wide(k["seg"][:], HA * P), ALU.mult).then_inc(s_kgm, 1)
                for half in range(2):
                    dve.wait_ge(s_sc, half + 1)
                    for bank in range(4):
                        j, g = bank // 2, bank % 2
                        b = 4 * half + 2 * j
                        v.scalar_tensor_tensor(sc[:, b:b + 2, g, :], ap[0:16, bank, :].rearrange("p (e q) -> p e q", e=2)[:, :, 0:W + NS],
                                               float(DB) ** -0.5, k["masks"][:].unsqueeze(1).broadcast_to([16, 2, W + NS]),
                                               ALU.mult, ALU.add).then_inc(s_mk, 1)
                dve.wait_ge(s_mk, 8)
                v.tensor_reduce(mx[:], sc[:], AX.X, ALU.max).then_inc(s_sm, 1)
                dve.wait_ge(s_sm, 1)
                sink = k["sink_s"][:].unsqueeze(1).broadcast_to([16, NB, 2])
                v.tensor_tensor(nm[:], mx[:], sink, ALU.max).then_inc(s_sm, 1)
                dve.wait_ge(s_sm, 2)
                v.tensor_tensor(esk[:], sink, nm[:], ALU.subtract).then_inc(s_sm, 1)
                v.tensor_tensor(sc[:], sc[:], wide(nm[:], W + NS), ALU.subtract).then_inc(s_sm, 1)
                dve.wait_ge(s_sm, 5)
                v.tensor_reduce(dn[:], sc[:], AX.X, ALU.add).then_inc(s_sm, 1)
                dve.wait_ge(s_sm, 6)
                v.tensor_tensor(dn[:], dn[:], esk[:], ALU.add).then_inc(s_sm, 1)
                dve.wait_ge(s_sm, 7)
                v.reciprocal(rc[:], dn[:]).then_inc(s_rcp, 1)
                dve.wait_ge(s_rcp, 1)
                v.tensor_tensor(sc[:], sc[:], wide(rc[:], W + NS), ALU.mult).then_inc(s_sm, 1)
                dve.wait_ge(s_osq, 1)
                v.tensor_reduce(oss[:], osq[:], AX.X, ALU.add).then_inc(s_oss, 1)
                dve.wait_ge(s_oss, 1)
                v.tensor_scalar(oms[:], oss[:], 1.0 / P, EPS, ALU.mult, ALU.add).then_inc(s_oms, 1)
                dve.wait_ge(s_ors, 1)
                v.tensor_tensor(on[:], F.gp[0:TS, 0, :].rearrange("p (h d) -> p h d", h=HA), wide(ors[:], P), ALU.mult).then_inc(s_on, 1)
                dve.wait_ge(s_av, 1)
                v.tensor_copy(k["oS"][:, 4:8, :].rearrange("p c (b s) -> p c b s", s=NS),
                              ap[:, 2, 0:P].rearrange("p (b s c) -> p c b s", b=NB, s=NS)).then_inc(s_ob, 1)
                dve.wait_ge(s_o2, 1)
                dve.wait_ge(s_zz, 2)
                v.scalar_tensor_tensor(k["oS"][:, 0:4, :].rearrange("p h t -> p (h t)"), F.gp[:, 1, 0:P], k["vcol"][:, V_GDN:V_GDN + 1],
                                       zs[:].rearrange("p h t -> p (h t)"), ALU.mult, ALU.mult).then_inc(s_oa, 1)
                for b in range(NB):
                    dve.wait_ge(s_add, b + 1)
                    for h in range(HA):
                        v.scalar_tensor_tensor(s0[:, b, h, :], s0[:, b, h, :], gl[:, h, b:b + 1], ap[:, b % 4, h * P:(h + 1) * P],
                                               ALU.mult, ALU.add).then_inc(s_new, 1)

            @block.gpsimd
            def _(pool):
                g = nc.gpsimd
                for s in (F.s_g, F.s_rs, F.s_c):
                    pool.sem_inc(s, 1)
                pool.wait_ge(s_pre, 6)
                place, rsqrt, cut = front_pool(nc, pool, F, k, 0, gg[:], lambda lv: k["lev"][0:TS, lv, 0:TS])
                place()
                rsqrt()
                cut()
                pool.wait_ge(s_oms, 1)
                g.tensor_tensor(ors[:], oms[:], k["nhalf"][0:TS, 0:HA], ALU.pow).then_inc(s_ors, 1)
        m.clear_sems()


def spread_gate(nc, pe, k, which, rows, at, sample, out):
    for c in range(KD):
        o = out[at:at + rows, c // 4, (c % 4) * P:(c % 4) * P + P]
        if sample:
            last = nc.tensor.matmul(o, k["gate_col_s"][:, which, c].rearrange("p b s -> p (b s)"), k["ident"][:],
                                    start=True, stop=True)
        else:
            last = nc.tensor.matmul(o, k["gate_col"][:, which, c:c + 1].broadcast_to([P, P]), k["ident"][:], start=True, stop=True)
    return last


def out_projection(nc, io, k):
    with ExitStack() as ctx:
        m = Mem(nc, ctx)
        wr = k["w_o_raw"]
        whi = m.sb("w_o_hi", [P, KD, D], FR)
        wlo = m.sb("w_o_lo", [P, KD, D], FR)
        gate = m.sb("gate_rows", [P, 2, 512])
        gate_s = m.sb("gate_rows_s", [TS, 2, 512])
        ot = m.sb("mixed_T", [P, 2, KD, P])
        ohi = m.sb("mixed_hi", [P, 2, KD, P], FR)
        olo = m.sb("mixed_lo", [P, 2, KD, P], FR)
        xt = m.sb("x_in", [P, 2, D])
        x1 = m.sb("x_mid", [P, 2, D])
        xn = m.sb("x_mid_normed", [P, 2, D])
        sq = m.sb("out_squares", [P, D])
        h2 = m.sb("h2_tile", [P, 2, KD, P])
        sm = m.sb("out_scalars", [P, 2, 2, 4])
        po = m.ps("out_ps", [P, 2, 2, 512])
        pt = m.ps("turn_ps", [P, 2, 2, 512])
        s_w, s_wh, s_wl = k["w_o_loaded"], m.sem("w_o_hi_split"), m.sem("w_o_lo_split")
        s_gt, s_gr = m.sem("gates_spread"), m.sem("gates_read")
        s_o = [m.sem(f"mixed_loaded_{p}") for p in range(2)]
        s_x = [m.sem(f"x_in_loaded_{p}") for p in range(2)]
        s_x1s = [m.sem(f"x_mid_stored_{p}") for p in range(2)]
        s_h2s = [m.sem(f"h2_stored_{p}") for p in range(2)]
        s_oh, s_ol, s_mm = m.sem("mixed_hi_split"), m.sem("mixed_lo_split"), m.sem("out_summed")
        s_sa, s_ma, s_ra, s_t, s_x1 = (m.sem(x) for x in ("mix_sumsq", "mix_meansq", "mix_rrms", "mix_gated", "x_mid_done"))
        s_sb, s_mb, s_rb, s_xn = (m.sem(x) for x in ("mid_sumsq", "mid_meansq", "mid_rrms", "mid_normed"))
        s_tr, s_ht, s_h2 = m.sem("mid_turned"), m.sem("h2_scaled"), m.sem("h2_done")
        h2T = io["h2T"]

        def skeleton(eng, pre, post):
            pre(0, 0, 0)
            with eng.Fori(0, NT // 2 - 1) as i:
                pre(i * 2 + 1, 1, i)
                post(i * 2, 0, i)
                pre(i * 2 + 2, 0, i + 1)
                post(i * 2 + 1, 1, i)
            last = NT // 2 - 1
            pre(NT - 1, 1, last)
            post(NT - 2, 0, last)
            pre(NT, 0, last + 1)
            post(NT - 1, 1, last)
            post(NT, 0, last + 1)

        is_sample = lambda t: isinstance(t, int) and t == NT
        rows = lambda t: TS if is_sample(t) else P
        with nc.Block() as block:
            @block.sync
            def _(sp):
                for p in range(2):
                    sp.sem_inc(s_x1s[p], 16)
                    sp.sem_inc(s_h2s[p], 16)

                def load(t, p, u):
                    sp.wait_ge(s_ol, t + 1)
                    if not is_sample(t):
                        sp.dma_start(ot[:, p], io["oT"][:, :, bass.ds(t * P, P)].rearrange("c p t -> p c t")).then_inc(s_o[p], 16)
                    sp.wait_ge(s_x1, t + 1)
                    src = io["xs"] if is_sample(t) else io["x"][bass.ds(t * P, P), :]
                    sp.dma_start(xt[0:rows(t), p], src).then_inc(s_x[p], 16)

                def store(t, p, u):
                    n = rows(t)
                    sp.wait_ge(s_x1, t + 3)
                    sp.dma_start(io["x1"][bass.ds(t * P, n), :], x1[0:n, p]).then_inc(s_x1s[p], 16)
                    sp.wait_ge(s_h2, t + 3)
                    sp.dma_start(h2T[bass.ds(t, 1), :, :, 0:n].rearrange("a p c t -> (a p) c t"), h2[:, p, :, 0:n]).then_inc(s_h2s[p], 16)

                load(0, 0, 0)
                load(1, 1, 0)
                with sp.Fori(0, NT // 2 - 1) as i:
                    for p in range(2):
                        load(i * 2 + p + 2, p, i + 1)
                        store(i * 2 + p, p, i)
                load(NT, 0, NT // 2)
                store(NT - 2, 0, NT // 2 - 1)
                store(NT - 1, 1, NT // 2 - 1)
                store(NT, 0, NT // 2)
                for p in range(2):
                    n = (NT // 2 + 1 + (p == 0)) * 16
                    sp.wait_ge(s_x1s[p], n)
                    sp.wait_ge(s_h2s[p], n)

            @block.tensor
            def _(pe):
                for s in (s_mm, s_tr):
                    pe.sem_inc(s, 2)
                spread_gate(nc, pe, k, 0, P, 0, False, pt[:, 0]).then_inc(s_gt, 1)
                spread_gate(nc, pe, k, 0, TS, 0, True, pt[:, 1]).then_inc(s_gt, 1)

                def pre(t, p, u):
                    if isinstance(t, int) and t == 0:
                        pe.wait_ge(s_wl, KD)
                        pe.wait_ge(s_gr, 2)
                    pe.wait_ge(s_oh, t + 3)
                    pe.wait_ge(s_ol, t + 3)
                    pe.wait_ge(s_t, t + 1)
                    for kk in range(KD):
                        for h in range(2):
                            at = slice(h * 512, (h + 1) * 512)
                            last = three_pass(nc, po[:, p, h, :], ohi[:, p, kk, :], olo[:, p, kk, :],
                                              whi[:, kk, at], wlo[:, kk, at], kk == 0, kk == KD - 1)
                    last.then_inc(s_mm, 1)

                def post(t, p, u):
                    n = rows(t)
                    pe.wait_ge(s_xn, t + 3)
                    pe.wait_ge(s_ht, t + 1)
                    for c in range(KD):
                        last = nc.tensor.transpose(pt[:, p, c // 4, (c % 4) * P:(c % 4) * P + n], xn[0:n, p, c * P:(c + 1) * P],
                                                   k["ident"][0:n, 0:n])
                    last.then_inc(s_tr, 1)
                skeleton(pe, pre, post)

            @block.scalar
            def _(act):
                a = nc.scalar
                for s in (s_oh, s_sa, s_sb, s_xn):
                    act.sem_inc(s, 2)
                act.wait_ge(s_w, 2 * KD * 16)
                for c in range(KD):
                    a.copy(whi[:, c], wr[:, c]).then_inc(s_wh, 1)
                act.wait_ge(s_gt, 1)
                a.copy(gate[:], pt[:, 0]).then_inc(s_gr, 1)
                act.wait_ge(s_gt, 2)
                a.copy(gate_s[:], pt[0:TS, 1]).then_inc(s_gr, 1)

                def pre(t, p, u):
                    act.wait_ge(s_mm, t + 1)
                    if is_sample(t):
                        a.copy(ohi[:, p, :, 0:TS], k["oS"][:]).then_inc(s_oh, 1)
                    else:
                        act.wait_ge(s_o[p], u * 16 + 16)
                        a.copy(ohi[:, p], ot[:, p]).then_inc(s_oh, 1)

                def ahead(t, p, u):
                    if not isinstance(t, int) or t + 2 <= NT:
                        pre(t + 2, p, u + 1)

                def post(t, p, u):
                    n = rows(t)
                    act.wait_ge(s_mm, t + 3)
                    act.wait_ge(s_sb, t + 2)
                    a.activation(sq[0:n].rearrange("p (b c) -> p b c", b=2), po[0:n, p], ACT.Square, accum_out=sm[0:n, p, 0, 0:1]
                                 ).then_inc(s_sa, 1)
                    ahead(t, p, u)
                    act.wait_ge(s_x1, t + 3)
                    act.wait_ge(s_sa, t + 3)
                    a.activation(sq[0:n], x1[0:n, p], ACT.Square, accum_out=sm[0:n, p, 1, 0:1]).then_inc(s_sb, 1)
                    act.wait_ge(s_rb, t + 1)
                    act.wait_ge(s_tr, t + 1)
                    a.mul(xn[0:n, p], x1[0:n, p], sm[0:n, p, 1, 2:3]).then_inc(s_xn, 1)
                pre(0, 0, 0)
                pre(1, 1, 0)
                skeleton(act, lambda *_: None, post)

            @block.gpsimd
            def _(pool):
                g = nc.gpsimd

                def rrms(t, p, norm, ready, done):
                    n = rows(t)
                    pool.wait_ge(ready, t + 3)
                    g.tensor_tensor(sm[0:n, p, norm, 2:3], sm[0:n, p, norm, 1:2], k["nhalf"][0:n, 0:1], ALU.pow).then_inc(done, 1)

                def post(t, p, u):
                    rrms(t, p, 0, s_ma, s_ra)
                    rrms(t, p, 1, s_mb, s_rb)
                skeleton(pool, lambda t, p, u: None, post)

            @block.vector
            def _(dve):
                v = nc.vector
                for s in (s_ol, s_ma, s_t, s_x1, s_mb, s_ht, s_h2):
                    dve.sem_inc(s, 2)
                for c in range(KD):
                    dve.wait_ge(s_wh, c + 1)
                    v.tensor_tensor(wlo[:, c], wr[:, c], whi[:, c].bitcast(F32), ALU.subtract).then_inc(s_wl, 1)

                def pre(t, p, u):
                    dve.wait_ge(s_oh, t + 3)
                    if is_sample(t):
                        v.tensor_tensor(olo[:, p, :, 0:TS], k["oS"][:], ohi[:, p, :, 0:TS].bitcast(F32), ALU.subtract).then_inc(s_ol, 1)
                    else:
                        v.tensor_tensor(olo[:, p], ot[:, p], ohi[:, p].bitcast(F32), ALU.subtract).then_inc(s_ol, 1)

                def ahead(t, p, u):
                    if not isinstance(t, int) or t + 2 <= NT:
                        pre(t + 2, p, u + 1)

                def post(t, p, u):
                    n = rows(t)
                    gr = gate_s if is_sample(t) else gate
                    dve.wait_ge(s_sa, t + 3)
                    v.tensor_scalar(sm[0:n, p, 0, 1:2], sm[0:n, p, 0, 0:1], 1.0 / D, EPS, ALU.mult, ALU.add).then_inc(s_ma, 1)
                    dve.wait_ge(s_ra, t + 1)
                    dve.wait_ge(s_x1s[p], u * 16 + 16)
                    x1v = x1[0:n, p].rearrange("p (b c) -> p b c", b=2)
                    v.scalar_tensor_tensor(x1v, po[0:n, p], sm[0:n, p, 0, 2:3], gr[0:n], ALU.mult, ALU.mult).then_inc(s_t, 1)
                    dve.wait_ge(s_t, t + 3)
                    dve.wait_ge(s_x[p], u * 16 + 16)
                    v.tensor_tensor(x1[0:n, p], x1[0:n, p], xt[0:n, p], ALU.add).then_inc(s_x1, 1)
                    dve.wait_ge(s_sb, t + 3)
                    v.tensor_scalar(sm[0:n, p, 1, 1:2], sm[0:n, p, 1, 0:1], 1.0 / D, EPS, ALU.mult, ALU.add).then_inc(s_mb, 1)
                    ahead(t, p, u)
                    dve.wait_ge(s_tr, t + 3)
                    dve.wait_ge(s_h2s[p], u * 16 + 16)
                    if is_sample(t):
                        src = pt[:, p].rearrange("p a (b q) -> p (a b) q", q=P)[:, :, 0:TS].rearrange("p c (b s) -> p c b s", s=NS)
                        dst = h2[:, p, :, 0:TS].rearrange("p c (b s) -> p c b s", s=NS)
                        spread = lambda x: x[:, 1, :, 1:9].unsqueeze(3).broadcast_to([P, KD, NB, NS])
                        scale, shift = spread(k["mscale"]), spread(k["mshift"])
                    else:
                        src = pt[:, p].rearrange("p a (b q) -> p (a b) q", q=P)
                        dst = h2[:, p]
                        scale, shift = (k[x][:, 1].unsqueeze(2).broadcast_to([P, KD, P]) for x in ("pscale", "pshift"))
                    v.tensor_tensor(dst, src, scale, ALU.mult).then_inc(s_ht, 1)
                    dve.wait_ge(s_ht, t + 3)
                    v.tensor_tensor(dst, dst, shift, ALU.add).then_inc(s_h2, 1)
                pre(0, 0, 0)
                pre(1, 1, 0)
                skeleton(dve, lambda *_: None, post)
        m.clear_sems()


def mlp(nc, io, k, half):
    with ExitStack() as ctx:
        m = Mem(nc, ctx)
        tiles = NT // 2 + (1 if half == 0 else 0)
        n = NT // 2 * P + (TS if half == 0 else 0)
        Q = 4
        qn = n // Q
        NG = FF // P // 2
        last0 = n - P
        tag = f"h{half}_"
        hhi, hlo = (m.sb(tag + x, [P, KD, n], FR) for x in ("h2_hi", "h2_lo"))
        ru = m.sb(tag + "relu", [P, 2, n])
        uhi, ulo = (m.sb(tag + x, [P, 2, 2, n], FR) for x in ("u_hi", "u_lo"))
        y = m.sb(tag + "y", [P, tiles, D])
        ur = m.sb(tag + "w_up_raw", [P, 2, KD, P])
        uwh, uwl = (m.sb(tag + x, [P, 2, KD, P], FR) for x in ("w_up_hi", "w_up_lo"))
        dr = m.sb(tag + "w_down_raw", [P, 2, D])
        dwh, dwl = (m.sb(tag + x, [P, 2, D], FR) for x in ("w_down_hi", "w_down_lo"))
        gate = m.sb(tag + "gate_rows", [P, 2, 512])
        gate_s = m.sb(tag + "gate_rows_s", [P, 2, 512]) if half == 0 else None
        ss, ms, rr = (m.sb(tag + x, [P, tiles]) for x in ("y_sumsq", "y_meansq", "y_rrms"))
        pu = m.ps(tag + "up_ps", [P, Q, 512])
        pd = m.ps(tag + "down_ps", [P, 2, 2, 512])
        sem = lambda x: m.sem(tag + x)
        s_h = [sem(f"h2_loaded_{q}") for q in range(2)]
        s_hh, s_hl = sem("h2_hi_split"), sem("h2_lo_split")
        s_ur = [sem(f"w_up_loaded_{q}") for q in range(2)]
        s_dr = [sem(f"w_down_loaded_{q}") for q in range(2)]
        s_uwh, s_uwl, s_dwh, s_dwl = (sem(x) for x in ("w_up_hi_split", "w_up_lo_split", "w_down_hi_split", "w_down_lo_split"))
        s_up, s_re, s_u, s_uh, s_ul = (sem(x) for x in ("up_summed", "relu_done", "squared", "u_hi_split", "u_lo_split"))
        s_dn, s_y, s_y0 = sem("down_summed"), sem("y_added"), sem("y_cleared")
        s_gt, s_gr = sem("gates_spread"), sem("gates_read")
        s_ss, s_ms, s_rr, s_yg, s_yo = (sem(x) for x in ("y_sumsq_done", "y_meansq_done", "y_rrms_done", "y_gated", "y_out"))
        s_x = [sem(f"x_mid_loaded_{q}") for q in range(2)]
        s_st = sem("y_stored")

        def skeleton(eng, up, down, split_down):
            up(0, 0, 0)
            with eng.Fori(0, NG // 2 - 1) as i:
                split_down(i * 2)
                up(i * 2 + 1, 1, i)
                down(i * 2, 0, i)
                split_down(i * 2 + 1)
                up(i * 2 + 2, 0, i + 1)
                down(i * 2 + 1, 1, i)
            split_down(NG - 2)
            up(NG - 1, 1, NG // 2 - 1)
            down(NG - 2, 0, NG // 2 - 1)
            split_down(NG - 1)
            down(NG - 1, 1, NG // 2 - 1)

        nothing = lambda *_: None
        def place(t):
            if half == 0 and t == tiles - 1:
                return slice(P - TS, P), slice(T, T + TS)
            return slice(0, P), slice((half * 8 + t) * P, (half * 8 + t + 1) * P)

        with nc.Block() as block:
            @block.sync
            def _(sp):
                def finish(sp, t):
                    r, rows = place(t)
                    sp.wait_ge(s_yo, t + 1)
                    dst = io["ys"] if rows.start == T else io["y"][rows, :]
                    sp.dma_start(dst, y[r, t]).then_inc(s_st, 16)

                def h_slice(kk):
                    q = kk % 2
                    if kk >= 2:
                        sp.wait_ge(s_hl, kk - 1)
                    sp.dma_start(ru[:, q, 0:NT // 2 * P].rearrange("p (t n) -> p t n", n=P),
                                 io["h2T"][half * NT // 2:(half + 1) * NT // 2, :, kk, :].rearrange("t p n -> p t n")).then_inc(s_h[q], 16)
                    if half == 0:
                        sp.dma_start(ru[:, q, NT // 2 * P:n], io["h2T"][NT, :, kk, 0:TS]).then_inc(s_h[q], 16)

                def load_up(f, c):
                    sp.wait_ge(s_uwl, f + 1)
                    sp.dma_start(ur[:, c], io["w_up"][:, bass.ds(f * P, P)].rearrange("(k p) n -> p k n", p=P)).then_inc(s_ur[c], 16)

                def load_down(G):
                    for c in range(2):
                        sp.wait_ge(s_dwl, G * 2 + c + 1)
                        sp.dma_start(dr[:, c], io["w_down"][bass.ds((G * 2 + c) * P, P), :]).then_inc(s_dr[c], 16)
                for c in range(2):
                    load_up(c, c)
                for kk in range(KD):
                    h_slice(kk)
                with sp.Fori(0, NG - 1) as G:
                    load_down(G)
                    for c in range(2):
                        load_up(G * 2 + (c + 2), c)
                load_down(NG - 1)
                for c in range(2):
                    sp.wait_ge(s_uwl, 2 * NG + c + 1)
                    sp.dma_start(ur[:, c], io["w_up"][:, c * P:(c + 1) * P].rearrange("(k p) n -> p k n", p=P)).then_inc(s_ur[c], 16)
                for t in range(tiles):
                    r, rows = place(t)
                    sp.wait_ge(s_dwl, 2 * NG + 2)
                    if t >= 2:
                        sp.wait_ge(s_yo, t - 1)
                    sp.dma_start(dr[r, t % 2], io["x1"][rows, :]).then_inc(s_x[t % 2], 16)
                    if t >= 1:
                        finish(sp, t - 1)
                finish(sp, tiles - 1)
                sp.wait_ge(s_st, 16 * tiles)

            @block.tensor
            def _(pe):
                pe.sem_inc(s_dn, tiles + 1)
                spread_gate(nc, pe, k, 1, P, 0, False, pd[:, 0]).then_inc(s_gt, 1)
                if half == 0:
                    spread_gate(nc, pe, k, 1, TS, P - TS, True, pd[:, 1]).then_inc(s_gt, 1)

                def up(G, par, i):
                    for c in range(2):
                        f = G * 2 + c
                        pe.wait_ge(s_uwh, f + 1)
                        pe.wait_ge(s_uwl, f + 3)
                        if isinstance(G, int) and f == 0:
                            for kk in range(KD):
                                pe.wait_ge(s_hh, kk + 1)
                                pe.wait_ge(s_hl, kk + 1)
                                for j in range(Q):
                                    at = slice(j * qn, (j + 1) * qn)
                                    last = three_pass(nc, pu[:, j, 0:qn], uwh[:, c, kk, :], uwl[:, c, kk, :],
                                                      hhi[:, kk, at], hlo[:, kk, at], kk == 0, kk == KD - 1)
                                    if kk == KD - 1:
                                        last.then_inc(s_up, 1)
                            continue
                        for j in range(Q):
                            pe.wait_ge(s_re, f * Q + j + 1)
                            at = slice(j * qn, (j + 1) * qn)
                            for kk in range(KD):
                                last = three_pass(nc, pu[:, j, 0:qn], uwh[:, c, kk, :], uwl[:, c, kk, :],
                                                  hhi[:, kk, at], hlo[:, kk, at], kk == 0, kk == KD - 1)
                            last.then_inc(s_up, 1)

                def down(G, par, i):
                    pe.wait_ge(s_gr, 2 if half == 0 else 1)
                    pe.wait_ge(s_dwh, G * 2 + 2)
                    pe.wait_ge(s_dwl, G * 2 + 4)
                    pe.wait_ge(s_uh, G * 2 + 2)
                    pe.wait_ge(s_ul, G * 2 + 4)
                    for t in range(tiles):
                        b = (par * tiles + t) % 2
                        at = slice(t * P, (t + 1) * P) if t < NT // 2 else slice(last0, n)
                        pe.wait_ge(s_y, G * tiles + t + 1)
                        for c in range(2):
                            for h in range(2):
                                ha = slice(h * 512, (h + 1) * 512)
                                last = three_pass(nc, pd[:, b, h, :], uhi[:, par, c, at], ulo[:, par, c, at],
                                                  dwh[:, c, ha], dwl[:, c, ha], c == 0, c == 1)
                        last.then_inc(s_dn, 1)
                skeleton(pe, up, down, nothing)

            @block.scalar
            def _(act):
                a = nc.scalar
                act.sem_inc(s_re, Q)
                def split_up(f, c, count):
                    act.wait_ge(s_ur[c], count * 16)
                    a.copy(uwh[:, c], ur[:, c]).then_inc(s_uwh, 1)
                split_up(0, 0, 1)
                split_up(1, 1, 1)
                for kk in range(KD):
                    q = kk % 2
                    act.wait_ge(s_h[q], (kk // 2 + 1) * (32 if half == 0 else 16))
                    a.copy(hhi[:, kk], ru[:, q]).then_inc(s_hh, 1)
                    if kk == 0:
                        act.wait_ge(s_gt, 1)
                        a.copy(gate[:], pd[:, 0]).then_inc(s_gr, 1)
                        if half == 0:
                            act.wait_ge(s_gt, 2)
                            a.copy(gate_s[P - TS:P], pd[P - TS:P, 1]).then_inc(s_gr, 1)

                def up(G, par, i):
                    for c in range(2):
                        f = G * 2 + c
                        act.wait_ge(s_ul, f + 1)
                        for j in range(Q):
                            at = slice(j * qn, (j + 1) * qn)
                            act.wait_ge(s_up, f * Q + j + 1)
                            a.activation(ru[:, c, at], pu[:, j, 0:qn], ACT.Relu).then_inc(s_re, 1)
                        split_up(f + 2, c, G + 2)
                        act.wait_ge(s_u, f + 1)
                        act.wait_ge(s_dn, G * tiles + 1)
                        a.copy(uhi[:, par, c], ru[:, c]).then_inc(s_uh, 1)

                def split_down(G):
                    for c in range(2):
                        act.wait_ge(s_dr[c], G * 16 + 16)
                        act.wait_ge(s_dn, G * tiles + tiles + 1)
                        a.copy(dwh[:, c], dr[:, c]).then_inc(s_dwh, 1)
                skeleton(act, up, nothing, split_down)
                for t in range(tiles):
                    r, _ = place(t)
                    act.wait_ge(s_y, (NG - 1) * tiles + t + 3)
                    if t > 0:
                        act.wait_ge(s_ss, t)
                    a.activation(ru[r, 0, 0:D], y[r, t], ACT.Square, accum_out=ss[r, t:t + 1]).then_inc(s_ss, 1)

            @block.gpsimd
            def _(pool):
                g = nc.gpsimd

                def residual(t):
                    r, _ = place(t)
                    pool.wait_ge(s_yg, t + 1)
                    pool.wait_ge(s_rr, min(t + 2, tiles))
                    if t > 0:
                        pool.wait_ge(s_yo, t)
                    pool.wait_ge(s_x[t % 2], 16 * (t // 2 + 1))
                    g.tensor_tensor(y[r, t], y[r, t], dr[r, t % 2], ALU.add).then_inc(s_yo, 1)

                g.memset(y[:], 0.0).then_inc(s_y0, 1)
                for t in range(tiles):
                    r, _ = place(t)
                    pool.wait_ge(s_ms, t + 1)
                    if t >= 2:
                        pool.wait_ge(s_yo, t - 1)
                    g.tensor_tensor(rr[r, t:t + 1], ms[r, t:t + 1], k["nhalf"][r, 0:1], ALU.pow).then_inc(s_rr, 1)
                    if t > 0:
                        residual(t - 1)
                residual(tiles - 1)

            @block.vector
            def _(dve):
                v = nc.vector
                for s in (s_uwl, s_dwl, s_ul, s_y):
                    dve.sem_inc(s, 2)
                def split_up(f, c):
                    dve.wait_ge(s_uwh, f + 1)
                    v.tensor_tensor(uwl[:, c], ur[:, c], uwh[:, c].bitcast(F32), ALU.subtract).then_inc(s_uwl, 1)
                split_up(0, 0)
                split_up(1, 1)
                for kk in range(KD):
                    dve.wait_ge(s_hh, kk + 1)
                    v.tensor_tensor(hlo[:, kk], ru[:, kk % 2], hhi[:, kk].bitcast(F32), ALU.subtract).then_inc(s_hl, 1)

                dve.wait_ge(s_y0, 1)

                def up(G, par, i):
                    for c in range(2):
                        f = G * 2 + c
                        dve.wait_ge(s_re, f * Q + 2 * Q)
                        v.tensor_tensor(ru[:, c], ru[:, c], ru[:, c], ALU.mult).then_inc(s_u, 1)
                        split_up(f + 2, c)
                        dve.wait_ge(s_uh, f + 1)
                        v.tensor_tensor(ulo[:, par, c], ru[:, c], uhi[:, par, c].bitcast(F32), ALU.subtract).then_inc(s_ul, 1)

                def scale_out(t):
                    r, _ = place(t)
                    dve.wait_ge(s_ss, t + 1)
                    v.tensor_scalar(ms[r, t:t + 1], ss[r, t:t + 1], 1.0 / D, EPS, ALU.mult, ALU.add).then_inc(s_ms, 1)
                    yt = y[r, t].rearrange("p (b c) -> p b c", b=2)
                    gr = gate_s if half == 0 and t == tiles - 1 else gate
                    dve.wait_ge(s_rr, t + 1)
                    v.scalar_tensor_tensor(yt, yt, rr[r, t:t + 1], gr[r], ALU.mult, ALU.mult).then_inc(s_yg, 1)

                def down(G, par, i):
                    for t in range(tiles):
                        r, _ = place(t)
                        b = (par * tiles + t) % 2
                        dve.wait_ge(s_dn, G * tiles + t + tiles + 2)
                        acc = y[r, t].rearrange("p (b c) -> p b c", b=2)
                        v.tensor_tensor(acc, acc, pd[r, b], ALU.add).then_inc(s_y, 1)
                        if isinstance(G, int) and G == NG - 1 and t > 0:
                            scale_out(t - 1)

                def split_down(G):
                    for c in range(2):
                        dve.wait_ge(s_dwh, G * 2 + c + 1)
                        v.tensor_tensor(dwl[:, c], dr[:, c], dwh[:, c].bitcast(F32), ALU.subtract).then_inc(s_dwl, 1)
                skeleton(dve, up, down, split_down)
                scale_out(tiles - 1)
        m.clear_sems()


def decoder_layer(nc, io):
    io["projT"] = nc.dram_tensor("proj_scratch", (NCH, P, PAD + T), F32, kind="Internal").ap()
    io["oT"] = nc.dram_tensor("mixed_scratch", (KD, P, T), F32, kind="Internal").ap()
    io["x1"] = nc.dram_tensor("x_mid_scratch", (T + TS, D), F32, kind="Internal").ap()
    io["h2T"] = nc.dram_tensor("h2_scratch", (NT + 1, P, KD, P), F32, kind="Internal").ap()
    with ExitStack() as whole, ExitStack() as ctx:
        k = {}
        k["chunk_stored"] = [Mem(nc, whole).sem(f"chunk_stored_{q}") for q in range(2)]
        k["states_stored"] = Mem(nc, whole).sem("states_stored")
        k["w_o_loaded"] = Mem(nc, whole).sem("w_o_loaded")
        for name, shape in (("ident", [P, P]), ("nhalf", [P, 16]), ("mscale", [P, 2, KD, 9]), ("mshift", [P, 2, KD, 9]),
                            ("pscale", [P, 2, KD]), ("pshift", [P, 2, KD]), ("gate_col", [P, 2, KD]),
                            ("gate_col_s", [P, 2, KD, NB, NS]), ("oS", [P, KD, TS])):
            k[name] = Mem(nc, whole).sb(name, shape)
        m = Mem(nc, ctx)
        for name, shape in (("vcol", [P, NV]), ("alog", [P, HA]), ("dtb", [P, HA]), ("sink", [P, HB]), ("sink_s", [16, 2]),
                            ("zeros", [P, 1, P]), ("ones", [P, P]), ("ut", [P, P]), ("neg", [P, P]),
                            ("band", [P, 2 * W]), ("band_now", [P, 2 * W]), ("lev", [P, 7, P]), ("state", [P, HA, P]),
                            ("same", [TS, TS]), ("seg", [TS, NB]), ("uts", [TS, TS]), ("negs", [TS, TS]),
                            ("masks", [16, W + NS]), ("taps", [P, CW * CC]),
                            ("xs_pad", [P, CC, NB, CW - 1 + NS]), ("scT", [P, KD, 9]), 
                            ("projS", [P, NCH, TS]), ("xlast", [P, 3, CC]), ("xrow", [CC * 3, P]),
                            ("ba", [P, NT, 2 * HA]), ("ba_s", [TS, 2 * HA])):
            k[name] = m.sb(name, shape)
        with ExitStack() as front:
            k["xnT"] = Mem(nc, front).sb("xnT", [P, KD, LEAD + T + TS])
            constants(nc, io, k)
            modulation(nc, io, k)
            projection(nc, io, k)
        k["w_o_raw"] = m.sb("w_o_raw", [P, KD, D])
        mixer(nc, io, k)
        sample_mixer(nc, io, k)
        out_projection(nc, io, k)
        ctx.close()
        mlp(nc, io, k, 0)
        mlp(nc, io, k, 1)
        if "dbg" in io:
            io["dbg"](nc, io, k)


_INS = ["x_prompt", "x_sample", "state_conv", "state_ssm", "cache_swa_k", "cache_swa_v", "c_prompt", "c_sample",
        "g_pre_mix", "g_post_mix", "g_pre_ffn", "g_post_ffn", "w_ada", "b_ada", "w_in", "conv_w", "a_log", "dt_bias",
        "gdn_norm_w", "sinks", "w_o", "w_up", "w_down"]
_OUTS = [("y_prompt", (1, T, D)), ("y_sample", (NB, NS, D)), ("conv_prompt", (1, 1, 3, CC * P)),
         ("ssm_prompt", (1, 1, HA, P, P)), ("swa_k_prompt", (1, 1, W, 2, DB)), ("swa_v_prompt", (1, 1, W, 2, DB)),
         ("conv_sample", (1, NB, 3, CC * P)), ("ssm_sample", (1, NB, HA, P, P)), ("swa_k_sample", (1, NB, W, 2, DB)),
         ("swa_v_sample", (1, NB, W, 2, DB))]


def kernel(**inputs):
    import numpy as _np
    import concourse.bacc as _bacc
    from concourse import mybir as _mybir
    from concourse.bass_utils import run_bass_kernel_spmd as _run

    nc = _bacc.Bacc("TRN2", target_bir_lowering=False, num_devices=1)
    arrays, io = {}, {}
    for name in _INS:
        a = _np.ascontiguousarray(inputs[name])
        arrays["in_" + name] = a
        io[name] = nc.dram_tensor("in_" + name, a.shape, _mybir.dt.from_np(a.dtype), kind="ExternalInput").ap()
    for name, shape in _OUTS:
        io[name] = nc.dram_tensor("out_" + name, shape, _mybir.dt.float32, kind="ExternalOutput").ap()
    io["x"] = io["x_prompt"].rearrange("a t d -> (a t) d")
    io["y"] = io["y_prompt"].rearrange("a t d -> (a t) d") if "y_prompt" in io else None
    io["ys"] = io["y_sample"].rearrange("b s d -> (b s) d") if "y_sample" in io else None
    io["xs"] = io["x_sample"].rearrange("b s d -> (b s) d")
    for name in ("w_ada", "w_in", "w_o", "w_up", "w_down"):
        io[name] = io[name].rearrange("a k n -> (a k) n")
    decoder_layer(nc, io)
    r = _run(nc, [arrays], core_ids=[0])
    return tuple(r.results[0]["out_" + name] for name, _ in _OUTS)
```
